# Optimizing a Trainium2 kernel written in Bass

```python
import math
import jax, jax.numpy as jnp
from jax import lax
import numpy as np

D_MODEL = 1024
BATCH = 1
SEQ = 256
DEPTH = 1

DA_HEADS = 8
DA_HEAD_DIM = 64
DA_V_DIM = 2 * DA_HEAD_DIM
ROPE_THETA = 10000.0
QUERY_BLOCK = 128
POOL_WINDOWS = (2, 4, 8, 16)
POOL_GROUPS = len(POOL_WINDOWS)
POOL_GROUP_DIM = 128
POOL_DIM = POOL_GROUPS * POOL_GROUP_DIM
MEM_LEN = 256
MEM_HEADS = 4
MEM_HEAD_DIM = 128
MEM_DIM = MEM_HEADS * MEM_HEAD_DIM
Q_DIM = DA_HEADS * 2 * DA_HEAD_DIM
K_DIM = DA_HEADS * 2 * DA_HEAD_DIM
V_DIM = DA_HEADS * DA_V_DIM
N_BRANCHES = 3
GATE_DIM = N_BRANCHES * D_MODEL
IN_DIM = Q_DIM + K_DIM + V_DIM + POOL_DIM + MEM_DIM + GATE_DIM
SPLITS = (Q_DIM, Q_DIM + K_DIM, Q_DIM + K_DIM + V_DIM,
          Q_DIM + K_DIM + V_DIM + POOL_DIM,
          Q_DIM + K_DIM + V_DIM + POOL_DIM + MEM_DIM)
N_EXPERTS = 32
TOP_K = 4
D_EXPERT = D_MODEL
SWIGLU_LIMIT = 7.0
SWIGLU_ALPHA = 1.702
EXPERT_BLOCK = 256
LAYER_INDEX = 1
LAMBDA_INIT = 0.8 - 0.6 * math.exp(-0.3 * (LAYER_INDEX - 1))
EPS = 1e-6
NEG_INF = -1e30

kernel_name = "hybrid_gated_diffattn_pool_memxattn_moe"

def rmsnorm(t, g):
    t32 = t.astype(jnp.float32)
    t32 = t32 * lax.rsqrt(jnp.mean(t32 * t32, axis=-1, keepdims=True) + EPS)
    return (t32 * g.astype(jnp.float32)).astype(t.dtype)

def rotary(t, cos, sin):
    half = t.shape[-1] // 2
    t32 = t.astype(jnp.float32)
    c = cos[None, :, None, None, :]
    s = sin[None, :, None, None, :]
    t1, t2 = t32[..., :half], t32[..., half:]
    return jnp.concatenate([t1 * c - t2 * s, t2 * c + t1 * s], axis=-1).astype(t.dtype)

def diff_attention(q, k, v, lam):
    B, S = q.shape[0], q.shape[1]
    nb = S // QUERY_BLOCK
    scale = 1.0 / math.sqrt(DA_HEAD_DIM)
    qb = q.reshape(B, nb, QUERY_BLOCK, DA_HEADS, 2, DA_HEAD_DIM).transpose(1, 0, 2, 3, 4, 5)
    key_pos = jnp.arange(S)

    def block(args):
        q_blk, i = args
        s = jnp.einsum('bqhcd,bkhcd->bhcqk', q_blk, k).astype(jnp.float32) * scale
        q_pos = i * QUERY_BLOCK + jnp.arange(QUERY_BLOCK)
        mask = key_pos[None, :] <= q_pos[:, None]
        s = jnp.where(mask, s, NEG_INF)
        p = jax.nn.softmax(s, axis=-1)
        a = p[:, :, 0] - lam * p[:, :, 1]
        return jnp.einsum('bhqk,bkhe->bqhe', a.astype(v.dtype), v)

    o = lax.map(block, (qb, jnp.arange(nb)))
    return o.transpose(1, 0, 2, 3, 4).reshape(B, S, DA_HEADS, DA_V_DIM)

def multiscale_pool(u, pool_w, pool_scale):
    B, S, _ = u.shape
    u32 = u.astype(jnp.float32)
    cs = jnp.concatenate([jnp.zeros((B, 1, POOL_DIM), jnp.float32),
                          jnp.cumsum(u32, axis=1)], axis=1)
    t1 = jnp.arange(S) + 1
    outs = []
    for g, w in enumerate(POOL_WINDOWS):
        sl = slice(g * POOL_GROUP_DIM, (g + 1) * POOL_GROUP_DIM)
        csg = cs[..., sl]
        prev = jnp.concatenate([jnp.zeros((B, w - 1, POOL_GROUP_DIM), jnp.float32),
                                csg[:, :S + 1 - w]], axis=1)
        count = jnp.minimum(t1, w).astype(jnp.float32)[None, :, None]
        outs.append((csg[:, 1:] - prev) / count - u32[..., sl])
    z = jnp.stack(outs, axis=2)
    z = jnp.einsum('bsgc,gcd->bsgd', z, pool_w.astype(jnp.float32)).reshape(B, S, POOL_DIM)
    return (z * pool_scale.astype(jnp.float32)).astype(u.dtype)

def memory_cross_attention(q_mem, mem, g_mem, w_mem_kv, mq_norm, mk_norm):
    B, S = q_mem.shape[0], q_mem.shape[1]
    M = mem.shape[1]
    qm = rmsnorm(q_mem.reshape(B, S, MEM_HEADS, MEM_HEAD_DIM), mq_norm)
    kv = rmsnorm(mem, g_mem) @ w_mem_kv
    km, vm = jnp.split(kv, 2, axis=-1)
    km = rmsnorm(km.reshape(B, M, MEM_HEADS, MEM_HEAD_DIM), mk_norm)
    vm = vm.reshape(B, M, MEM_HEADS, MEM_HEAD_DIM)
    s = jnp.einsum('bshd,bmhd->bhsm', qm, km).astype(jnp.float32) / math.sqrt(MEM_HEAD_DIM)
    p = jax.nn.softmax(s, axis=-1)
    o = jnp.einsum('bhsm,bmhd->bshd', p.astype(vm.dtype), vm)
    return o.reshape(B, S, MEM_DIM)

def moe(hn, w_router, b_router, w_gate, b_gate, w_up, b_up, w_down, b_down):
    B, S, D = hn.shape
    T = B * S
    xt = hn.reshape(T, D)
    logits = (xt @ w_router + b_router).astype(jnp.float32)
    top_val, top_idx = lax.top_k(logits, TOP_K)
    gates = jax.nn.softmax(top_val, axis=-1)
    A = T * TOP_K
    e_flat = top_idx.reshape(A).astype(jnp.int32)
    tok_flat = jnp.arange(A, dtype=jnp.int32) // TOP_K
    w_flat = gates.reshape(A)
    order = jnp.argsort(e_flat)
    e_sorted, tok_sorted, w_sorted = e_flat[order], tok_flat[order], w_flat[order]
    counts = jnp.zeros((N_EXPERTS,), jnp.int32).at[e_flat].add(1)
    padded = ((counts + EXPERT_BLOCK - 1) // EXPERT_BLOCK) * EXPERT_BLOCK
    off = jnp.cumsum(counts) - counts
    pend = jnp.cumsum(padded)
    poff = pend - padded
    dest = poff[e_sorted] + (jnp.arange(A, dtype=jnp.int32) - off[e_sorted])
    n_blocks = -(-A // EXPERT_BLOCK) + N_EXPERTS
    P = n_blocks * EXPERT_BLOCK
    tok_buf = jnp.zeros((P,), jnp.int32).at[dest].set(tok_sorted)
    w_buf = jnp.zeros((P,), jnp.float32).at[dest].set(w_sorted)
    block_e = jnp.minimum(
        jnp.searchsorted(pend, jnp.arange(n_blocks, dtype=jnp.int32) * EXPERT_BLOCK, side='right'),
        N_EXPERTS - 1)

    def body(i, y):
        rows = lax.dynamic_slice(tok_buf, (i * EXPERT_BLOCK,), (EXPERT_BLOCK,))
        wts = lax.dynamic_slice(w_buf, (i * EXPERT_BLOCK,), (EXPERT_BLOCK,))
        e = block_e[i]
        xb = xt[rows]
        g = jnp.minimum(xb @ w_gate[e] + b_gate[e], SWIGLU_LIMIT)
        u = jnp.clip(xb @ w_up[e] + b_up[e], -SWIGLU_LIMIT, SWIGLU_LIMIT)
        act = g * jax.nn.sigmoid(SWIGLU_ALPHA * g) * (u + 1.0)
        out = act @ w_down[e] + b_down[e]
        return y.at[rows].add(out * wts[:, None].astype(out.dtype))

    y = lax.fori_loop(0, n_blocks, body, jnp.zeros_like(xt))
    return y.reshape(B, S, D)

def setup_inputs(seed: int = 0) -> dict:
    key = jax.random.key(seed)
    ks = jax.random.split(key, 32)
    f32 = jnp.float32
    nrm = lambda k, shape, fan_in: jax.random.normal(k, shape, f32) * (fan_in ** -0.5)
    gain = lambda k, n: 1.0 + 0.05 * jax.random.normal(k, (n,), f32)
    return {
        "x": jax.random.normal(ks[0], (BATCH, SEQ, D_MODEL), f32),
        "mem": jax.random.normal(ks[1], (BATCH, MEM_LEN, D_MODEL), f32),
        "g_mix": gain(ks[2], D_MODEL),
        "w_in": nrm(ks[3], (D_MODEL, IN_DIM), D_MODEL),
        "b_gates": 0.02 * jax.random.normal(ks[4], (GATE_DIM,), f32),
        "q_norm": gain(ks[5], DA_HEAD_DIM),
        "k_norm": gain(ks[6], DA_HEAD_DIM),
        "lambda_q1": 0.1 * jax.random.normal(ks[7], (DA_HEAD_DIM,), f32),
        "lambda_k1": 0.1 * jax.random.normal(ks[8], (DA_HEAD_DIM,), f32),
        "lambda_q2": 0.1 * jax.random.normal(ks[9], (DA_HEAD_DIM,), f32),
        "lambda_k2": 0.1 * jax.random.normal(ks[10], (DA_HEAD_DIM,), f32),
        "g_subln": gain(ks[11], DA_V_DIM),
        "pool_w": nrm(ks[12], (POOL_GROUPS, POOL_GROUP_DIM, POOL_GROUP_DIM), POOL_GROUP_DIM),
        "pool_scale": 1.0 + 0.1 * jax.random.normal(ks[13], (POOL_DIM,), f32),
        "g_mem": gain(ks[14], D_MODEL),
        "w_mem_kv": nrm(ks[15], (D_MODEL, 2 * MEM_DIM), D_MODEL),
        "mq_norm": gain(ks[16], MEM_HEAD_DIM),
        "mk_norm": gain(ks[17], MEM_HEAD_DIM),
        "w_b_attn": nrm(ks[18], (V_DIM, D_MODEL), V_DIM),
        "w_b_pool": nrm(ks[19], (POOL_DIM, D_MODEL), POOL_DIM),
        "w_b_mem": nrm(ks[20], (MEM_DIM, D_MODEL), MEM_DIM),
        "w_out": nrm(ks[21], (D_MODEL, D_MODEL), D_MODEL),
        "g_ffn": gain(ks[22], D_MODEL),
        "w_router": nrm(ks[23], (D_MODEL, N_EXPERTS), D_MODEL),
        "b_router": 0.01 * jax.random.normal(ks[24], (N_EXPERTS,), f32),
        "w_gate": nrm(ks[25], (N_EXPERTS, D_MODEL, D_EXPERT), D_MODEL),
        "b_gate": 0.02 * jax.random.normal(ks[26], (N_EXPERTS, D_EXPERT), f32),
        "w_up": nrm(ks[27], (N_EXPERTS, D_MODEL, D_EXPERT), D_MODEL),
        "b_up": 0.02 * jax.random.normal(ks[28], (N_EXPERTS, D_EXPERT), f32),
        "w_down": nrm(ks[29], (N_EXPERTS, D_EXPERT, D_MODEL), D_EXPERT),
        "b_down": 0.02 * jax.random.normal(ks[30], (N_EXPERTS, D_MODEL), f32),
    }

def reference(x, mem, g_mix, w_in, b_gates, q_norm, k_norm, lambda_q1, lambda_k1,
              lambda_q2, lambda_k2, g_subln, pool_w, pool_scale, g_mem, w_mem_kv,
              mq_norm, mk_norm, w_b_attn, w_b_pool, w_b_mem, w_out, g_ffn,
              w_router, b_router, w_gate, b_gate, w_up, b_up, w_down, b_down):
    B, S, D = x.shape
    inv_freq = ROPE_THETA ** (-jnp.arange(0, DA_HEAD_DIM, 2, dtype=jnp.float32) / DA_HEAD_DIM)
    ang = jnp.arange(S, dtype=jnp.float32)[:, None] * inv_freq[None, :]
    cos, sin = jnp.cos(ang), jnp.sin(ang)
    lam = (jnp.exp(jnp.sum(lambda_q1.astype(jnp.float32) * lambda_k1.astype(jnp.float32)))
           - jnp.exp(jnp.sum(lambda_q2.astype(jnp.float32) * lambda_k2.astype(jnp.float32)))
           + LAMBDA_INIT)

    h = x
    for _ in range(DEPTH):
        xn = rmsnorm(h, g_mix)
        proj = xn @ w_in
        q, k, v, u_pool, q_mem, gate_logits = jnp.split(proj, SPLITS, axis=-1)

        q = rotary(rmsnorm(q.reshape(B, S, DA_HEADS, 2, DA_HEAD_DIM), q_norm), cos, sin)
        k = rotary(rmsnorm(k.reshape(B, S, DA_HEADS, 2, DA_HEAD_DIM), k_norm), cos, sin)
        v = v.reshape(B, S, DA_HEADS, DA_V_DIM)
        o = diff_attention(q, k, v, lam)
        o = rmsnorm(o, g_subln) * (1.0 - LAMBDA_INIT)
        y_attn = o.reshape(B, S, V_DIM) @ w_b_attn

        y_pool = multiscale_pool(u_pool, pool_w, pool_scale) @ w_b_pool

        y_mem = memory_cross_attention(q_mem, mem, g_mem, w_mem_kv, mq_norm, mk_norm) @ w_b_mem

        g = jax.nn.sigmoid((gate_logits + b_gates).astype(jnp.float32)).reshape(B, S, N_BRANCHES, D)
        merged = (g[:, :, 0] * y_attn.astype(jnp.float32)
                  + g[:, :, 1] * y_pool.astype(jnp.float32)
                  + g[:, :, 2] * y_mem.astype(jnp.float32)).astype(h.dtype)
        h = h + merged @ w_out

        h = h + moe(rmsnorm(h, g_ffn), w_router, b_router, w_gate, b_gate,
                    w_up, b_up, w_down, b_down)
    return h


_drawn_inputs = setup_inputs


def setup_inputs(seed=0):
    import zlib

    import numpy as np

    out = dict(_drawn_inputs(seed))
    spreads = {}
    factors = {'b_gates': 3.606,
     'lambda_q2': 2.728,
     'lambda_k2': 13.124,
     'g_mem': 3.472,
     'mq_norm': 3.964,
     'mk_norm': 4.294,
     'b_gate': 7.062,
     'b_up': 8.0,
     'b_down': 6.793,
     'q_norm': 3.681,
     'k_norm': 3.055,
     'lambda_q1': 3.646,
     'lambda_k1': 5.134,
     'g_subln': 3.233,
     'b_router': 3.652}
    for name, (base, spread) in spreads.items():
        noise = np.random.default_rng([zlib.crc32(name.encode()), seed]).standard_normal(out[name].shape)
        drawn = base * np.exp(spread * noise) if base else spread * noise
        out[name] = __import__('jax').numpy.asarray(drawn.astype(out[name].dtype))
    for name, factor in factors.items():
        out[name] = (out[name] * factor).astype(out[name].dtype)
    return out
```

```python
from contextlib import ExitStack

import numpy as np

import concourse.bass as bass
from concourse import mybir

F32 = mybir.dt.float32
I32 = mybir.dt.int32
ALU = mybir.AluOpType
ACT = mybir.ActivationFunctionType
AX_X = mybir.AxisListType.X

P = 128
SEQ, D = 256, 1024
NT = SEQ // P
KD = D // P
HALF = 512
HEADS, HD = 8, 64
MHEADS, MHD = 4, 128
GROUPS = 4
WINDOWS = (2, 4, 8, 16)
EXPERTS, TOP_K = 32, 4
SLOTS = 64
PAIRS = EXPERTS // 2
EPS = 1e-6
LAMBDA_INIT = 0.2
LIMIT, ALPHA = 7.0, 1.702
NEG = -1e30

PIECES = ["pool", "mk", "mv", "qm", "q0", "q1", "k0", "k1", "v0", "v1", "gp0", "gp1", "wbp",
          "gm0", "gm1", "wbm", "ga0", "ga1", "wba0", "wba1", "wo0", "wo1"]
RING = 6
PER_PAIR = 12
UNITS = []
LAST_UNIT = []
for _n, _name in enumerate(PIECES):
    _cuts = 2 if _name in ("wbp", "wbm") else 1
    for _c in range(_cuts):
        for _t in range(NT):
            UNITS.append((_n, _name, _t, _c))
    LAST_UNIT.append(len(UNITS) - 1)
UNIT_OF = {(name, t, c): u for u, (n, name, t, c) in enumerate(UNITS)}

C_ID, C_TRI, C_MASK, C_IOTA, C_COS, C_SIN, C_NSIN, C_SEL, C_ONE = 0, 128, 256, 512, 640, 704, 768, 832, 1088
C_ALL = 1216


def constants():
    c = np.zeros((P, C_ALL), np.float32)
    i = np.arange(P)
    c[:, C_ID:C_ID + P] = np.eye(P)
    c[:, C_TRI:C_TRI + P] = i[:, None] < i[None, :]
    c[:, C_MASK + P:C_MASK + 2 * P] = np.where(i[None, :] <= i[:, None], 0.0, NEG)
    c[:, C_IOTA:C_IOTA + P] = np.tile(np.arange(SLOTS), 2)[None, :]
    inv = np.float32(10000.0) ** (-np.arange(0, HD, 2, dtype=np.float32) / np.float32(HD))
    ang = (np.arange(SEQ, dtype=np.float32)[:, None] * inv[None, :].astype(np.float32)).astype(np.float32)
    for base, table in ((C_COS, np.cos(ang)), (C_SIN, np.sin(ang)), (C_NSIN, -np.sin(ang))):
        c[:, base:base + NT * HD // 2] = table.reshape(NT, P, HD // 2).transpose(1, 0, 2).reshape(P, -1)
    sel = (np.arange(4)[:, None, None] == np.arange(4)[None, :, None]) * np.ones((1, 1, SLOTS))
    c[0:4, C_SEL:C_SEL + 4 * SLOTS] = sel.reshape(4, -1)
    c[:, C_ONE:C_ONE + P] = 1.0
    band = np.zeros((SEQ, GROUPS, SEQ), np.float32)
    for g, w in enumerate(WINDOWS):
        for t in range(SEQ):
            band[max(0, t - w + 1):t + 1, g, t] = 1.0 / min(t + 1, w)
            band[t, g, t] -= 1.0
    return c, band


def decoder_layer(nc, x, mem, g_mix, w_in, b_gates, q_norm, k_norm, lambda_q1, lambda_k1, lambda_q2,
                  lambda_k2, g_subln, pool_w, pool_scale, g_mem, w_mem_kv, mq_norm, mk_norm, w_b_attn,
                  w_b_pool, w_b_mem, w_out, g_ffn, w_router, b_router, w_gate, b_gate, w_up, b_up,
                  w_down, b_down, table, band, out):
    with ExitStack() as ctx:
        def sb(name, shape, dt=F32):
            return ctx.enter_context(nc.sbuf_tensor(name, shape, dt))

        def sem(name):
            return ctx.enter_context(nc.semaphore(name))

        ring = sb("ring", [P, RING, 4096])
        region = [sb(f"region{i}", [P, 2048]) for i in range(11)]
        con = sb("con", [P, C_ALL])
        small = sb("small", [P, 64])
        stat = sb("stat", [P, 208])
        rot = sb("rot", [P, 2, 2, NT, HD])
        gqk = sb("gqk", [P, 2, HD])
        qkt = region[9][:, 0:1024].rearrange("p (b n) -> p b n", b=2)
        prob = sb("prob", [P, 2, 768])
        probT = sb("probT", [P, 2, HALF])
        tmp = sb("tmp", [P, 2, HALF])
        rounds = sb("rounds", [P, 1], I32)

        ident = con[:, C_ID:C_ID + P]
        tri = con[:, C_TRI:C_TRI + P]
        ones = con[:, C_ONE:C_ONE + P]
        mask = con[:, C_MASK:C_MASK + 2 * P]
        iota = con[:, C_IOTA:C_IOTA + P]
        sel = con[0:4, C_SEL:C_SEL + 4 * SLOTS].rearrange("r (a s) -> r a s", a=4)

        mq_col, mk_col, sub_col = small[:, 0:1], small[:, 1:2], small[:, 2:3]
        psc_col = small[:, 4:8]
        nlam = small[:, 8:9]
        lam_e = small[:, 9:11]
        b_rt = small[:, 32:64]

        def rows(i, inner):
            return region[i][:, :].rearrange("p (t n) -> p t n", t=NT) if inner == "t" else \
                region[i][:, :].rearrange("p (k n) -> p k n", k=KD)

        X = rows(0, "t")
        XNT = rows(1, "k")
        XH = region[2][:, :].rearrange("p (t k n) -> p t k n", t=NT, k=KD)
        Q = rows(2, "t")
        MEM = rows(3, "t")
        MH = region[8][:, :].rearrange("p (t k n) -> p t k n", t=NT, k=KD)
        K = rows(3, "t")
        MEMT = rows(4, "k")
        V = rows(4, "t")
        BAND = region[5][:, :].rearrange("p (t g n) -> p t g n", t=NT, g=GROUPS)
        O = rows(5, "t")
        U = region[6][:, 0:1024].rearrange("p (t n) -> p t n", t=NT)
        QM = region[6][:, 1024:2048].rearrange("p (t n) -> p t n", t=NT)
        KM = region[7][:, 0:1024].rearrange("p (t n) -> p t n", t=NT)
        VM = region[7][:, 1024:2048].rearrange("p (t n) -> p t n", t=NT)
        G = {"p": rows(6, "t"), "m": rows(7, "t"), "a": rows(6, "t")}
        MG = rows(8, "t")
        ZT = region[8][:, 0:1024].rearrange("p (g n) -> p g n", g=GROUPS)
        KMT = region[9][:, 0:1024].rearrange("p (h n) -> p h n", h=MHEADS)
        QMT = region[9][:, 1024:2048].rearrange("p (h n) -> p h n", h=MHEADS)
        OT = rows(9, "k")
        OMT = region[10][:, 0:1024].rearrange("p (h n) -> p h n", h=MHEADS)
        Z2T = region[10][:, 1024:2048].rearrange("p (g n) -> p g n", g=GROUPS)
        MGT = rows(10, "k")
        GBC = region[9][:, :].rearrange("p (a n) -> p a n", a=2)
        POOLW = region[10][:, 0:512].rearrange("p (g n) -> p g n", g=GROUPS)
        JUNK = region[8][:, 1024:2048]

        HN = region[1][:, :].rearrange("p (t k n) -> p t k n", t=NT, k=KD)
        HNT = rows(2, "k")
        GFF = region[3][:, 0:1024]
        WR = region[3][:, 1024:1280].rearrange("p (k e) -> p k e", k=KD)
        LG = region[3][:, 1280:1344].rearrange("p (t e) -> p t e", t=NT)
        RG = region[3][:, 1792:1928].rearrange("p (a t e) -> p a t e", a=2, t=NT)
        RANKS, GATES = RG[:, 0], RG[:, 1]
        RANK, GATE = RANKS[:, :, 0:EXPERTS], GATES[:, :, 0:EXPERTS]
        MASK = region[3][:, 1408:1472].rearrange("p (t e) -> p t e", t=NT)
        SCR = region[3][:, 1536:1792].rearrange("p (a e) -> p a e", e=EXPERTS)
        XE = region[4][:, 0:1024].rearrange("p (k s) -> p k s", k=KD)
        OE = region[4][:, 1024:2048]
        GS, SG, US = region[5][:, 0:512], region[5][:, 512:1024], region[5][:, 1024:1536]
        AH = region[6][:, 0:1024].rearrange("p (e n) -> p e n", e=2)
        AHT = region[6][:, 1024:1536].rearrange("p (j s) -> p j s", j=4)
        PT = region[7][:, 0:256].rearrange("p (t s) -> p t s", t=NT)
        PW = region[7][:, 256:512].rearrange("p (t s) -> p t s", t=NT)
        PWT = region[7][:, 512:768]
        B4 = region[9][0:4, 0:1024]

        bank = [ctx.enter_context(nc.psum_tensor(f"bank{i}", [P, HALF], F32)) for i in range(8)]
        UB = bank[0:3]

        x_in, mem_in, con_in, gain_in, vec_in, late_in = (sem(n) for n in (
            "x_in", "mem_in", "con_in", "gain_in", "vec_in", "late_in"))
        ring_in = [sem(f"ring_in{i}") for i in range(RING)]
        gbias_in = [sem(f"gbias_in{i}") for i in range(3)]
        squares = sem("squares")
        ms_ready, root_done = sem("ms_ready"), sem("root_done")
        xhat_ready, xT_done, xT_copied = sem("xhat_ready"), sem("xT_done"), sem("xT_copied")
        mT_done, mT_copied = sem("mT_done"), sem("mT_copied")
        unit_done = sem("unit_done")
        bank_read = [sem(f"bank_read{i}") for i in range(3)]
        z_done, zT_copied, z2_done, z2T_copied = (sem(n) for n in ("z_done", "zT_copied", "z2_done", "z2T_copied"))
        mem_normed, kq_done, kqT_copied = sem("mem_normed"), sem("kq_done"), sem("kqT_copied")
        ms_done, mmax_ready, mexp_done, mp_ready = (sem(n) for n in ("ms_done", "mmax_ready", "mexp_done", "mp_ready"))
        mt_done, pt_copied, mo_done, omT_copied = (sem(n) for n in ("mt_done", "pt_copied", "mo_done", "omT_copied"))
        rot_ready, normed = sem("rot_ready"), sem("normed")
        lam_sum, lam_exp = sem("lam_sum"), sem("lam_exp")
        qk_done, qkT_copied, sc_done, max_ready = (sem(n) for n in ("qk_done", "qkT_copied", "sc_done", "max_ready"))
        exp_done, a_ready, at_done, at_copied = (sem(n) for n in ("exp_done", "a_ready", "at_done", "at_copied"))
        pv_done, o_copied = sem("pv_done"), sem("o_copied")
        gexp_done, o_normed, oT_done, oT_copied = (sem(n) for n in ("gexp_done", "o_normed", "oT_done", "oT_copied"))
        merged, mgT_done, mgT_copied = sem("merged"), sem("mgT_done"), sem("mgT_copied")
        h_ready, hn_ready, hT_done, hT_copied = (sem(n) for n in ("h_ready", "hn_ready", "hT_done", "hT_copied"))
        logit_done, top_ready, lexp_done, mask_ready = (sem(n) for n in ("logit_done", "top_ready", "lexp_done", "mask_ready"))
        rank_done, gate_ready, gT_done, rounds_ready = (sem(n) for n in ("rank_done", "gate_ready", "gT_done", "rounds_ready"))
        seed_clear, seed_in = sem("seed_clear"), sem("seed_in")
        dve_step = sem("dve_step")
        slots_free, slots_built = sem("slots_free"), sem("slots_built")
        disp_done, xe_lo, xe_hi = sem("disp_done"), sem("xe_lo"), sem("xe_hi")
        comb_done, y_added, rank_ready, wT_copied = (sem(n) for n in ("comb_done", "y_added", "rank_ready", "wT_copied"))
        bias_in, used = sem("bias_in"), sem("used")
        g_read, sig_done, gs_done, u_read = (sem(n) for n in ("g_read", "sig_done", "gs_done", "u_read"))
        act_ready, actT_done, actT_copied = sem("act_ready"), sem("actT_done"), sem("actT_copied")
        o_lo, o_hi, out_done = sem("o_lo"), sem("o_hi"), sem("out_done")

        win = w_in.rearrange("(p k) n -> p k n", k=KD)
        wkv = w_mem_kv.rearrange("(p k) n -> p k n", k=KD)
        wba = w_b_attn.rearrange("(k p) n -> p k n", p=P)
        wo = w_out.rearrange("(k p) n -> p k n", p=P)
        src = {"pool": win[:, :, 3072:3584], "mk": wkv[:, :, 0:512], "mv": wkv[:, :, 512:1024],
               "qm": win[:, :, 3584:4096], "wbp": w_b_pool.rearrange("(k p) n -> p k n", p=P),
               "wbm": w_b_mem.rearrange("(k p) n -> p k n", p=P)}
        for h in range(2):
            for name, base in (("q", 0), ("k", 1024), ("v", 2048), ("ga", 4096), ("gp", 5120), ("gm", 6144)):
                src[f"{name}{h}"] = win[:, :, base + h * 512:base + h * 512 + 512]
            src[f"wba{h}"] = wba[:, :, h * 512:h * 512 + 512]
            src[f"wo{h}"] = wo[:, :, h * 512:h * 512 + 512]

        def slot_k(n):
            k = 4 if PIECES[n] in ("wbp", "wbm") else 8
            return ring[:, n % RING, :].rearrange("p (k n) -> p k n", k=k)

        N0 = len(PIECES)
        BATCH = ["gate", "gate", "up", "up"]

        def expert_piece(j):
            m, h = divmod(j, 2)
            which = [(w_gate, 0), (w_up, 0), (w_gate, 1), (w_up, 1), (w_down, 0), (w_down, 1)][m]
            return which[0], which[1], h

        def moe_slot(j):
            return (N0 + j) % RING

        def moe_landed(it, j):
            return it * (16 * PER_PAIR // RING) + 16 * ((N0 + j) // RING + 1)

        block = ctx.enter_context(nc.Block())

        @block.sync
        def _(sp):
            sp.dma_start(X[:, 0, :], x[0, 0:P, :]).then_inc(x_in, 16)
            sp.dma_start(X[:, 1, :], x[0, P:SEQ, :]).then_inc(x_in, 16)

            def load(n):
                if n >= RING:
                    sp.wait_ge(unit_done, LAST_UNIT[n - RING] + 1)
                sp.dma_start(slot_k(n), src[PIECES[n]]).then_inc(ring_in[n % RING], 16)

            load(0)
            sp.dma_start(MEM, mem[0].rearrange("(t p) n -> p t n", p=P)).then_inc(mem_in, 16)
            for n in range(1, N0):
                load(n)

            def load_expert(i, j):
                w, e, h = expert_piece(j)
                one = w[bass.ds(i * 2 + e, 1), :, :].rearrange("e r n -> (e r) n")
                if j < 8:
                    part = one.rearrange("(p k) n -> p k n", k=KD)[:, 4 * h:4 * h + 4, :]
                else:
                    part = one.rearrange("(k p) n -> p k n", p=P)[:, 4 * h:4 * h + 4, :]
                dst = ring[:, moe_slot(j), :].rearrange("p (k n) -> p k n", k=4)
                sp.dma_start(dst, part).then_inc(ring_in[moe_slot(j)], 16)

            def rest_of_pair(it, i):
                for j in range(RING, PER_PAIR):
                    sp.wait_ge(used, it * PER_PAIR + (j - RING + 1))
                    load_expert(i, j)

            def start_of_pair(it, i):
                for j in range(RING):
                    sp.wait_ge(used, it * PER_PAIR + (j - RING + 1))
                    if j == 1:
                        biases(i)
                    load_expert(i, j)

            def biases(i):
                sp.dma_start(B4[0:2, :], b_gate[bass.ds(i * 2, 2), :]).then_inc(bias_in, 16)
                sp.dma_start(B4[2:4, :], b_up[bass.ds(i * 2, 2), :]).then_inc(bias_in, 16)

            for j in range(RING):
                sp.wait_ge(unit_done, LAST_UNIT[N0 + j - RING] + 1)
                load_expert(0, j)
                if j == 3:
                    biases(0)

            def round_of(r):
                base = r * PAIRS
                with sp.Fori(0, PAIRS - 1) as i:
                    rest_of_pair(base + i, i)
                    start_of_pair(base + i + 1, i + 1)
                rest_of_pair(base + (PAIRS - 1), PAIRS - 1)

            round_of(0)
            sp.wait_ge(rounds_ready, 1)
            n_rounds = sp.value_load(rounds[0:1, 0:1], min_val=1, max_val=SEQ // SLOTS)
            with sp.If(n_rounds > 1):
                with sp.Fori(1, n_rounds) as r:
                    start_of_pair(r * PAIRS, 0)
                    round_of(r)
            sp.wait_ge(y_added, n_rounds * (4 * PAIRS) + 2 + 4)
            for t in range(NT):
                sp.dma_start(out[0, t * P:(t + 1) * P, :], X[:, t, :]).then_inc(out_done, 16)
            sp.wait_ge(out_done, 16 * NT)

        @block.gpsimd
        def _(pool):
            pool.wait_ge(con_in, 16 * 5)
            pool.wait_ge(vec_in, 16 * 9)
            h = HD // 2

            def angles(base):
                return con[:, base:base + NT * h].rearrange("p (t n) -> p t n", t=NT)

            for w in range(2):
                lo = gqk[:, w, 0:h].unsqueeze(1).to_broadcast([P, NT, h])
                hi = gqk[:, w, h:HD].unsqueeze(1).to_broadcast([P, NT, h])
                for o, a, b in ((rot[:, w, 0, :, 0:h], lo, angles(C_COS)), (rot[:, w, 0, :, h:HD], hi, angles(C_COS)),
                                (rot[:, w, 1, :, 0:h], hi, angles(C_NSIN)), (rot[:, w, 1, :, h:HD], lo, angles(C_SIN))):
                    nc.gpsimd.tensor_tensor(o, a, b, ALU.mult).then_inc(rot_ready, 1)

            def gate_bias(n, branch, first):
                for t in range(NT):
                    pool.dma_start(G[branch][:, t, :], b_gates[first:first + D].rearrange("(a n) -> a n", a=1)
                                   .to_broadcast([P, D])).then_inc(gbias_in[n], 16)

            pool.wait_ge(kq_done, 4)
            pool.wait_ge(z_done, 2)
            gate_bias(0, "p", D)
            pool.wait_ge(mo_done, MHEADS)
            gate_bias(1, "m", 2 * D)
            last = UNIT_OF[("wbp", 1, 1)]
            pool.wait_ge(bank_read[last % 3], last // 3 + 1)
            gate_bias(2, "a", 0)

            pool.wait_ge(pv_done, HEADS)
            nc.gpsimd.memset(OE, 0.0).then_inc(seed_clear, 1)
            pool.wait_ge(oT_done, 4)
            pool.wait_ge(merged, 8)
            pool.wait_ge(seed_clear, 1)
            pool.dma_start(OE[0:EXPERTS, :], b_down).then_inc(seed_in, 16)
            nc.gpsimd.memset(PWT, 0.0).then_inc(seed_clear, 1)
            pool.dma_start(GFF, g_ffn.rearrange("(a n) -> a n", a=1).to_broadcast([P, D])).then_inc(late_in, 16)
            pool.dma_start(WR, w_router.rearrange("(p k) e -> p k e", k=KD)).then_inc(late_in, 16)

        @block.scalar
        def _(act):
            def row(v):
                return v.rearrange("(a n) -> a n", a=1)

            act.dma_start(con[:, :], table).then_inc(con_in, 16)
            act.dma_start(GBC[:, 0, :], row(g_mix).to_broadcast([P, D])).then_inc(gain_in, 16)
            act.dma_start(GBC[:, 1, :], row(g_mem).to_broadcast([P, D])).then_inc(gain_in, 16)
            act.dma_start(gqk[:, 0, :], row(q_norm).to_broadcast([P, HD])).then_inc(vec_in, 16)
            act.dma_start(gqk[:, 1, :], row(k_norm).to_broadcast([P, HD])).then_inc(vec_in, 16)
            lam4 = tmp[:, 1, 0:4 * HD].rearrange("p (a n) -> p a n", a=4)
            for a, v in enumerate((lambda_q1, lambda_k1, lambda_q2, lambda_k2)):
                act.dma_start(lam4[:, a, :], row(v).to_broadcast([P, HD])).then_inc(vec_in, 16)
            act.dma_start(BAND, band.rearrange("(t p) g n -> p t g n", p=P)).then_inc(vec_in, 16)
            act.dma_start(POOLW, pool_w.rearrange("g p n -> p g n")).then_inc(vec_in, 16)
            act.dma_start(b_rt, row(b_router).to_broadcast([P, EXPERTS])).then_inc(vec_in, 16)
            with nc.allow_non_contiguous_dma(reason="short per-partition vectors"):
                act.dma_start(mq_col, mq_norm.rearrange("(p a) -> p a", a=1)).then_inc(con_in, 16)
                act.dma_start(mk_col, mk_norm.rearrange("(p a) -> p a", a=1)).then_inc(con_in, 16)
                act.dma_start(sub_col, g_subln.rearrange("(p a) -> p a", a=1)).then_inc(con_in, 16)
                act.dma_start(psc_col, pool_scale.rearrange("(g p) -> p g", p=P)).then_inc(con_in, 16)

            def root(n, cols):
                act.wait_ge(ms_ready, n + 1)
                nc.scalar.activation(stat[:, cols], stat[:, cols], ACT.Sqrt).then_inc(root_done, 1)

            def evac(u, dst):
                act.wait_ge(unit_done, u + 1)
                nc.scalar.activation(dst, UB[u % 3][:, :], ACT.Copy).then_inc(bank_read[u % 3], 1)

            def gate_exp(u):
                _, name, t, _ = UNITS[u]
                g = G[name[1]][:, t, int(name[2]) * HALF:(int(name[2]) + 1) * HALF]
                act.wait_ge(bank_read[u % 3], u // 3 + 1)
                nc.scalar.activation(g, g, ACT.Exp, scale=-1.0).then_inc(gexp_done, 1)

            act.wait_ge(x_in, 16 * NT)
            for t in range(NT):
                if t:
                    act.wait_ge(squares, t)
                nc.scalar.activation(JUNK, X[:, t, :], ACT.Square, accum_out=stat[:, t:t + 1]).then_inc(squares, 1)
            root(0, slice(0, 2))
            act.wait_ge(mem_in, 16)
            for t in range(NT):
                act.wait_ge(squares, 2 + t)
                nc.scalar.activation(JUNK, MEM[:, t, :], ACT.Square, accum_out=stat[:, 2 + t:3 + t]).then_inc(squares, 1)
            root(1, slice(2, 4))
            evac(0, U[:, 0, :])
            evac(1, U[:, 1, :])
            for j in range(4):
                act.wait_ge(mT_done, j + 1)
                t, h = divmod(j, 2)
                nc.scalar.activation(MEMT[:, 4 * h:4 * h + 4, t * P:(t + 1) * P],
                                     bank[3 + j][:, :].rearrange("p (k n) -> p k n", k=4), ACT.Copy).then_inc(mT_copied, 1)
            evac(2, KM[:, 0, :])
            evac(3, KM[:, 1, :])
            root(2, slice(8, 16))
            evac(4, VM[:, 0, :])
            evac(5, VM[:, 1, :])
            evac(6, QM[:, 0, :])
            evac(7, QM[:, 1, :])
            root(3, slice(16, 24))
            for j in range(2):
                act.wait_ge(z_done, j + 1)
                nc.scalar.activation(ZT[:, 2 * j:2 * j + 2, :], bank[4 + j][:, :].rearrange("p (g n) -> p g n", g=2),
                                     ACT.Copy).then_inc(zT_copied, 1)

            def qk_dst(u):
                _, name, t, _ = UNITS[u]
                return {"q": Q, "k": K, "v": V}[name[0]][:, t, int(name[1]) * HALF:(int(name[1]) + 1) * HALF]

            def qk_unit(u):
                evac(u, qk_dst(u))
                root(u - 4, slice(24 + 8 * (u % 2), 32 + 8 * (u % 2)))

            for u in range(8, 14):
                qk_unit(u)
            act.wait_ge(lam_sum, 1)
            nc.scalar.activation(lam_e, lam_e, ACT.Exp).then_inc(lam_exp, 1)

            def mem_exp(h):
                act.wait_ge(mmax_ready, h + 1)
                for t in range(NT):
                    c = 64 + 4 * (h % 2) + t
                    ins = nc.scalar.activation(prob[:, h % 2, t * SEQ:(t + 1) * SEQ], bank[4 + h % 2][:, t * SEQ:(t + 1) * SEQ],
                                               ACT.Exp, bias=stat[:, c:c + 1], scale=MHD ** -0.5,
                                               accum_out=stat[:, c + 2:c + 3])
                ins.then_inc(mexp_done, 1)

            def mem_probT(h):
                act.wait_ge(mt_done, h + 1)
                nc.scalar.activation(probT[:, h % 2, :], bank[6][:, :], ACT.Copy).then_inc(pt_copied, 1)

            mem_exp(0)
            qk_unit(14)
            mem_exp(1)
            mem_probT(0)
            qk_unit(15)
            mem_exp(2)
            mem_probT(1)
            evac(16, qk_dst(16))
            mem_exp(3)
            mem_probT(2)
            evac(17, qk_dst(17))
            mem_probT(3)
            evac(18, qk_dst(18))
            evac(19, qk_dst(19))

            def qkT(h):
                act.wait_ge(qk_done, h + 1)
                nc.scalar.activation(qkt[:, h % 2, :], bank[3][:, :], ACT.Copy).then_inc(qkT_copied, 1)

            def exps(h):
                act.wait_ge(max_ready, h + 1)
                for c in range(2):
                    for t, (a, b) in enumerate(((0, P), (P, 3 * P))):
                        s = prob[:, h % 2, c * 384 + a:c * 384 + b]
                        m = 96 + 16 * (h % 2) + 2 * c + t
                        ins = nc.scalar.activation(s, s, ACT.Exp, bias=stat[:, m:m + 1], scale=HD ** -0.5,
                                                   accum_out=stat[:, m + 4:m + 5])
                ins.then_inc(exp_done, 1)

            def aT(h):
                act.wait_ge(at_done, h + 1)
                nc.scalar.activation(probT[:, h % 2, 0:384], bank[6][:, 0:384], ACT.Copy).then_inc(at_copied, 1)

            def o_out(h):
                act.wait_ge(pv_done, h + 1)
                nc.scalar.activation(O[:, :, h * P:(h + 1) * P], bank[7][:, 0:256].rearrange("p (t n) -> p t n", t=NT),
                                     ACT.Copy).then_inc(o_copied, 1)

            qkT(0)
            gate_exp(20)
            exps(0)
            qkT(1)
            gate_exp(21)
            for h in range(HEADS):
                for_gate = [u for u in (22 + 2 * h, 23 + 2 * h) if UNITS[u][1][0] == "g"]
                if h + 1 < HEADS:
                    exps(h + 1)
                if 22 + 2 * h in for_gate:
                    gate_exp(22 + 2 * h)
                aT(h)
                if h + 2 < HEADS:
                    qkT(h + 2)
                if h == HEADS - 1:
                    o_out(h)
                    root(12, slice(128, 144))
                if 23 + 2 * h in for_gate:
                    gate_exp(23 + 2 * h)
                if h < HEADS - 1:
                    o_out(h)
            gate_exp(38)
            gate_exp(39)
            for j in range(4):
                act.wait_ge(mgT_done, j + 1)
                t, h = divmod(j, 2)
                nc.scalar.activation(MGT[:, 4 * h:4 * h + 4, t * P:(t + 1) * P],
                                     bank[3 + j][:, :].rearrange("p (k n) -> p k n", k=4), ACT.Copy).then_inc(mgT_copied, 1)
            for t in range(NT):
                act.wait_ge(h_ready, 3 + t)
                if t:
                    act.wait_ge(squares, 5)
                nc.scalar.activation(JUNK, X[:, t, :], ACT.Square, accum_out=stat[:, 4 + t:5 + t]).then_inc(squares, 1)
            root(13, slice(4, 6))
            for j in range(4):
                act.wait_ge(hT_done, j + 1)
                t, h = divmod(j, 2)
                nc.scalar.activation(HNT[:, 4 * h:4 * h + 4, t * P:(t + 1) * P],
                                     bank[3 + j][:, :].rearrange("p (k n) -> p k n", k=4), ACT.Copy).then_inc(hT_copied, 1)
            act.wait_ge(top_ready, 1)
            for t in range(NT):
                nc.scalar.activation(GATE[:, t, :], LG[:, t, :], ACT.Exp,
                                     bias=stat[:, 180 + t:181 + t]).then_inc(lexp_done, 1)
            act.wait_ge(gT_done, 1)
            act.wait_ge(seed_clear, 2)
            nc.scalar.activation(PWT[0:EXPERTS, :], bank[4][0:EXPERTS, 0:SEQ], ACT.Copy).then_inc(wT_copied, 1)
            act.wait_ge(rounds_ready, 1)
            n_rounds = act.value_load(rounds[0:1, 0:1], min_val=1, max_val=SEQ // SLOTS)
            with act.Fori(0, n_rounds) as r:
                with act.Fori(0, PAIRS) as i:
                    it = r * PAIRS + i
                    act.wait_ge(disp_done, it * 2 + 1)
                    nc.scalar.activation(XE[:, 0:4, :], bank[4][:, :].rearrange("p (k n) -> p k n", k=4),
                                         ACT.Copy).then_inc(xe_lo, 1)
                    act.wait_ge(slots_free, it + 1)
                    nc.scalar.activation(PWT, bank[3][:, 0:SEQ], ACT.Copy).then_inc(wT_copied, 1)
                    for e in range(2):
                        act.wait_ge(g_read, it * 2 + (e + 1))
                        nc.scalar.activation(SG, GS, ACT.Sigmoid, scale=ALPHA).then_inc(sig_done, 1)
                    for e in range(2):
                        act.wait_ge(actT_done, it * 2 + (e + 1))
                        nc.scalar.activation(AHT, bank[3][:, :].rearrange("p (j s) -> p j s", j=4),
                                             ACT.Copy).then_inc(actT_copied, 1)
                        act.wait_ge(used, it * PER_PAIR + (10 + 2 * e))
                        nc.scalar.activation(OE[e * SLOTS:(e + 1) * SLOTS, 0:HALF], bank[2][0:SLOTS, :],
                                             ACT.Copy).then_inc(o_lo, 1)

        @block.vector
        def _(dve):
            n_step = [0]

            def link(ins):
                n_step[0] += 1
                ins.then_inc(dve_step, 1)
                dve.wait_ge(dve_step, n_step[0])

            def mean_square(n, cols, width):
                nc.vector.tensor_scalar(stat[:, cols], stat[:, cols], 1.0 / width, EPS, ALU.mult, ALU.add).then_inc(ms_ready, 1)

            def rroot(n, cols):
                dve.wait_ge(root_done, n + 1)
                link(nc.vector.reciprocal(stat[:, cols], stat[:, cols]))

            dve.wait_ge(gain_in, 32)
            for n, (rows_, dst) in enumerate(((X, XH), (MEM, MH))):
                dve.wait_ge(squares, 2 * n + 2)
                mean_square(n, slice(2 * n, 2 * n + 2), D)
                rroot(n, slice(2 * n, 2 * n + 2))
                for t in range(NT):
                    nc.vector.scalar_tensor_tensor(
                        out=dst[:, t, :, :], in0=rows_[:, t, :].rearrange("p (n k) -> p k n", k=KD),
                        scalar=stat[:, 2 * n + t:2 * n + t + 1],
                        in1=GBC[:, n, :].rearrange("p (n k) -> p k n", k=KD),
                        op0=ALU.mult, op1=ALU.mult).then_inc(xhat_ready, 1)
                if n == 0:
                    for j in range(4):
                        dve.wait_ge(xT_done, j + 1)
                        t, h = divmod(j, 2)
                        nc.vector.tensor_copy(XNT[:, 4 * h:4 * h + 4, t * P:(t + 1) * P],
                                              bank[3 + j][:, :].rearrange("p (k n) -> p k n", k=4)).then_inc(xT_copied, 1)
            dve.wait_ge(vec_in, 16 * 9)
            lam4 = tmp[:, 1, 0:4 * HD].rearrange("p (a n) -> p a n", a=4)
            for a in range(2):
                link(nc.vector.tensor_tensor(tmp[:, 0, a * HD:(a + 1) * HD], lam4[:, 2 * a, :], lam4[:, 2 * a + 1, :], ALU.mult))
            nc.vector.tensor_reduce(lam_e, tmp[:, 0, 0:2 * HD].rearrange("p (a n) -> p a n", a=2), AX_X,
                                    ALU.add).then_inc(lam_sum, 1)

            def group_stats(rows3, groups, sq, col, width):
                link(nc.vector.tensor_tensor(sq, rows3, rows3, ALU.mult))
                link(nc.vector.tensor_reduce(stat[:, col:col + groups], sq, AX_X, ALU.add))
                mean_square(0, slice(col, col + groups), width)

            dve.wait_ge(lam_sum, 1)
            for n, (rows_, first, col) in enumerate(((KM, 2, 8), (QM, 6, 16))):
                for u in (first, first + 1):
                    dve.wait_ge(bank_read[u % 3], u // 3 + 1)
                flat = rows_.rearrange("p t (h n) -> p (t h) n", n=MHD)
                group_stats(flat, 8, tmp[:, :, :].rearrange("p t (h n) -> p (t h) n", n=MHD), col, MHD)
                rroot(2 + n, slice(col, col + 8))
                nc.vector.tensor_tensor(flat, flat, stat[:, col:col + 8].unsqueeze(2).to_broadcast([P, 8, MHD]),
                                        ALU.mult).then_inc(mem_normed, 1)

            def norm_rotate(u):
                _, name, t, _ = UNITS[u]
                w = 0 if name[0] == "q" else 1
                raw = (Q if w == 0 else K)[:, t, int(name[1]) * HALF:(int(name[1]) + 1) * HALF].rearrange("p (m n) -> p m n", n=HD)
                a = tmp[:, 0, :].rearrange("p (m n) -> p m n", n=HD)
                b = tmp[:, 1, :].rearrange("p (m n) -> p m n", n=HD)
                col = 24 + 8 * (u % 2)
                hf = HD // 2
                if u > 8:
                    dve.wait_ge(normed, u - 8)
                dve.wait_ge(bank_read[u % 3], u // 3 + 1)
                group_stats(raw, 8, a, col, HD)
                rroot(u - 4, slice(col, col + 8))
                link(nc.vector.tensor_tensor(a, raw, stat[:, col:col + 8].unsqueeze(2).to_broadcast([P, 8, HD]), ALU.mult))
                nc.vector.tensor_tensor(b[:, :, 0:hf], a[:, :, hf:HD],
                                        rot[:, w, 1, t, 0:hf].unsqueeze(1).to_broadcast([P, 8, hf]), ALU.mult)
                link(nc.vector.tensor_tensor(b[:, :, hf:HD], a[:, :, 0:hf],
                                             rot[:, w, 1, t, hf:HD].unsqueeze(1).to_broadcast([P, 8, hf]), ALU.mult))
                link(nc.vector.tensor_tensor(a, a, rot[:, w, 0, t, :].unsqueeze(1).to_broadcast([P, 8, HD]), ALU.mult))
                nc.vector.tensor_tensor(raw, a, b, ALU.add).then_inc(normed, 1)

            dve.wait_ge(lam_sum, 1)
            dve.wait_ge(rot_ready, 8)
            norm_rotate(8)
            norm_rotate(9)
            dve.wait_ge(con_in, 16 * 5)
            for j in range(2):
                dve.wait_ge(z2_done, j + 1)
                nc.vector.tensor_tensor(Z2T[:, 2 * j:2 * j + 2, :], bank[4 + j][:, :].rearrange("p (g n) -> p g n", g=2),
                                        psc_col[:, 2 * j:2 * j + 2].unsqueeze(2).to_broadcast([P, 2, SEQ]),
                                        ALU.mult).then_inc(z2T_copied, 1)
            norm_rotate(10)
            norm_rotate(11)
            for j, (dst, t, gain) in enumerate(((KMT, 0, mk_col), (KMT, 1, mk_col), (QMT, 0, mq_col), (QMT, 1, mq_col))):
                dve.wait_ge(kq_done, j + 1)
                nc.vector.tensor_scalar(dst[:, :, t * P:(t + 1) * P], bank[(3, 6, 4, 5)[j]][:, :].rearrange("p (h n) -> p h n", h=MHEADS),
                                        gain, None, ALU.mult).then_inc(kqT_copied, 1)
            norm_rotate(12)
            norm_rotate(13)

            def mem_max(h):
                c = 64 + 4 * (h % 2)
                dve.wait_ge(ms_done, h + 1)
                link(nc.vector.tensor_reduce(stat[:, c:c + 2], bank[4 + h % 2][:, :].rearrange("p (t n) -> p t n", t=NT), AX_X,
                                             ALU.max, negate=True))
                nc.vector.tensor_scalar(stat[:, c:c + 2], stat[:, c:c + 2], MHD ** -0.5, None, ALU.mult).then_inc(mmax_ready, 1)

            def mem_scale(h):
                c = 66 + 4 * (h % 2)
                dve.wait_ge(mexp_done, h + 1)
                link(nc.vector.reciprocal(stat[:, c:c + 2], stat[:, c:c + 2]))
                p = prob[:, h % 2, 0:HALF].rearrange("p (t n) -> p t n", t=NT)
                nc.vector.tensor_tensor(p, p, stat[:, c:c + 2].unsqueeze(2).to_broadcast([P, NT, SEQ]), ALU.mult).then_inc(mp_ready, 1)

            def mem_out(h):
                dve.wait_ge(mo_done, h + 1)
                nc.vector.tensor_copy(OMT[:, h, :], bank[7][:, 0:SEQ]).then_inc(omT_copied, 1)

            mem_max(0)
            mem_scale(0)
            norm_rotate(14)
            mem_max(1)
            mem_scale(1)
            norm_rotate(15)
            mem_out(0)
            mem_max(2)
            mem_scale(2)
            mem_out(1)
            mem_max(3)
            mem_scale(3)
            mem_out(2)
            mem_out(3)
            dve.wait_ge(lam_exp, 1)
            link(nc.vector.tensor_tensor(nlam, lam_e[:, 1:2], lam_e[:, 0:1], ALU.subtract))
            link(nc.vector.tensor_scalar(nlam, nlam, -LAMBDA_INIT, None, ALU.add))

            def add_bias(u):
                _, name, t, _ = UNITS[u]
                g = G[name[1]][:, t, int(name[2]) * HALF:(int(name[2]) + 1) * HALF]
                dve.wait_ge(gbias_in["pma".index(name[1])], 16 * NT)
                dve.wait_ge(unit_done, u + 1)
                nc.vector.tensor_tensor(g, UB[u % 3][:, :], g, ALU.add).then_inc(bank_read[u % 3], 1)

            gates_before = {}
            seen = 0
            for u, (_, name, t, _) in enumerate(UNITS):
                if name[0] == "g":
                    seen += 1
                    gates_before[(name[1], t, int(name[2]))] = seen

            def merge(u):
                _, name, t, c = UNITS[u]
                branch, n = {"wbp": ("p", c), "wbm": ("m", c), "wba0": ("a", 0), "wba1": ("a", 1)}[name]
                cols = slice(n * HALF, (n + 1) * HALF)
                g = G[branch][:, t, cols]
                dve.wait_ge(gexp_done, gates_before[(branch, t, n)])
                link(nc.vector.tensor_scalar(g, g, 1.0, None, ALU.add))
                link(nc.vector.reciprocal(g, g))
                dve.wait_ge(unit_done, u + 1)
                if branch == "p":
                    nc.vector.tensor_tensor(MG[:, t, cols], UB[u % 3][:, :], g, ALU.mult).then_inc(bank_read[u % 3], 1)
                    dve.wait_ge(bank_read[u % 3], u // 3 + 1)
                    return
                nc.vector.tensor_tensor(tmp[:, 0, :], UB[u % 3][:, :], g, ALU.mult).then_inc(bank_read[u % 3], 1)
                dve.wait_ge(bank_read[u % 3], u // 3 + 1)
                nc.vector.tensor_tensor(MG[:, t, cols], MG[:, t, cols], tmp[:, 0, :], ALU.add).then_inc(merged, 1)
                n_merged[0] += 1
                dve.wait_ge(merged, n_merged[0])

            n_merged = [0]

            def unit(u):
                (add_bias if UNITS[u][1][0] == "g" else merge)(u)

            def head_max(h):
                dve.wait_ge(sc_done, h + 1)
                m = 96 + 16 * (h % 2)
                for c in range(2):
                    s = prob[:, h % 2, c * 384:(c + 1) * 384]
                    b = bank[4 + c]
                    nc.vector.tensor_tensor(s[:, 0:P], b[:, 0:P], mask[:, P:2 * P], ALU.add)
                    link(nc.vector.tensor_tensor(s[:, P:3 * P], b[:, P:3 * P], mask, ALU.add))
                    nc.vector.tensor_reduce(stat[:, m + 2 * c:m + 2 * c + 1], s[:, 0:P], AX_X, ALU.max)
                    link(nc.vector.tensor_reduce(stat[:, m + 2 * c + 1:m + 2 * c + 2], s[:, P:3 * P], AX_X, ALU.max))
                nc.vector.tensor_scalar(stat[:, m:m + 4], stat[:, m:m + 4], -HD ** -0.5, None, ALU.mult).then_inc(max_ready, 1)

            def head_weights(h):
                m = 96 + 16 * (h % 2) + 4
                dve.wait_ge(exp_done, h + 1)
                link(nc.vector.reciprocal(stat[:, m:m + 4], stat[:, m:m + 4]))
                link(nc.vector.tensor_scalar(stat[:, m + 2:m + 4], stat[:, m + 2:m + 4], nlam, None, ALU.mult))
                for t, (a, b) in enumerate(((0, P), (P, 3 * P))):
                    p0, p1 = prob[:, h % 2, a:b], prob[:, h % 2, 384 + a:384 + b]
                    link(nc.vector.tensor_scalar(p0, p0, stat[:, m + t:m + t + 1], None, ALU.mult))
                    ins = nc.vector.scalar_tensor_tensor(out=p0, in0=p1, scalar=stat[:, m + 2 + t:m + 3 + t], in1=p0,
                                                         op0=ALU.mult, op1=ALU.add)
                ins.then_inc(a_ready, 1)

            unit(20)
            head_max(0)
            head_weights(0)
            unit(21)
            for h in range(HEADS):
                if h + 1 < HEADS:
                    head_max(h + 1)
                unit(22 + 2 * h)
                if h + 1 < HEADS:
                    head_weights(h + 1)
                    unit(23 + 2 * h)
            dve.wait_ge(o_copied, HEADS)
            sq = region[2][:, 0:1024].rearrange("p (h n) -> p h n", h=HEADS)
            for t in range(NT):
                link(nc.vector.tensor_tensor(sq, O[:, t, :].rearrange("p (h n) -> p h n", h=HEADS),
                                             O[:, t, :].rearrange("p (h n) -> p h n", h=HEADS), ALU.mult))
                link(nc.vector.tensor_reduce(stat[:, 128 + 8 * t:136 + 8 * t], sq, AX_X, ALU.add))
            mean_square(12, slice(128, 144), P)
            rroot(12, slice(128, 144))
            for t in range(NT):
                o3 = O[:, t, :].rearrange("p (h n) -> p h n", h=HEADS)
                nc.vector.tensor_tensor(o3, o3, stat[:, 128 + 8 * t:136 + 8 * t].unsqueeze(2).to_broadcast([P, HEADS, P]),
                                        ALU.mult).then_inc(o_normed, 1)
            unit(37)
            unit(38)
            unit(39)
            for j in range(4):
                dve.wait_ge(oT_done, j + 1)
                t, h = divmod(j, 2)
                nc.vector.tensor_scalar(OT[:, 4 * h:4 * h + 4, t * P:(t + 1) * P],
                                        bank[3 + j][:, :].rearrange("p (k n) -> p k n", k=4), sub_col,
                                        1.0 - LAMBDA_INIT, ALU.mult, ALU.mult).then_inc(oT_copied, 1)
            for u in range(40, 44):
                unit(u)
            for u in range(44, 48):
                _, name, t, _ = UNITS[u]
                cols = slice(int(name[2]) * HALF, (int(name[2]) + 1) * HALF)
                dve.wait_ge(unit_done, u + 1)
                nc.vector.tensor_tensor(X[:, t, cols], UB[u % 3][:, :], X[:, t, cols], ALU.add).then_inc(h_ready, 1)
            dve.wait_ge(squares, 6)
            mean_square(13, slice(4, 6), D)
            rroot(13, slice(4, 6))
            dve.wait_ge(late_in, 32)
            for t in range(NT):
                nc.vector.scalar_tensor_tensor(
                    out=HN[:, t, :, :], in0=X[:, t, :].rearrange("p (n k) -> p k n", k=KD), scalar=stat[:, 4 + t:5 + t],
                    in1=GFF.rearrange("p (n k) -> p k n", k=KD), op0=ALU.mult, op1=ALU.mult).then_inc(hn_ready, 1)
            dve.wait_ge(logit_done, 1)
            link(nc.vector.tensor_tensor(LG, bank[7][:, 0:2 * EXPERTS].rearrange("p (t e) -> p t e", t=NT),
                                         b_rt.unsqueeze(1).to_broadcast([P, NT, EXPERTS]), ALU.add))
            top = [stat[:, 160 + 8 * t:168 + 8 * t] for t in range(NT)]
            for t in range(NT):
                link(nc.vector.max(top[t], LG[:, t, :]))
            for t in range(NT):
                ins = nc.vector.tensor_scalar(stat[:, 180 + t:181 + t], top[t][:, 0:1], -1.0, None, ALU.mult)
            ins.then_inc(top_ready, 1)
            for t in range(NT):
                fourth = top[t][:, TOP_K - 1:TOP_K]
                above, equal, run, zero = (SCR[:, i, :] for i in range(4))
                count = stat[:, 184 + t:185 + t]
                if t:
                    dve.wait_ge(mask_ready, t)
                nc.vector.memset(zero, 0.0)
                nc.vector.tensor_scalar(above, LG[:, t, :], fourth, None, ALU.is_gt)
                link(nc.vector.tensor_scalar(equal, LG[:, t, :], fourth, None, ALU.is_equal))
                nc.vector.tensor_reduce(count, above, AX_X, ALU.add)
                link(nc.vector.tensor_tensor_scan(run, equal, zero, 0.0, ALU.add, ALU.add))
                link(nc.vector.tensor_scalar(run, run, count, float(TOP_K), ALU.add, ALU.is_le))
                link(nc.vector.tensor_tensor(equal, equal, run, ALU.mult))
                nc.vector.tensor_tensor(MASK[:, t, :], above, equal, ALU.add).then_inc(mask_ready, 1)
            dve.wait_ge(mask_ready, 2)
            dve.wait_ge(lexp_done, 2)
            link(nc.vector.tensor_tensor(GATE, GATE, MASK, ALU.mult))
            link(nc.vector.tensor_reduce(stat[:, 188:190], GATE, AX_X, ALU.add))
            link(nc.vector.reciprocal(stat[:, 188:190], stat[:, 188:190]))
            nc.vector.tensor_tensor(GATE, GATE, stat[:, 188:190].unsqueeze(2).to_broadcast([P, NT, EXPERTS]),
                                    ALU.mult).then_inc(gate_ready, 1)
            dve.wait_ge(gate_ready, 1)
            dve.wait_ge(rank_done, 1)
            link(nc.vector.scalar_tensor_tensor(out=RANK, in0=bank[3][:, 0:64].rearrange("p (t e) -> p t e", t=NT), scalar=1.0,
                                                in1=MASK, op0=ALU.add, op1=ALU.mult))
            link(nc.vector.tensor_reduce(stat[:, 190:191], bank[3][:, 64:96], AX_X, ALU.max))
            nc.vector.tensor_scalar(stat[:, 192:193], stat[:, 190:191], float(SLOTS), 1.0, ALU.is_gt, ALU.add)
            nc.vector.tensor_scalar(stat[:, 193:194], stat[:, 190:191], float(2 * SLOTS), None, ALU.is_gt)
            link(nc.vector.tensor_scalar(stat[:, 194:195], stat[:, 190:191], float(3 * SLOTS), None, ALU.is_gt))
            link(nc.vector.tensor_reduce(stat[:, 191:192], stat[:, 192:195], AX_X, ALU.add))
            nc.vector.tensor_copy(rounds[:, :], stat[:, 191:192]).then_inc(rounds_ready, 1)
            link(nc.vector.tensor_scalar(RANK, RANK, -1.0, None, ALU.add))

            def next_round_pair():
                nc.vector.tensor_scalar(RANKS[:, :, EXPERTS:EXPERTS + 2], RANK[:, :, 0:2], -float(SLOTS), None,
                                        ALU.add).then_inc(rank_ready, 1)

            def build_slots(first):
                for t in range(NT):
                    for e in range(2):
                        cols = slice(e * SLOTS, (e + 1) * SLOTS)
                        rank = RANKS[:, t, bass.ds(first + e, 1)]
                        nc.vector.tensor_scalar(PT[:, t, cols], iota[:, cols], rank, None,
                                                ALU.is_equal).then_inc(slots_built, 1)
                        nc.vector.tensor_scalar(PW[:, t, cols], iota[:, cols], rank, GATES[:, t, bass.ds(first + e, 1)],
                                                ALU.is_equal, ALU.mult).then_inc(slots_built, 1)

            next_round_pair()
            nc.vector.tensor_copy(GATES[:, :, EXPERTS:EXPERTS + 2], GATE[:, :, 0:2]).then_inc(rank_ready, 1)
            dve.wait_ge(rank_ready, 2)
            build_slots(0)
            for c in (200, 203):
                nc.vector.memset(stat[:, c:c + 1], 0.0).then_inc(y_added, 1)
                nc.vector.memset(stat[:, c + 1:c + 2], 0.0).then_inc(o_hi, 1)
                nc.vector.memset(stat[:, c + 2:c + 3], 0.0).then_inc(o_lo, 1)
            dve.wait_ge(rounds_ready, 1)
            n_rounds = dve.value_load(rounds[0:1, 0:1], min_val=1, max_val=SEQ // SLOTS)

            def add_results(count):
                for j in range(4):
                    t, h = divmod(j, 2)
                    dve.wait_ge(comb_done, count + (j + 1))
                    nc.vector.tensor_tensor(X[:, t, h * HALF:(h + 1) * HALF], bank[6 + j % 2][:, :],
                                            X[:, t, h * HALF:(h + 1) * HALF], ALU.add).then_inc(y_added, 1)

            with dve.Fori(0, n_rounds) as r:
                with dve.Fori(0, PAIRS) as i:
                    it = r * PAIRS + i
                    dve.wait_ge(disp_done, it * 2 + 2)
                    nc.vector.tensor_copy(XE[:, 4:8, :], bank[5][:, :].rearrange("p (k n) -> p k n", k=4)).then_inc(xe_hi, 1)
                    add_results(it * 4)
                    dve.wait_ge(slots_free, it + 1)
                    build_slots(i * 2 + 2)
                    for e in range(2):
                        dve.wait_ge(used, it * PER_PAIR + (4 * e + 2))
                        nc.vector.tensor_scalar(GS, bank[0][:, :], LIMIT, None, ALU.min).then_inc(g_read, 1)
                        dve.wait_ge(sig_done, it * 2 + (e + 1))
                        dve.wait_ge(g_read, it * 2 + (e + 1))
                        nc.vector.tensor_tensor(SG, SG, GS, ALU.mult).then_inc(gs_done, 1)
                        dve.wait_ge(used, it * PER_PAIR + (4 * e + 4))
                        if e:
                            dve.wait_ge(act_ready, it * 2 + 1)
                        nc.vector.tensor_scalar(US, bank[1][:, :], LIMIT, -LIMIT, ALU.min, ALU.max).then_inc(u_read, 1)
                        dve.wait_ge(u_read, it * 2 + (e + 1))
                        dve.wait_ge(gs_done, it * 2 + (e + 1))
                        nc.vector.scalar_tensor_tensor(out=AH[:, e, :], in0=US, scalar=1.0, in1=SG, op0=ALU.add,
                                                       op1=ALU.mult).then_inc(act_ready, 1)
                    for e in range(2):
                        dve.wait_ge(used, it * PER_PAIR + (10 + 2 * e))
                        nc.vector.tensor_copy(OE[e * SLOTS:(e + 1) * SLOTS, HALF:D], bank[2][SLOTS:2 * SLOTS, :]).then_inc(o_hi, 1)
                dve.wait_ge(slots_built, (r + 1) * (8 * PAIRS) + 8)
                nc.vector.tensor_scalar(RANK, RANK, -float(SLOTS), None, ALU.add).then_inc(rank_ready, 1)
                dve.wait_ge(rank_ready, r * 2 + 3)
                next_round_pair()
                dve.wait_ge(rank_ready, r * 2 + 4)
            add_results(n_rounds * (4 * PAIRS))

        @block.tensor
        def _(pe):
            def turn4(dst, srcs, signal):
                for b in range(4):
                    ins = nc.tensor.transpose(dst[:, b * P:(b + 1) * P], srcs[b], ident)
                ins.then_inc(signal, 1)

            stationary = {}
            for name in PIECES:
                stationary[name] = {"mk": MEMT, "mv": MEMT, "wbp": Z2T, "wbm": OMT, "wba0": OT, "wba1": OT,
                                    "wo0": MGT, "wo1": MGT}.get(name, XNT)

            def unit(u):
                n, name, t, c = UNITS[u]
                k_n = 4 if name in ("wbp", "wbm") else KD
                if u - 3 >= UNIT_OF[("wo0", 0, 0)]:
                    pe.wait_ge(h_ready, u - 3 - UNIT_OF[("wo0", 0, 0)] + 1)
                elif u >= 3:
                    pe.wait_ge(bank_read[u % 3], u // 3)
                pe.wait_ge(ring_in[n % RING], 16 * (n // RING + 1))
                w = slot_k(n)
                for k in range(k_n):
                    ins = nc.tensor.matmul(UB[u % 3][:, :], stationary[name][:, k, t * P:(t + 1) * P],
                                           w[:, k, c * HALF:(c + 1) * HALF], start=(k == 0), stop=(k == k_n - 1))
                ins.then_inc(unit_done, 1)

            pe.wait_ge(con_in, 16 * 5)
            for j in range(4):
                t, h = divmod(j, 2)
                pe.wait_ge(xhat_ready, t + 1)
                turn4(bank[3 + j], [XH[:, t, 4 * h + b, :] for b in range(4)], xT_done)
            pe.wait_ge(xT_copied, 4)
            unit(0)
            unit(1)
            for j in range(4):
                t, h = divmod(j, 2)
                pe.wait_ge(xhat_ready, 2 + t + 1)
                turn4(bank[3 + j], [MH[:, t, 4 * h + b, :] for b in range(4)], mT_done)
            pe.wait_ge(mT_copied, 4)
            for u in range(2, 8):
                unit(u)
            pe.wait_ge(vec_in, 16 * 9)
            for j in range(2):
                for g in (2 * j, 2 * j + 1):
                    for t in range(NT):
                        ins = nc.tensor.matmul(bank[4 + j][:, (g % 2) * SEQ:(g % 2 + 1) * SEQ], U[:, t, g * P:(g + 1) * P],
                                               BAND[:, t, g, :], start=(t == 0), stop=(t == NT - 1))
                ins.then_inc(z_done, 1)
            unit(8)
            unit(9)
            for j in range(2):
                pe.wait_ge(zT_copied, 2)
                for g in (2 * j, 2 * j + 1):
                    ins = nc.tensor.matmul(bank[4 + j][:, (g % 2) * SEQ:(g % 2 + 1) * SEQ], POOLW[:, g, :], ZT[:, g, :],
                                           start=True, stop=True)
                ins.then_inc(z2_done, 1)
            unit(10)
            unit(11)
            for j, (rows_, t) in enumerate(((KM, 0), (KM, 1), (QM, 0), (QM, 1))):
                pe.wait_ge(mem_normed, j // 2 + 1)
                pe.wait_ge(z2T_copied, 2)
                turn4(bank[(3, 6, 4, 5)[j]], [rows_[:, t, h * P:(h + 1) * P] for h in range(MHEADS)], kq_done)
            unit(12)
            unit(13)

            def mem_scores(h):
                if h == 0:
                    pe.wait_ge(kqT_copied, 4)
                if h >= 2:
                    pe.wait_ge(mexp_done, h - 1)
                for t in range(NT):
                    ins = nc.tensor.matmul(bank[4 + h % 2][:, t * SEQ:(t + 1) * SEQ], QMT[:, h, t * P:(t + 1) * P], KMT[:, h, :],
                                           start=True, stop=True)
                ins.then_inc(ms_done, 1)

            def mem_turn(h):
                if h >= 1:
                    pe.wait_ge(pt_copied, h)
                pe.wait_ge(mp_ready, h + 1)
                turn4(bank[6], [prob[:, h % 2, t * SEQ + m * P:t * SEQ + (m + 1) * P] for m in range(2) for t in range(NT)], mt_done)

            def mem_values(h):
                if h >= 1:
                    pe.wait_ge(omT_copied, h)
                pe.wait_ge(pt_copied, h + 1)
                for m in range(2):
                    ins = nc.tensor.matmul(bank[7][:, 0:SEQ], VM[:, m, h * P:(h + 1) * P], probT[:, h % 2, m * SEQ:(m + 1) * SEQ],
                                           start=(m == 0), stop=(m == 1))
                ins.then_inc(mo_done, 1)

            mem_scores(0)
            unit(14)
            mem_scores(1)
            mem_turn(0)
            unit(15)
            mem_values(0)
            mem_scores(2)
            mem_turn(1)
            unit(16)
            mem_values(1)
            mem_scores(3)
            mem_turn(2)
            unit(17)
            mem_values(2)
            mem_turn(3)
            unit(18)
            mem_values(3)
            unit(19)

            def turn_qk(h):
                if h == 0:
                    pe.wait_ge(normed, 8)
                else:
                    pe.wait_ge(qkT_copied, h)
                turn4(bank[3], [r[:, t, h * P:(h + 1) * P] for r in (Q, K) for t in range(NT)], qk_done)

            def scores(h):
                pe.wait_ge(qkT_copied, h + 1)
                if h >= 1:
                    pe.wait_ge(max_ready, h)
                else:
                    pe.wait_ge(mexp_done, MHEADS)
                for c in range(2):
                    part = qkt[c * HD:(c + 1) * HD, h % 2, :]
                    nc.tensor.matmul(bank[4 + c][:, 0:P], part[:, 0:P], part[:, SEQ:SEQ + P], start=True, stop=True)
                    ins = nc.tensor.matmul(bank[4 + c][:, P:3 * P], part[:, P:SEQ], part[:, SEQ:2 * SEQ], start=True, stop=True)
                ins.then_inc(sc_done, 1)

            def turn_a(h):
                pe.wait_ge(a_ready, h + 1)
                if h >= 1:
                    pe.wait_ge(at_copied, h)
                else:
                    pe.wait_ge(pt_copied, MHEADS)
                for b in range(3):
                    ins = nc.tensor.transpose(bank[6][:, b * P:(b + 1) * P], prob[:, h % 2, b * P:(b + 1) * P], ident)
                ins.then_inc(at_done, 1)

            def values(h):
                pe.wait_ge(at_copied, h + 1)
                if h >= 1:
                    pe.wait_ge(o_copied, h)
                else:
                    pe.wait_ge(omT_copied, MHEADS)
                cols = slice(h * P, (h + 1) * P)
                nc.tensor.matmul(bank[7][:, 0:P], probT[:, h % 2, 0:P], V[:, 0, cols], start=True, stop=True)
                nc.tensor.matmul(bank[7][:, P:2 * P], probT[:, h % 2, P:2 * P], V[:, 0, cols], start=True, stop=False)
                nc.tensor.matmul(bank[7][:, P:2 * P], probT[:, h % 2, 2 * P:3 * P], V[:, 1, cols], start=False,
                                 stop=True).then_inc(pv_done, 1)

            turn_qk(0)
            unit(20)
            scores(0)
            turn_qk(1)
            unit(21)
            pe.wait_ge(bank_read[19 % 3], 19 // 3 + 1)
            for h in range(HEADS):
                if h == 1:
                    pe.wait_ge(z2T_copied, 2)
                if h + 1 < HEADS:
                    scores(h + 1)
                if h == 0:
                    pe.wait_ge(omT_copied, MHEADS)
                unit(22 + 2 * h)
                turn_a(h)
                if h + 2 < HEADS:
                    turn_qk(h + 2)
                if h == HEADS - 1:
                    values(h)
                unit(23 + 2 * h)
                if h < HEADS - 1:
                    values(h)
            unit(38)
            unit(39)
            for j in range(4):
                t, h = divmod(j, 2)
                pe.wait_ge(o_normed, t + 1)
                turn4(bank[3 + j], [O[:, t, (4 * h + b) * P:(4 * h + b + 1) * P] for b in range(4)], oT_done)
            pe.wait_ge(oT_copied, 4)
            for u in range(40, 44):
                unit(u)
            pe.wait_ge(merged, 8)
            for j in range(4):
                t, h = divmod(j, 2)
                turn4(bank[3 + j], [MG[:, t, (4 * h + b) * P:(4 * h + b + 1) * P] for b in range(4)], mgT_done)
            pe.wait_ge(mgT_copied, 4)
            for u in range(44, 48):
                unit(u)
            for j in range(4):
                t, h = divmod(j, 2)
                pe.wait_ge(hn_ready, t + 1)
                turn4(bank[3 + j], [HN[:, t, 4 * h + b, :] for b in range(4)], hT_done)
            pe.wait_ge(hT_copied, 4)
            pe.wait_ge(late_in, 32)
            for t in range(NT):
                for k in range(KD):
                    ins = nc.tensor.matmul(bank[7][:, t * EXPERTS:(t + 1) * EXPERTS], HNT[:, k, t * P:(t + 1) * P], WR[:, k, :],
                                           start=(k == 0), stop=(k == KD - 1))
            ins.then_inc(logit_done, 1)
            pe.wait_ge(mask_ready, 2)
            for cols, parts in ((slice(0, 32), ((tri, 0),)), (slice(32, 64), ((ones, 0), (tri, 1))), (slice(64, 96), ((ones, 0), (ones, 1)))):
                for n, (m, t) in enumerate(parts):
                    ins = nc.tensor.matmul(bank[3][:, cols], m, MASK[:, t, :], start=(n == 0), stop=(n == len(parts) - 1))
            ins.then_inc(rank_done, 1)
            pe.wait_ge(gate_ready, 1)
            for t in range(NT):
                ins = nc.tensor.transpose(bank[4][0:EXPERTS, t * P:(t + 1) * P], GATE[:, t, :], ident)
            ins.then_inc(gT_done, 1)
            pe.wait_ge(seed_in, 16)
            pe.wait_ge(rounds_ready, 1)
            n_rounds = pe.value_load(rounds[0:1, 0:1], min_val=1, max_val=SEQ // SLOTS)

            def combine(it):
                pe.wait_ge(o_lo, it * 2 + 2)
                pe.wait_ge(o_hi, it * 2 + 2)
                pe.wait_ge(wT_copied, it + 1)
                for j in range(4):
                    t, h = divmod(j, 2)
                    pe.wait_ge(y_added, it * 4 + (j + 1))
                    nc.tensor.matmul(bank[6 + j % 2][:, :], PWT[:, t * P:(t + 1) * P], OE[:, h * HALF:(h + 1) * HALF],
                                     start=True, stop=True).then_inc(comb_done, 1)

            def project(it, e, m, first, dst):
                row = 2 * m + e
                for j in (first, first + 1):
                    s = moe_slot(j)
                    pe.wait_ge(ring_in[s], moe_landed(it, j))
                    w = ring[:, s, :].rearrange("p (k n) -> p k n", k=4)
                    for k in range(4):
                        kk = 4 * (j - first) + k
                        for h in range(2):
                            ins = nc.tensor.matmul(dst[h * SLOTS:(h + 1) * SLOTS, :], XE[:, kk, e * SLOTS:(e + 1) * SLOTS],
                                                   w[:, k, h * HALF:(h + 1) * HALF], start=(kk == 0), stop=False)
                    if j == first:
                        ins.then_inc(used, 1)
                for h in range(2):
                    ins = nc.tensor.matmul(dst[h * SLOTS:(h + 1) * SLOTS, :], sel[:, row, :],
                                           B4[:, h * HALF:(h + 1) * HALF], start=False, stop=True)
                ins.then_inc(used, 1)

            with pe.Fori(0, n_rounds) as r:
                with pe.Fori(0, PAIRS) as i:
                    it = r * PAIRS + i
                    pe.wait_ge(slots_built, it * 8 + 8)
                    pe.wait_ge(wT_copied, it + 1)
                    for half in range(2):
                        for b in range(4):
                            for t in range(NT):
                                ins = nc.tensor.matmul(bank[4 + half][:, b * P:(b + 1) * P], HN[:, t, 4 * half + b, :], PT[:, t, :],
                                                       start=(t == 0), stop=(t == NT - 1))
                        ins.then_inc(disp_done, 1)
                    combine(it)
                    for t in range(NT):
                        ins = nc.tensor.transpose(bank[3][:, t * P:(t + 1) * P], PW[:, t, :], ident)
                    ins.then_inc(slots_free, 1)
                    pe.wait_ge(xe_lo, it + 1)
                    pe.wait_ge(xe_hi, it + 1)
                    pe.wait_ge(bias_in, it * 32 + 32)
                    project(it, 0, 0, 0, bank[0])
                    project(it, 0, 1, 2, bank[1])
                    pe.wait_ge(g_read, it * 2 + 1)
                    project(it, 1, 0, 4, bank[0])
                    pe.wait_ge(u_read, it * 2 + 1)
                    project(it, 1, 1, 6, bank[1])
                    for e in range(2):
                        pe.wait_ge(act_ready, it * 2 + (e + 1))
                        if e == 0:
                            pe.wait_ge(wT_copied, it + 2)
                        turn4(bank[3], [AH[:, e, j * P:(j + 1) * P] for j in range(4)], actT_done)
                        if e == 1:
                            pe.wait_ge(o_lo, it * 2 + 3)
                            pe.wait_ge(o_hi, it * 2 + 3)
                        pe.wait_ge(actT_copied, it * 2 + (e + 1))
                        for j in (8 + 2 * e, 9 + 2 * e):
                            s = moe_slot(j)
                            pe.wait_ge(ring_in[s], moe_landed(it, j))
                            w = ring[:, s, :].rearrange("p (k n) -> p k n", k=4)
                            half = j % 2
                            for k in range(4):
                                for h in range(2):
                                    ins = nc.tensor.matmul(bank[2][h * SLOTS:(h + 1) * SLOTS, :],
                                                           AHT[:, k, half * SLOTS:(half + 1) * SLOTS],
                                                           w[:, k, h * HALF:(h + 1) * HALF], start=(half == 0 and k == 0),
                                                           stop=(half == 1 and k == 3))
                            ins.then_inc(used, 1)
            combine(n_rounds * PAIRS)


_INS = ["x", "mem", "g_mix", "w_in", "b_gates", "q_norm", "k_norm", "lambda_q1", "lambda_k1", "lambda_q2", "lambda_k2",
        "g_subln", "pool_w", "pool_scale", "g_mem", "w_mem_kv", "mq_norm", "mk_norm", "w_b_attn", "w_b_pool", "w_b_mem",
        "w_out", "g_ffn", "w_router", "b_router", "w_gate", "b_gate", "w_up", "b_up", "w_down", "b_down"]


def kernel(**inputs):
    import concourse.bacc as bacc
    from concourse.bass_utils import run_bass_kernel_spmd

    nc = bacc.Bacc("TRN2", target_bir_lowering=False, num_devices=1)
    table, band = constants()
    arrays, args = {}, []
    for name in _INS + ["table", "band"]:
        a = {"table": table, "band": band}.get(name)
        a = np.ascontiguousarray(inputs[name]) if a is None else a
        arrays[f"in_{name}"] = a
        args.append(nc.dram_tensor(f"in_{name}", a.shape, mybir.dt.from_np(a.dtype), kind="ExternalInput").ap())
    args.append(nc.dram_tensor("out_0", (1, SEQ, D), F32, kind="ExternalOutput").ap())
    decoder_layer(nc, *args)
    r = run_bass_kernel_spmd(nc, [arrays], core_ids=[0])
    return r.results[0]["out_0"]
```

```python
from contextlib import ExitStack

import numpy as np

import concourse.bass as bass
from concourse import mybir

F32 = mybir.dt.float32
F32R = mybir.dt.float32r
I32 = mybir.dt.int32
ALU = mybir.AluOpType
ACT = mybir.ActivationFunctionType
AX_X = mybir.AxisListType.X

P = 128
SEQ, D = 256, 1024
NT = SEQ // P
KD = D // P
HALF = 512
HEADS, HD = 8, 64
MHEADS, MHD = 4, 128
GROUPS = 4
WINDOWS = (2, 4, 8, 16)
EXPERTS, TOP_K = 32, 4
SLOTS = 64
PAIRS = EXPERTS // 2
EPS = 1e-6
LAMBDA_INIT = 0.2
LIMIT, ALPHA = 7.0, 1.702
NEG = -1e30

PIECES = ["pool", "mk", "mv", "qm", "q0", "q1", "k0", "k1", "v0", "v1", "gp0", "gp1", "wbp",
          "gm0", "gm1", "wbm", "ga0", "ga1", "wba0", "wba1", "wo0", "wo1"]
RING = 6
PER_PAIR = 12
MOE_SLOT = (5, 4, 0, 2, 1, 3)
HALVES = 5
HI_SLOT = (0, 1, 2, 3, 9)
RAW_SLOT = (4, 5, 6, 7, 8)
XLO_SLOT, LO_SLOT = 10, 11
BY_ACT = 23
EARLY = 3
UNITS = []
LAST_UNIT = []
for _n, _name in enumerate(PIECES):
    _cuts = 2 if _name in ("wbp", "wbm") else 1
    for _c in range(_cuts):
        for _t in range(NT):
            UNITS.append((_n, _name, _t, _c))
    LAST_UNIT.append(len(UNITS) - 1)
N_FULL = [sum(_m not in ("wbp", "wbm") for _m in PIECES[:_n + 1]) for _n in range(len(PIECES))]
UNIT_OF = {(name, t, c): u for u, (n, name, t, c) in enumerate(UNITS)}

C_ID, C_TRI, C_MASK, C_IOTA, C_COS, C_SIN, C_NSIN, C_SEL, C_ONE = 0, 128, 256, 512, 640, 704, 768, 832, 1088
C_ALL = 1216


def constants():
    c = np.zeros((P, C_ALL), np.float32)
    i = np.arange(P)
    c[:, C_ID:C_ID + P] = np.eye(P)
    c[:, C_TRI:C_TRI + P] = i[:, None] < i[None, :]
    c[:, C_MASK + P:C_MASK + 2 * P] = np.where(i[None, :] <= i[:, None], 0.0, NEG)
    c[:, C_IOTA:C_IOTA + P] = np.tile(np.arange(SLOTS), 2)[None, :]
    inv = np.float32(10000.0) ** (-np.arange(0, HD, 2, dtype=np.float32) / np.float32(HD))
    ang = (np.arange(SEQ, dtype=np.float32)[:, None] * inv[None, :].astype(np.float32)).astype(np.float32)
    for base, table in ((C_COS, np.cos(ang)), (C_SIN, np.sin(ang)), (C_NSIN, -np.sin(ang))):
        c[:, base:base + NT * HD // 2] = table.reshape(NT, P, HD // 2).transpose(1, 0, 2).reshape(P, -1)
    sel = (np.arange(4)[:, None, None] == np.arange(4)[None, :, None]) * np.ones((1, 1, SLOTS))
    c[0:4, C_SEL:C_SEL + 4 * SLOTS] = sel.reshape(4, -1)
    c[:, C_ONE:C_ONE + P] = 1.0
    band = np.zeros((SEQ, GROUPS, SEQ), np.float32)
    for g, w in enumerate(WINDOWS):
        for t in range(SEQ):
            band[max(0, t - w + 1):t + 1, g, t] = 1.0 / min(t + 1, w)
            band[t, g, t] -= 1.0
    return c, band


def decoder_layer(nc, x, mem, g_mix, w_in, b_gates, q_norm, k_norm, lambda_q1, lambda_k1, lambda_q2,
                  lambda_k2, g_subln, pool_w, pool_scale, g_mem, w_mem_kv, mq_norm, mk_norm, w_b_attn,
                  w_b_pool, w_b_mem, w_out, g_ffn, w_router, b_router, w_gate, b_gate, w_up, b_up,
                  w_down, b_down, table, band, out):
    with ExitStack() as ctx:
        def sb(name, shape, dt=F32):
            return ctx.enter_context(nc.sbuf_tensor(name, shape, dt))

        def sem(name):
            return ctx.enter_context(nc.semaphore(name))

        with ExitStack() as first_names:
            ring = first_names.enter_context(nc.sbuf_tensor("ring", [P, RING, 4096], F32))
            region = [first_names.enter_context(nc.sbuf_tensor(f"region{i}", [P, 2048], F32)) for i in range(11)]
        ring_r = sb("ring_split", [P, RING, 4096], F32R)
        region_r = [sb(f"region{i}_split", [P, 2048], F32R) for i in range(11)]
        half_slot = ring[:, :, :].rearrange("p s (h n) -> p (s h) n", h=2)
        half_slot_r = ring_r[:, :, :].rearrange("p s (h n) -> p (s h) n", h=2)
        con = sb("con", [P, C_ALL])
        small = sb("small", [P, 68])
        stat = sb("stat", [P, 208])
        rot = sb("rot", [P, 2, 2, NT, HD])
        gqk = sb("gqk", [P, 2, HD])
        qkt = region[9][:, 0:1024].rearrange("p (b n) -> p b n", b=2)
        prob = sb("prob", [P, 2, 768])
        probT = sb("probT", [P, 2, HALF])
        tmp = sb("tmp", [P, 2, HALF])
        rounds = sb("rounds", [P, 1], I32)

        ident = con[:, C_ID:C_ID + P]
        tri = con[:, C_TRI:C_TRI + P]
        ones = con[:, C_ONE:C_ONE + P]
        mask = con[:, C_MASK:C_MASK + 2 * P]
        iota = con[:, C_IOTA:C_IOTA + P]
        sel = con[0:4, C_SEL:C_SEL + 4 * SLOTS].rearrange("r (a s) -> r a s", a=4)

        minus_half = small[:, 3:4]
        mq_col, mk_col, sub_col = small[:, 0:1], small[:, 1:2], small[:, 2:3]
        psc_col = small[:, 4:8]
        nlam = small[:, 8:9]
        lam_e = small[:, 9:11]
        gain_col = [small[:, 12 + 8 * i:20 + 8 * i] for i in range(3)]
        b_rt = small[:, 36:68]

        def rows_r(i, k=KD):
            return region_r[i][:, :].rearrange("p (k n) -> p k n", k=k)

        def lo_pair(slot):
            return [x[:, slot, :].rearrange("p (k n) -> p k n", k=KD) for x in (half_slot, half_slot_r)]

        def rows(i, inner):
            return region[i][:, :].rearrange("p (t n) -> p t n", t=NT) if inner == "t" else \
                region[i][:, :].rearrange("p (k n) -> p k n", k=KD)

        X = rows(0, "t")
        XLO, XLO_R = lo_pair(XLO_SLOT)
        LO, LO_R = lo_pair(LO_SLOT)
        XNT = (rows_r(1), XLO_R, XLO)
        Q = rows(2, "t")
        MEM = rows(3, "t")
        K = rows(3, "t")
        MEMT = (rows_r(4), LO_R, LO)
        V = rows(4, "t")
        BAND = region[5][:, :].rearrange("p (t g n) -> p t g n", t=NT, g=GROUPS)
        O = rows(5, "t")
        U = region[6][:, 0:1024].rearrange("p (t n) -> p t n", t=NT)
        QM = region[6][:, 1024:2048].rearrange("p (t n) -> p t n", t=NT)
        KM = region[7][:, 0:1024].rearrange("p (t n) -> p t n", t=NT)
        VM = region[7][:, 1024:2048].rearrange("p (t n) -> p t n", t=NT)
        G = {"p": rows(6, "t"), "m": rows(7, "t"), "a": rows(6, "t")}
        MG = rows(8, "t")
        ZT = region[8][:, 0:1024].rearrange("p (g n) -> p g n", g=GROUPS)
        KMT = region[9][:, 0:1024].rearrange("p (h n) -> p h n", h=MHEADS)
        QMT = region[9][:, 1024:2048].rearrange("p (h n) -> p h n", h=MHEADS)
        OT = (rows_r(9), rows_r(2), rows(2, "k"))
        OMT = (rows_r(10)[:, 0:4, :], LO_R[:, 4:8, :], LO[:, 4:8, :])
        Z2T = (rows_r(10)[:, 4:8, :], LO_R[:, 0:4, :], LO[:, 0:4, :])
        MGT = (rows_r(10), rows_r(5), None)
        POOLW = region[10][:, 0:512].rearrange("p (g n) -> p g n", g=GROUPS)
        JUNK = region[8][:, 1024:2048]
        SQ = JUNK.rearrange("p (b n) -> p b n", b=2)

        HN = region[1][:, :].rearrange("p (t k n) -> p t k n", t=NT, k=KD)
        HNT = rows(2, "k")
        GFF = region[3][:, 0:1024]
        WR = region[3][:, 1024:1280].rearrange("p (k e) -> p k e", k=KD)
        LG = region[3][:, 1280:1344].rearrange("p (t e) -> p t e", t=NT)
        RG = region[3][:, 1792:1928].rearrange("p (a t e) -> p a t e", a=2, t=NT)
        RANKS, GATES = RG[:, 0], RG[:, 1]
        RANK, GATE = RANKS[:, :, 0:EXPERTS], GATES[:, :, 0:EXPERTS]
        MASK = region[3][:, 1408:1472].rearrange("p (t e) -> p t e", t=NT)
        SCR = region[3][:, 1536:1792].rearrange("p (a e) -> p a e", e=EXPERTS)
        XE = region[4][:, 0:1024].rearrange("p (k s) -> p k s", k=KD)
        OE = region[4][:, 1024:2048]
        GS, SG, US = region[5][:, 0:512], region[5][:, 512:1024], region[5][:, 1024:1536]
        AH = region[6][:, 0:1024].rearrange("p (e n) -> p e n", e=2)
        AHT = region[6][:, 1024:1536].rearrange("p (j s) -> p j s", j=4)
        PT = region[7][:, 0:256].rearrange("p (t s) -> p t s", t=NT)
        PW = region[7][:, 256:512].rearrange("p (t s) -> p t s", t=NT)
        PWT = region[7][:, 512:768]
        B4 = region[9][0:4, 0:1024]

        bank = [ctx.enter_context(nc.psum_tensor(f"bank{i}", [P, HALF], F32)) for i in range(8)]
        UB = bank[0:3]

        ident_in, x_in, mem_in, con_in, gain_in, mem_gain_in, vec_in, band_in, late_in = (sem(n) for n in (
            "ident_in", "x_in", "mem_in", "con_in", "gain_in", "mem_gain_in", "vec_in", "band_in", "late_in"))
        raw_in = [sem(f"raw_in{i}") for i in range(HALVES)]
        hi_act, hi_dve, lo_ready, lo_early, first_half_used = (sem(n) for n in ("hi_act", "hi_dve", "lo_ready", "lo_early", "first_half_used"))
        mgT_split = sem("mgT_split")
        ring_in = [sem(f"ring_in{i}") for i in range(RING)]
        gbias_in = [sem(f"gbias_in{i}") for i in range(3)]
        squares = sem("squares")
        exponent_ready, ms_ready, root_done = sem("exponent_ready"), sem("ms_ready"), sem("root_done")
        gms_ready, groot_done, sq_done = sem("gms_ready"), sem("groot_done"), sem("sq_done")
        xT_done, xT_copied = sem("xT_done"), sem("xT_copied")
        mT_done, mT_copied = sem("mT_done"), sem("mT_copied")
        unit_done = sem("unit_done")
        bank_read = [sem(f"bank_read{i}") for i in range(3)]
        z_done, zT_copied, z2_done, z2T_copied = (sem(n) for n in ("z_done", "zT_copied", "z2_done", "z2T_copied"))
        mem_normed, kq_done, kqT_copied = sem("mem_normed"), sem("kq_done"), sem("kqT_copied")
        ms_done, mmax_ready, mexp_done, mp_ready = (sem(n) for n in ("ms_done", "mmax_ready", "mexp_done", "mp_ready"))
        mt_done, pt_copied, mo_done, omT_copied = (sem(n) for n in ("mt_done", "pt_copied", "mo_done", "omT_copied"))
        rot_ready, normed = sem("rot_ready"), sem("normed")
        lam_sum, lam_exp = sem("lam_sum"), sem("lam_exp")
        qk_done, qkT_copied, sc_done, max_ready = (sem(n) for n in ("qk_done", "qkT_copied", "sc_done", "max_ready"))
        exp_done, a_ready, at_done, at_copied = (sem(n) for n in ("exp_done", "a_ready", "at_done", "at_copied"))
        pv_done, o_copied = sem("pv_done"), sem("o_copied")
        gexp_done, o_normed, oT_done, oT_copied = (sem(n) for n in ("gexp_done", "o_normed", "oT_done", "oT_copied"))
        merged, mgT_done, mgT_copied = sem("merged"), sem("mgT_done"), sem("mgT_copied")
        h_ready, hn_ready, hT_done, hT_copied = (sem(n) for n in ("h_ready", "hn_ready", "hT_done", "hT_copied"))
        logit_done, top_ready, lexp_done, mask_ready = (sem(n) for n in ("logit_done", "top_ready", "lexp_done", "mask_ready"))
        rank_done, gate_ready, gT_done, rounds_ready = (sem(n) for n in ("rank_done", "gate_ready", "gT_done", "rounds_ready"))
        seed_clear, seed_in = sem("seed_clear"), sem("seed_in")
        dve_step = sem("dve_step")
        slots_free, slots_built = sem("slots_free"), sem("slots_built")
        disp_done, xe_lo, xe_hi = sem("disp_done"), sem("xe_lo"), sem("xe_hi")
        comb_done, y_added, rank_ready, wT_copied = (sem(n) for n in ("comb_done", "y_added", "rank_ready", "wT_copied"))
        bias_in, used = sem("bias_in"), sem("used")
        g_read, sig_done, gs_done, u_read = (sem(n) for n in ("g_read", "sig_done", "gs_done", "u_read"))
        act_ready, actT_done, actT_copied = sem("act_ready"), sem("actT_done"), sem("actT_copied")
        o_lo, o_hi, out_done = sem("o_lo"), sem("o_hi"), sem("out_done")

        win = w_in.rearrange("(k p) n -> p k n", p=P)
        wkv = w_mem_kv.rearrange("(k p) n -> p k n", p=P)
        wba = w_b_attn.rearrange("(k p) n -> p k n", p=P)
        wo = w_out.rearrange("(k p) n -> p k n", p=P)
        src = {"pool": win[:, :, 3072:3584], "mk": wkv[:, :, 0:512], "mv": wkv[:, :, 512:1024],
               "qm": win[:, :, 3584:4096], "wbp": w_b_pool.rearrange("(k p) n -> p k n", p=P),
               "wbm": w_b_mem.rearrange("(k p) n -> p k n", p=P)}
        for h in range(2):
            for name, base in (("q", 0), ("k", 1024), ("v", 2048), ("ga", 4096), ("gp", 5120), ("gm", 6144)):
                src[f"{name}{h}"] = win[:, :, base + h * 512:base + h * 512 + 512]
            src[f"wba{h}"] = wba[:, :, h * 512:h * 512 + 512]
            src[f"wo{h}"] = wo[:, :, h * 512:h * 512 + 512]

        def half_source(H):
            n, h = divmod(H, 2)
            w = src[PIECES[n]]
            return w[:, :, h * HALF:(h + 1) * HALF] if PIECES[n] in ("wbp", "wbm") else w[:, 4 * h:4 * h + 4, :]

        def raw(H):
            return half_slot[:, RAW_SLOT[H % HALVES], :]

        def lower(H):
            return half_slot_r[:, RAW_SLOT[H % HALVES], :]

        def upper(H):
            return half_slot_r[:, HI_SLOT[H % HALVES], :]

        def upper_made(engine, H):
            if H < BY_ACT:
                engine.wait_ge(hi_act, H + 1)
            else:
                engine.wait_ge(hi_dve, H - BY_ACT + 1)

        def half_free(engine, H):
            n, h = divmod(H, 2)
            if h == 1:
                engine.wait_ge(unit_done, LAST_UNIT[n] + 1)
            elif PIECES[n] in ("wbp", "wbm"):
                engine.wait_ge(unit_done, LAST_UNIT[n] - 1)
            else:
                engine.wait_ge(first_half_used, N_FULL[n])

        N0 = len(PIECES)
        BATCH = ["gate", "gate", "up", "up"]

        def expert_piece(j):
            m, h = divmod(j, 2)
            which = [(w_gate, 0), (w_up, 0), (w_gate, 1), (w_up, 1), (w_down, 0), (w_down, 1)][m]
            return which[0], which[1], h

        def moe_slot(j):
            return MOE_SLOT[j % RING]

        def moe_landed(it, j):
            return it * (16 * PER_PAIR // RING) + 16 * (j // RING + 1)

        block = ctx.enter_context(nc.Block())

        @block.sync
        def _(sp):
            sp.dma_start(X[:, 0, :], x[0, 0:P, :]).then_inc(x_in, 16)
            sp.dma_start(X[:, 1, :], x[0, P:SEQ, :]).then_inc(x_in, 16)

            def load(H):
                if H >= HALVES:
                    half_free(sp, H - HALVES)
                sp.dma_start(raw(H).rearrange("p (k n) -> p k n", k=4), half_source(H)).then_inc(raw_in[H % HALVES], 16)

            load(0)
            load(1)
            sp.dma_start(MEM, mem[0].rearrange("(t p) n -> p t n", p=P)).then_inc(mem_in, 16)
            load(2)
            load(3)
            def row(v):
                return v.rearrange("(a n) -> a n", a=1)

            lam4 = tmp[:, 1, 0:4 * HD].rearrange("p (a n) -> p a n", a=4)
            with nc.allow_non_contiguous_dma(reason="short per-partition vectors"):
                sp.dma_start(gain_col[1], g_mem.rearrange("(k p) -> p k", p=P)).then_inc(mem_gain_in, 16)
                for a, v in enumerate((lambda_q1, lambda_k1, lambda_q2, lambda_k2)):
                    sp.dma_start(lam4[:, a, :], row(v).to_broadcast([P, HD])).then_inc(vec_in, 16)
                sp.dma_start(gqk[:, 0, :], row(q_norm).to_broadcast([P, HD])).then_inc(vec_in, 16)
                sp.dma_start(gqk[:, 1, :], row(k_norm).to_broadcast([P, HD])).then_inc(vec_in, 16)
                for dst, v in ((mq_col, mq_norm.rearrange("(p a) -> p a", a=1)), (mk_col, mk_norm.rearrange("(p a) -> p a", a=1)),
                               (sub_col, g_subln.rearrange("(p a) -> p a", a=1)), (psc_col, pool_scale.rearrange("(g p) -> p g", p=P)),
                               (gain_col[2], g_ffn.rearrange("(k p) -> p k", p=P)), (b_rt, row(b_router).to_broadcast([P, EXPERTS])),
                               (con[:, P:C_ALL], table[:, P:C_ALL])):
                    sp.dma_start(dst, v).then_inc(con_in, 16)
            load(4)
            sp.dma_start(BAND, band.rearrange("(t p) g n -> p t g n", p=P)).then_inc(band_in, 16)
            sp.dma_start(POOLW, pool_w.rearrange("g p n -> p g n")).then_inc(band_in, 16)
            for H in range(HALVES, 2 * N0):
                load(H)

            def load_expert(i, j):
                w, e, h = expert_piece(j)
                one = w[bass.ds(i * 2 + e, 1), :, :].rearrange("e r n -> (e r) n")
                if j < 8:
                    part = one.rearrange("(p k) n -> p k n", k=KD)[:, 4 * h:4 * h + 4, :]
                else:
                    part = one.rearrange("(k p) n -> p k n", p=P)[:, 4 * h:4 * h + 4, :]
                dst = ring[:, moe_slot(j), :].rearrange("p (k n) -> p k n", k=4)
                sp.dma_start(dst, part).then_inc(ring_in[moe_slot(j)], 16)

            def rest_of_pair(it, i):
                for j in range(RING, PER_PAIR):
                    sp.wait_ge(used, it * PER_PAIR + (j - RING + 1))
                    load_expert(i, j)

            def start_of_pair(it, i):
                for j in range(RING):
                    sp.wait_ge(used, it * PER_PAIR + (j - RING + 1))
                    if j == 1:
                        biases(i)
                    load_expert(i, j)

            def biases(i):
                sp.dma_start(B4[0:2, :], b_gate[bass.ds(i * 2, 2), :]).then_inc(bias_in, 16)
                sp.dma_start(B4[2:4, :], b_up[bass.ds(i * 2, 2), :]).then_inc(bias_in, 16)

            for j in range(RING):
                last = (UNIT_OF[("ga1", 1, 0)], UNIT_OF[("wba1", 1, 0)], UNIT_OF[("wo0", 1, 0)], UNIT_OF[("wo0", 1, 0)],
                        UNIT_OF[("wo1", 1, 0)], UNIT_OF[("wo1", 1, 0)])[j]
                sp.wait_ge(unit_done, last + 1)
                load_expert(0, j)
                if j == 3:
                    biases(0)

            def round_of(r):
                base = r * PAIRS
                with sp.Fori(0, PAIRS - 1) as i:
                    rest_of_pair(base + i, i)
                    start_of_pair(base + i + 1, i + 1)
                rest_of_pair(base + (PAIRS - 1), PAIRS - 1)

            round_of(0)
            sp.wait_ge(rounds_ready, 1)
            n_rounds = sp.value_load(rounds[0:1, 0:1], min_val=1, max_val=SEQ // SLOTS)
            with sp.If(n_rounds > 1):
                with sp.Fori(1, n_rounds) as r:
                    start_of_pair(r * PAIRS, 0)
                    round_of(r)
            sp.wait_ge(y_added, n_rounds * (4 * PAIRS) + 2 + 4)
            for t in range(NT):
                sp.dma_start(out[0, t * P:(t + 1) * P, :], X[:, t, :]).then_inc(out_done, 16)
            sp.wait_ge(out_done, 16 * NT)

        @block.gpsimd
        def _(pool):
            def root(n, cols):
                pool.wait_ge(ms_ready, n + 1)
                nc.gpsimd.tensor_tensor(stat[:, cols], stat[:, cols], minus_half.to_broadcast([P, cols.stop - cols.start]),
                                        ALU.pow).then_inc(root_done, 1)

            nc.gpsimd.memset(minus_half, -0.5).then_inc(exponent_ready, 1)
            def lower_parts(first, after):
                for H in range(first, after):
                    upper_made(pool, H)
                    nc.gpsimd.tensor_tensor(lower(H), raw(H), upper(H), ALU.subtract).then_inc(lo_ready, 1)

            pool.wait_ge(exponent_ready, 1)
            root(0, slice(0, 2))
            lower_parts(EARLY, 4)
            root(1, slice(2, 4))
            lower_parts(4, 8)
            pool.wait_ge(con_in, 16 * 7)
            pool.wait_ge(vec_in, 16 * 6)
            h = HD // 2

            def angles(base):
                return con[:, base:base + NT * h].rearrange("p (t n) -> p t n", t=NT)

            for w in range(2):
                lo = gqk[:, w, 0:h].unsqueeze(1).to_broadcast([P, NT, h])
                hi = gqk[:, w, h:HD].unsqueeze(1).to_broadcast([P, NT, h])
                for o, a, b in ((rot[:, w, 0, :, 0:h], lo, angles(C_COS)), (rot[:, w, 0, :, h:HD], hi, angles(C_COS)),
                                (rot[:, w, 1, :, 0:h], hi, angles(C_NSIN)), (rot[:, w, 1, :, h:HD], lo, angles(C_SIN))):
                    nc.gpsimd.tensor_tensor(o, a, b, ALU.mult).then_inc(rot_ready, 1)

            def gate_bias(n, branch, first):
                for t in range(NT):
                    pool.dma_start(G[branch][:, t, :], b_gates[first:first + D].rearrange("(a n) -> a n", a=1)
                                   .to_broadcast([P, D])).then_inc(gbias_in[n], 16)

            lower_parts(8, 20)
            pool.wait_ge(kq_done, 4)
            pool.wait_ge(z_done, 2)
            gate_bias(0, "p", D)
            lower_parts(20, 23)
            pool.wait_ge(mo_done, MHEADS)
            gate_bias(1, "m", 2 * D)
            lower_parts(23, 30)
            last = UNIT_OF[("wbp", 1, 1)]
            pool.wait_ge(bank_read[last % 3], last // 3 + 1)
            gate_bias(2, "a", 0)

            lower_parts(30, 37)
            pool.wait_ge(pv_done, HEADS)
            nc.gpsimd.memset(OE, 0.0).then_inc(seed_clear, 1)
            root(2, slice(128, 144))
            lower_parts(37, 41)
            pool.wait_ge(merged, 4)
            pool.wait_ge(seed_clear, 1)
            pool.dma_start(OE[0:EXPERTS, :], b_down).then_inc(seed_in, 16)
            nc.gpsimd.memset(PWT, 0.0).then_inc(seed_clear, 1)
            pool.dma_start(GFF, g_ffn.rearrange("(a n) -> a n", a=1).to_broadcast([P, D])).then_inc(late_in, 16)
            pool.dma_start(WR, w_router.rearrange("(k p) e -> p k e", p=P)).then_inc(late_in, 16)
            lower_parts(41, 44)
            root(3, slice(4, 5))
            root(4, slice(5, 6))

        @block.scalar
        def _(act):
            act.dma_start(con[:, C_ID:C_ID + P], table[:, C_ID:C_ID + P]).then_inc(ident_in, 16)
            with nc.allow_non_contiguous_dma(reason="short per-partition vectors"):
                act.dma_start(gain_col[0], g_mix.rearrange("(k p) -> p k", p=P)).then_inc(gain_in, 16)

            def evac(u, dst):
                _, name, t, _ = UNITS[u]
                n = 1 if name in ("mk", "mv") else 0
                act.wait_ge(unit_done, u + 1)
                act.wait_ge(root_done, n + 1)
                nc.scalar.activation(dst, UB[u % 3][:, :], ACT.Copy, scale=stat[:, 2 * n + t:2 * n + t + 1]).then_inc(bank_read[u % 3], 1)

            def hi(H):
                act.wait_ge(raw_in[H % HALVES], 16 * (H // HALVES + 1))
                nc.scalar.activation(upper(H), raw(H), ACT.Copy).then_inc(hi_act, 1)

            def root(n, cols):
                act.wait_ge(gms_ready, n + 1)
                nc.scalar.activation(stat[:, cols], stat[:, cols], ACT.Sqrt).then_inc(groot_done, 1)

            def gate_exp(u):
                _, name, t, _ = UNITS[u]
                g = G[name[1]][:, t, int(name[2]) * HALF:(int(name[2]) + 1) * HALF]
                act.wait_ge(bank_read[u % 3], u // 3 + 1)
                nc.scalar.activation(g, g, ACT.Tanh, scale=0.5).then_inc(gexp_done, 1)

            act.wait_ge(x_in, 16 * NT)
            for t in range(NT):
                if t:
                    act.wait_ge(squares, t)
                nc.scalar.activation(JUNK, X[:, t, :], ACT.Square, accum_out=stat[:, t:t + 1]).then_inc(squares, 1)
            hi(0)
            hi(1)
            act.wait_ge(mem_in, 16)
            for t in range(NT):
                act.wait_ge(squares, 2 + t)
                nc.scalar.activation(JUNK, MEM[:, t, :], ACT.Square, accum_out=stat[:, 2 + t:3 + t]).then_inc(squares, 1)
            hi(2)
            hi(3)
            evac(0, U[:, 0, :])
            hi(4)
            evac(1, U[:, 1, :])
            hi(5)
            hi(6)
            evac(2, KM[:, 0, :])
            evac(3, KM[:, 1, :])
            hi(7)
            hi(8)
            evac(4, VM[:, 0, :])
            root(0, slice(8, 16))
            evac(5, VM[:, 1, :])
            hi(9)
            hi(10)
            evac(6, QM[:, 0, :])
            evac(7, QM[:, 1, :])
            hi(11)
            for j in range(2):
                act.wait_ge(z_done, j + 1)
                nc.scalar.activation(ZT[:, 2 * j:2 * j + 2, :], bank[4 + j][:, :].rearrange("p (g n) -> p g n", g=2),
                                     ACT.Copy).then_inc(zT_copied, 1)
            root(1, slice(16, 24))

            def qk_dst(u):
                _, name, t, _ = UNITS[u]
                return {"q": Q, "k": K, "v": V}[name[0]][:, t, int(name[1]) * HALF:(int(name[1]) + 1) * HALF]

            def qk_unit(u):
                if u % 2 == 0:
                    hi(u + 4)
                act.wait_ge(unit_done, u + 1)
                act.wait_ge(root_done, 1)
                if u >= 10:
                    act.wait_ge(gms_ready, u - 7)
                else:
                    act.wait_ge(squares, 4)
                t = UNITS[u][2]
                nc.scalar.activation(SQ[:, u % 2, :], UB[u % 3][:, :], ACT.Square, scale=stat[:, t:t + 1]).then_inc(sq_done, 1)
                evac(u, qk_dst(u))
                root(u - 6, slice(24 + 8 * (u % 2), 32 + 8 * (u % 2)))
                if u % 2 == 1:
                    hi(u + 4)

            for u in range(8, 14):
                qk_unit(u)
            act.wait_ge(lam_sum, 1)
            nc.scalar.activation(lam_e, lam_e, ACT.Exp).then_inc(lam_exp, 1)

            def mem_exp(h):
                act.wait_ge(mmax_ready, h + 1)
                for t in range(NT):
                    c = 64 + 4 * (h % 2) + t
                    ins = nc.scalar.activation(prob[:, h % 2, t * SEQ:(t + 1) * SEQ], bank[4 + h % 2][:, t * SEQ:(t + 1) * SEQ],
                                               ACT.Exp, bias=stat[:, c:c + 1], scale=MHD ** -0.5,
                                               accum_out=stat[:, c + 2:c + 3])
                ins.then_inc(mexp_done, 1)

            def mem_probT(h):
                act.wait_ge(mt_done, h + 1)
                nc.scalar.activation(probT[:, h % 2, :], bank[6][:, :], ACT.Copy).then_inc(pt_copied, 1)

            mem_exp(0)
            qk_unit(14)
            mem_exp(1)
            mem_probT(0)
            qk_unit(15)
            mem_exp(2)
            mem_probT(1)
            hi(20)
            evac(16, qk_dst(16))
            mem_exp(3)
            mem_probT(2)
            evac(17, qk_dst(17))
            hi(21)
            mem_probT(3)
            hi(22)
            evac(18, qk_dst(18))
            evac(19, qk_dst(19))

            def qkT(h):
                act.wait_ge(qk_done, h + 1)
                nc.scalar.activation(qkt[:, h % 2, :], bank[3][:, :], ACT.Copy).then_inc(qkT_copied, 1)

            def exps(h):
                act.wait_ge(max_ready, h + 1)
                for c in range(2):
                    for t, (a, b) in enumerate(((0, P), (P, 3 * P))):
                        s = prob[:, h % 2, c * 384 + a:c * 384 + b]
                        m = 96 + 16 * (h % 2) + 2 * c + t
                        ins = nc.scalar.activation(s, s, ACT.Exp, bias=stat[:, m:m + 1], scale=HD ** -0.5,
                                                   accum_out=stat[:, m + 4:m + 5])
                ins.then_inc(exp_done, 1)

            def aT(h):
                act.wait_ge(at_done, h + 1)
                nc.scalar.activation(probT[:, h % 2, 0:384], bank[6][:, 0:384], ACT.Copy).then_inc(at_copied, 1)

            def o_out(h):
                act.wait_ge(pv_done, h + 1)
                nc.scalar.activation(O[:, :, h * P:(h + 1) * P], bank[7][:, 0:256].rearrange("p (t n) -> p t n", t=NT),
                                     ACT.Copy).then_inc(o_copied, 1)

            qkT(0)
            gate_exp(20)
            exps(0)
            qkT(1)
            gate_exp(21)
            for h in range(HEADS):
                for_gate = [u for u in (22 + 2 * h, 23 + 2 * h) if UNITS[u][1][0] == "g"]
                if h + 1 < HEADS:
                    exps(h + 1)
                if 22 + 2 * h in for_gate:
                    gate_exp(22 + 2 * h)
                aT(h)
                if h + 2 < HEADS:
                    qkT(h + 2)
                if h == HEADS - 1:
                    o_out(h)
                if 23 + 2 * h in for_gate:
                    gate_exp(23 + 2 * h)
                if h < HEADS - 1:
                    o_out(h)
            gate_exp(38)
            gate_exp(39)
            for j in range(4):
                act.wait_ge(mgT_done, j + 1)
                t, h = divmod(j, 2)
                nc.scalar.activation(MGT[0][:, 4 * h:4 * h + 4, t * P:(t + 1) * P],
                                     bank[3 + j][:, :].rearrange("p (k n) -> p k n", k=4), ACT.Copy, scale=0.5).then_inc(mgT_copied, 1)
            def h_square(t):
                act.wait_ge(h_ready, 3 + t)
                act.wait_ge(squares, 4 + t)
                nc.scalar.activation(JUNK, X[:, t, :], ACT.Square, accum_out=stat[:, 4 + t:5 + t]).then_inc(squares, 1)

            h_square(0)
            for t in range(NT):
                act.wait_ge(top_ready, t + 1)
                nc.scalar.activation(GATE[:, t, :], LG[:, t, :], ACT.Exp, bias=stat[:, 180 + t:181 + t]).then_inc(lexp_done, 1)
                if t == 0:
                    h_square(1)
            act.wait_ge(gT_done, 1)
            act.wait_ge(seed_clear, 2)
            nc.scalar.activation(PWT[0:EXPERTS, :], bank[6][0:EXPERTS, 0:SEQ], ACT.Copy).then_inc(wT_copied, 1)
            act.wait_ge(rounds_ready, 1)
            n_rounds = act.value_load(rounds[0:1, 0:1], min_val=1, max_val=SEQ // SLOTS)
            with act.Fori(0, n_rounds) as r:
                with act.Fori(0, PAIRS) as i:
                    it = r * PAIRS + i
                    act.wait_ge(disp_done, it * 2 + 1)
                    nc.scalar.activation(XE[:, 0:4, :], bank[4][:, :].rearrange("p (k n) -> p k n", k=4),
                                         ACT.Copy).then_inc(xe_lo, 1)
                    act.wait_ge(slots_free, it + 1)
                    nc.scalar.activation(PWT, bank[3][:, 0:SEQ], ACT.Copy).then_inc(wT_copied, 1)
                    for e in range(2):
                        act.wait_ge(g_read, it * 2 + (e + 1))
                        nc.scalar.activation(SG, GS, ACT.Sigmoid, scale=ALPHA).then_inc(sig_done, 1)
                    for e in range(2):
                        act.wait_ge(actT_done, it * 2 + (e + 1))
                        nc.scalar.activation(AHT, bank[3][:, :].rearrange("p (j s) -> p j s", j=4),
                                             ACT.Copy).then_inc(actT_copied, 1)
                        act.wait_ge(used, it * PER_PAIR + (10 + 2 * e))
                        nc.scalar.activation(OE[e * SLOTS:(e + 1) * SLOTS, 0:HALF], bank[2][0:SLOTS, :],
                                             ACT.Copy).then_inc(o_lo, 1)

        @block.vector
        def _(dve):
            n_step = [0]

            def link(ins):
                n_step[0] += 1
                ins.then_inc(dve_step, 1)
                dve.wait_ge(dve_step, n_step[0])

            def mean_square(n, cols, width):
                nc.vector.tensor_scalar(stat[:, cols], stat[:, cols], 1.0 / width, EPS, ALU.mult, ALU.add).then_inc(ms_ready, 1)

            def group_root(n, cols, width):
                nc.vector.tensor_scalar(stat[:, cols], stat[:, cols], 1.0 / width, EPS, ALU.mult, ALU.add).then_inc(gms_ready, 1)
                dve.wait_ge(groot_done, n + 1)
                link(nc.vector.reciprocal(stat[:, cols], stat[:, cols]))

            def hi(H):
                dve.wait_ge(raw_in[H % HALVES], 16 * (H // HALVES + 1))
                nc.vector.tensor_copy(upper(H), raw(H)).then_inc(hi_dve, 1)

            def lo(H):
                upper_made(dve, H)
                nc.vector.tensor_tensor(lower(H), raw(H), upper(H), ALU.subtract).then_inc(lo_early, 1)

            def split(product, operand, blocks, cols, signal):
                high, low, place = (x[:, blocks, cols] for x in operand)
                link(product(place))
                link(nc.vector.tensor_copy(high, place))
                nc.vector.tensor_tensor(low, place, high, ALU.subtract).then_inc(signal, 1)

            def turned(n, j):
                dst, done, copied = ((XNT, xT_done, xT_copied), (MEMT, mT_done, mT_copied))[n]
                dve.wait_ge(done, j + 1)
                t, h = divmod(j, 2)
                split(lambda place: nc.vector.tensor_tensor(place, bank[3 + j][:, :].rearrange("p (k n) -> p k n", k=4),
                                                            gain_col[n][:, 4 * h:4 * h + 4].unsqueeze(2).to_broadcast([P, 4, P]),
                                                            ALU.mult),
                      dst, slice(4 * h, 4 * h + 4), slice(t * P, (t + 1) * P), copied)

            dve.wait_ge(gain_in, 16)
            turned(0, 0)
            turned(0, 1)
            lo(0)
            turned(0, 2)
            turned(0, 3)
            lo(1)
            dve.wait_ge(squares, 2)
            mean_square(0, slice(0, 2), D)
            dve.wait_ge(mem_gain_in, 16)
            turned(1, 0)
            turned(1, 1)
            lo(2)
            turned(1, 2)
            turned(1, 3)
            dve.wait_ge(squares, 4)
            mean_square(1, slice(2, 4), D)
            dve.wait_ge(vec_in, 16 * 6)
            lam4 = tmp[:, 1, 0:4 * HD].rearrange("p (a n) -> p a n", a=4)
            for a in range(2):
                link(nc.vector.tensor_tensor(tmp[:, 0, a * HD:(a + 1) * HD], lam4[:, 2 * a, :], lam4[:, 2 * a + 1, :], ALU.mult))
            nc.vector.tensor_reduce(lam_e, tmp[:, 0, 0:2 * HD].rearrange("p (a n) -> p a n", a=2), AX_X,
                                    ALU.add).then_inc(lam_sum, 1)

            def group_stats(rows3, groups, sq, col, width):
                link(nc.vector.tensor_tensor(sq, rows3, rows3, ALU.mult))
                link(nc.vector.tensor_reduce(stat[:, col:col + groups], sq, AX_X, ALU.add))

            dve.wait_ge(lam_sum, 1)
            for n, (rows_, first, col) in enumerate(((KM, 2, 8), (QM, 6, 16))):
                for u in (first, first + 1):
                    dve.wait_ge(bank_read[u % 3], u // 3 + 1)
                flat = rows_.rearrange("p t (h n) -> p (t h) n", n=MHD)
                group_stats(flat, 8, tmp[:, :, :].rearrange("p t (h n) -> p (t h) n", n=MHD), col, MHD)
                group_root(n, slice(col, col + 8), MHD)
                nc.vector.tensor_tensor(flat, flat, stat[:, col:col + 8].unsqueeze(2).to_broadcast([P, 8, MHD]),
                                        ALU.mult).then_inc(mem_normed, 1)

            def norm_rotate(u):
                _, name, t, _ = UNITS[u]
                w = 0 if name[0] == "q" else 1
                raw = (Q if w == 0 else K)[:, t, int(name[1]) * HALF:(int(name[1]) + 1) * HALF].rearrange("p (m n) -> p m n", n=HD)
                a = tmp[:, 0, :].rearrange("p (m n) -> p m n", n=HD)
                b = tmp[:, 1, :].rearrange("p (m n) -> p m n", n=HD)
                col = 24 + 8 * (u % 2)
                hf = HD // 2
                if u > 8:
                    dve.wait_ge(normed, u - 8)
                dve.wait_ge(bank_read[u % 3], u // 3 + 1)
                dve.wait_ge(sq_done, u - 7)
                link(nc.vector.tensor_reduce(stat[:, col:col + 8], SQ[:, u % 2, :].rearrange("p (m n) -> p m n", n=HD), AX_X, ALU.add))
                group_root(u - 6, slice(col, col + 8), HD)
                link(nc.vector.tensor_tensor(a, raw, stat[:, col:col + 8].unsqueeze(2).to_broadcast([P, 8, HD]), ALU.mult))
                nc.vector.tensor_tensor(b[:, :, 0:hf], a[:, :, hf:HD],
                                        rot[:, w, 1, t, 0:hf].unsqueeze(1).to_broadcast([P, 8, hf]), ALU.mult)
                link(nc.vector.tensor_tensor(b[:, :, hf:HD], a[:, :, 0:hf],
                                             rot[:, w, 1, t, hf:HD].unsqueeze(1).to_broadcast([P, 8, hf]), ALU.mult))
                link(nc.vector.tensor_tensor(a, a, rot[:, w, 0, t, :].unsqueeze(1).to_broadcast([P, 8, HD]), ALU.mult))
                nc.vector.tensor_tensor(raw, a, b, ALU.add).then_inc(normed, 1)

            dve.wait_ge(lam_sum, 1)
            dve.wait_ge(rot_ready, 8)
            norm_rotate(8)
            norm_rotate(9)
            dve.wait_ge(con_in, 16 * 7)
            for j in range(2):
                dve.wait_ge(z2_done, j + 1)
                split(lambda place: nc.vector.tensor_tensor(place, bank[4 + j][:, :].rearrange("p (g n) -> p g n", g=2),
                                                            psc_col[:, 2 * j:2 * j + 2].unsqueeze(2).to_broadcast([P, 2, SEQ]),
                                                            ALU.mult),
                      Z2T, slice(2 * j, 2 * j + 2), slice(0, SEQ), z2T_copied)
            norm_rotate(10)
            norm_rotate(11)
            for j, (dst, t, gain) in enumerate(((KMT, 0, mk_col), (KMT, 1, mk_col), (QMT, 0, mq_col), (QMT, 1, mq_col))):
                dve.wait_ge(kq_done, j + 1)
                nc.vector.tensor_scalar(dst[:, :, t * P:(t + 1) * P], bank[(3, 6, 4, 5)[j]][:, :].rearrange("p (h n) -> p h n", h=MHEADS),
                                        gain, None, ALU.mult).then_inc(kqT_copied, 1)
            norm_rotate(12)
            norm_rotate(13)

            def mem_max(h):
                c = 64 + 4 * (h % 2)
                dve.wait_ge(ms_done, h + 1)
                link(nc.vector.tensor_reduce(stat[:, c:c + 2], bank[4 + h % 2][:, :].rearrange("p (t n) -> p t n", t=NT), AX_X,
                                             ALU.max, negate=True))
                nc.vector.tensor_scalar(stat[:, c:c + 2], stat[:, c:c + 2], MHD ** -0.5, None, ALU.mult).then_inc(mmax_ready, 1)

            def mem_scale(h):
                c = 66 + 4 * (h % 2)
                dve.wait_ge(mexp_done, h + 1)
                link(nc.vector.reciprocal(stat[:, c:c + 2], stat[:, c:c + 2]))
                p = prob[:, h % 2, 0:HALF].rearrange("p (t n) -> p t n", t=NT)
                nc.vector.tensor_tensor(p, p, stat[:, c:c + 2].unsqueeze(2).to_broadcast([P, NT, SEQ]), ALU.mult).then_inc(mp_ready, 1)

            def mem_out(h):
                dve.wait_ge(mo_done, h + 1)
                split(lambda place: nc.vector.tensor_copy(place, bank[7][:, 0:SEQ]), OMT, h, slice(0, SEQ), omT_copied)

            mem_max(0)
            mem_scale(0)
            norm_rotate(14)
            mem_max(1)
            mem_scale(1)
            norm_rotate(15)
            mem_out(0)
            mem_max(2)
            mem_scale(2)
            mem_out(1)
            mem_max(3)
            mem_scale(3)
            mem_out(2)
            mem_out(3)
            dve.wait_ge(lam_exp, 1)
            link(nc.vector.tensor_tensor(nlam, lam_e[:, 1:2], lam_e[:, 0:1], ALU.subtract))
            link(nc.vector.tensor_scalar(nlam, nlam, -LAMBDA_INIT, None, ALU.add))

            def add_bias(u):
                _, name, t, _ = UNITS[u]
                g = G[name[1]][:, t, int(name[2]) * HALF:(int(name[2]) + 1) * HALF]
                dve.wait_ge(gbias_in["pma".index(name[1])], 16 * NT)
                dve.wait_ge(unit_done, u + 1)
                nc.vector.scalar_tensor_tensor(out=g, in0=UB[u % 3][:, :], scalar=stat[:, t:t + 1], in1=g, op0=ALU.mult,
                                               op1=ALU.add).then_inc(bank_read[u % 3], 1)

            gates_before = {}
            seen = 0
            for u, (_, name, t, _) in enumerate(UNITS):
                if name[0] == "g":
                    seen += 1
                    gates_before[(name[1], t, int(name[2]))] = seen

            def merge(u):
                _, name, t, c = UNITS[u]
                branch, n = {"wbp": ("p", c), "wbm": ("m", c), "wba0": ("a", 0), "wba1": ("a", 1)}[name]
                cols = slice(n * HALF, (n + 1) * HALF)
                g = G[branch][:, t, cols]
                dve.wait_ge(gexp_done, gates_before[(branch, t, n)])
                dve.wait_ge(unit_done, u + 1)
                dst = MG[:, t, cols] if branch == "p" else tmp[:, 0, :]
                nc.vector.scalar_tensor_tensor(out=dst, in0=g, scalar=1.0, in1=UB[u % 3][:, :], op0=ALU.add,
                                               op1=ALU.mult).then_inc(bank_read[u % 3], 1)
                dve.wait_ge(bank_read[u % 3], u // 3 + 1)
                if branch == "p":
                    return
                nc.vector.tensor_tensor(MG[:, t, cols], MG[:, t, cols], tmp[:, 0, :], ALU.add).then_inc(merged, 1)
                n_merged[0] += 1
                dve.wait_ge(merged, n_merged[0])

            n_merged = [0]

            split_after = {u: n for n, u in [(n, LAST_UNIT[n] - (2 if PIECES[n] in ("wbp", "wbm") else 1)) for n in range(10, 22)]}

            def split_next(u):
                n = split_after.get(u)
                if n is not None:
                    for H in (2 * n + 3, 2 * n + 4):
                        if H < 2 * N0:
                            hi(H)

            def unit(u):
                (add_bias if UNITS[u][1][0] == "g" else merge)(u)
                split_next(u)

            def head_max(h):
                dve.wait_ge(sc_done, h + 1)
                m = 96 + 16 * (h % 2)
                for c in range(2):
                    s = prob[:, h % 2, c * 384:(c + 1) * 384]
                    b = bank[4 + c]
                    nc.vector.tensor_tensor(s[:, 0:P], b[:, 0:P], mask[:, P:2 * P], ALU.add)
                    link(nc.vector.tensor_tensor(s[:, P:3 * P], b[:, P:3 * P], mask, ALU.add))
                    nc.vector.tensor_reduce(stat[:, m + 2 * c:m + 2 * c + 1], s[:, 0:P], AX_X, ALU.max)
                    link(nc.vector.tensor_reduce(stat[:, m + 2 * c + 1:m + 2 * c + 2], s[:, P:3 * P], AX_X, ALU.max))
                nc.vector.tensor_scalar(stat[:, m:m + 4], stat[:, m:m + 4], -HD ** -0.5, None, ALU.mult).then_inc(max_ready, 1)

            def head_weights(h):
                m = 96 + 16 * (h % 2) + 4
                dve.wait_ge(exp_done, h + 1)
                link(nc.vector.reciprocal(stat[:, m:m + 4], stat[:, m:m + 4]))
                link(nc.vector.tensor_scalar(stat[:, m + 2:m + 4], stat[:, m + 2:m + 4], nlam, None, ALU.mult))
                for t, (a, b) in enumerate(((0, P), (P, 3 * P))):
                    p0, p1 = prob[:, h % 2, a:b], prob[:, h % 2, 384 + a:384 + b]
                    link(nc.vector.tensor_scalar(p0, p0, stat[:, m + t:m + t + 1], None, ALU.mult))
                    ins = nc.vector.scalar_tensor_tensor(out=p0, in0=p1, scalar=stat[:, m + 2 + t:m + 3 + t], in1=p0,
                                                         op0=ALU.mult, op1=ALU.add)
                ins.then_inc(a_ready, 1)

            unit(20)
            head_max(0)
            head_weights(0)
            unit(21)
            for h in range(HEADS):
                if h + 1 < HEADS:
                    head_max(h + 1)
                unit(22 + 2 * h)
                if h + 1 < HEADS:
                    head_weights(h + 1)
                    unit(23 + 2 * h)
            dve.wait_ge(o_copied, HEADS)
            sq = region[2][:, 0:1024].rearrange("p (h n) -> p h n", h=HEADS)
            for t in range(NT):
                link(nc.vector.tensor_tensor(sq, O[:, t, :].rearrange("p (h n) -> p h n", h=HEADS),
                                             O[:, t, :].rearrange("p (h n) -> p h n", h=HEADS), ALU.mult))
                link(nc.vector.tensor_reduce(stat[:, 128 + 8 * t:136 + 8 * t], sq, AX_X, ALU.add))
            mean_square(2, slice(128, 144), P)
            dve.wait_ge(root_done, 3)
            for t in range(NT):
                o3 = O[:, t, :].rearrange("p (h n) -> p h n", h=HEADS)
                nc.vector.tensor_tensor(o3, o3, stat[:, 128 + 8 * t:136 + 8 * t].unsqueeze(2).to_broadcast([P, HEADS, P]),
                                        ALU.mult).then_inc(o_normed, 1)
            unit(37)
            unit(38)
            unit(39)
            for j in range(4):
                dve.wait_ge(oT_done, j + 1)
                t, h = divmod(j, 2)
                split(lambda place: nc.vector.tensor_scalar(place, bank[3 + j][:, :].rearrange("p (k n) -> p k n", k=4), sub_col,
                                                            1.0 - LAMBDA_INIT, ALU.mult, ALU.mult),
                      OT, slice(4 * h, 4 * h + 4), slice(t * P, (t + 1) * P), oT_copied)
            for u in range(40, 44):
                unit(u)
            for j in range(4):
                dve.wait_ge(mgT_copied, j + 1)
                t, h = divmod(j, 2)
                at = (slice(None), slice(4 * h, 4 * h + 4), slice(t * P, (t + 1) * P))
                nc.vector.scalar_tensor_tensor(out=MGT[1][at], in0=bank[3 + j][:, :].rearrange("p (k n) -> p k n", k=4), scalar=0.5,
                                               in1=MGT[0][at], op0=ALU.mult, op1=ALU.subtract).then_inc(mgT_split, 1)

            def add_h(u):
                _, name, t, _ = UNITS[u]
                cols = slice(int(name[2]) * HALF, (int(name[2]) + 1) * HALF)
                dve.wait_ge(unit_done, u + 1)
                nc.vector.tensor_tensor(X[:, t, cols], UB[u % 3][:, :], X[:, t, cols], ALU.add).then_inc(h_ready, 1)
                split_next(u)

            def copy_hT(n, t, h):
                dve.wait_ge(hT_done, n + 1)
                nc.vector.tensor_tensor(HNT[:, 4 * h:4 * h + 4, t * P:(t + 1) * P],
                                        bank[3 + n][:, :].rearrange("p (k n) -> p k n", k=4),
                                        gain_col[2][:, 4 * h:4 * h + 4].unsqueeze(2).to_broadcast([P, 4, P]),
                                        ALU.mult).then_inc(hT_copied, 1)

            def norm_h(t):
                dve.wait_ge(late_in, 32)
                nc.vector.scalar_tensor_tensor(
                    out=HN[:, t, :, :], in0=X[:, t, :].rearrange("p (n k) -> p k n", k=KD), scalar=stat[:, 4 + t:5 + t],
                    in1=GFF.rearrange("p (n k) -> p k n", k=KD), op0=ALU.mult, op1=ALU.mult).then_inc(hn_ready, 1)

            def route(t):
                top = stat[:, 160 + 8 * t:168 + 8 * t]
                dve.wait_ge(root_done, 4 + t)
                dve.wait_ge(logit_done, t + 1)
                link(nc.vector.scalar_tensor_tensor(out=LG[:, t, :], in0=bank[7][:, t * EXPERTS:(t + 1) * EXPERTS],
                                                    scalar=stat[:, 4 + t:5 + t], in1=b_rt, op0=ALU.mult, op1=ALU.add))
                link(nc.vector.max(top, LG[:, t, :]))
                nc.vector.tensor_scalar(stat[:, 180 + t:181 + t], top[:, 0:1], -1.0, None, ALU.mult).then_inc(top_ready, 1)
                fourth = top[:, TOP_K - 1:TOP_K]
                above, equal, run, zero = (SCR[:, 4 * t + i, :] for i in range(4))
                count = stat[:, 184 + t:185 + t]
                nc.vector.memset(zero, 0.0)
                nc.vector.tensor_scalar(above, LG[:, t, :], fourth, None, ALU.is_gt)
                link(nc.vector.tensor_scalar(equal, LG[:, t, :], fourth, None, ALU.is_equal))
                nc.vector.tensor_reduce(count, above, AX_X, ALU.add)
                link(nc.vector.tensor_tensor_scan(run, equal, zero, 0.0, ALU.add, ALU.add))
                link(nc.vector.tensor_scalar(run, run, count, float(TOP_K), ALU.add, ALU.is_le))
                link(nc.vector.tensor_tensor(equal, equal, run, ALU.mult))
                nc.vector.tensor_tensor(MASK[:, t, :], above, equal, ALU.add).then_inc(mask_ready, 1)

            def weigh(t):
                s = stat[:, 188 + t:189 + t]
                dve.wait_ge(mask_ready, t + 1)
                dve.wait_ge(lexp_done, t + 1)
                link(nc.vector.tensor_tensor(GATE[:, t, :], GATE[:, t, :], MASK[:, t, :], ALU.mult))
                link(nc.vector.tensor_reduce(s, GATE[:, t, :], AX_X, ALU.add))
                link(nc.vector.reciprocal(s, s))
                nc.vector.tensor_scalar(GATE[:, t, :], GATE[:, t, :], s, None, ALU.mult).then_inc(gate_ready, 1)

            for u in range(44, 47):
                add_h(u)
            for n, (t, h) in enumerate(((0, 0), (1, 0), (0, 1))):
                copy_hT(n, t, h)
            dve.wait_ge(squares, 5)
            mean_square(3, slice(4, 5), D)
            route(0)
            weigh(0)
            norm_h(0)
            add_h(47)
            copy_hT(3, 1, 1)
            dve.wait_ge(squares, 6)
            mean_square(4, slice(5, 6), D)
            route(1)
            weigh(1)
            norm_h(1)
            dve.wait_ge(gate_ready, 2)
            dve.wait_ge(rank_done, 1)
            link(nc.vector.scalar_tensor_tensor(out=RANK, in0=bank[3][:, 0:64].rearrange("p (t e) -> p t e", t=NT), scalar=1.0,
                                                in1=MASK, op0=ALU.add, op1=ALU.mult))
            link(nc.vector.tensor_reduce(stat[:, 190:191], bank[3][:, 64:96], AX_X, ALU.max))
            nc.vector.tensor_scalar(stat[:, 192:193], stat[:, 190:191], float(SLOTS), 1.0, ALU.is_gt, ALU.add)
            nc.vector.tensor_scalar(stat[:, 193:194], stat[:, 190:191], float(2 * SLOTS), None, ALU.is_gt)
            link(nc.vector.tensor_scalar(stat[:, 194:195], stat[:, 190:191], float(3 * SLOTS), None, ALU.is_gt))
            link(nc.vector.tensor_reduce(stat[:, 191:192], stat[:, 192:195], AX_X, ALU.add))
            nc.vector.tensor_copy(rounds[:, :], stat[:, 191:192]).then_inc(rounds_ready, 1)
            link(nc.vector.tensor_scalar(RANK, RANK, -1.0, None, ALU.add))

            def next_round_pair():
                nc.vector.tensor_scalar(RANKS[:, :, EXPERTS:EXPERTS + 2], RANK[:, :, 0:2], -float(SLOTS), None,
                                        ALU.add).then_inc(rank_ready, 1)

            def build_slots(first):
                for dst, weighted in ((PT, False), (PW, True)):
                    for t in range(NT):
                        for e in range(2):
                            cols = slice(e * SLOTS, (e + 1) * SLOTS)
                            rank = RANKS[:, t, bass.ds(first + e, 1)]
                            if weighted:
                                nc.vector.tensor_scalar(PW[:, t, cols], iota[:, cols], rank, GATES[:, t, bass.ds(first + e, 1)],
                                                        ALU.is_equal, ALU.mult).then_inc(slots_built, 1)
                            else:
                                nc.vector.tensor_scalar(PT[:, t, cols], iota[:, cols], rank, None,
                                                        ALU.is_equal).then_inc(slots_built, 1)

            next_round_pair()
            nc.vector.tensor_copy(GATES[:, :, EXPERTS:EXPERTS + 2], GATE[:, :, 0:2]).then_inc(rank_ready, 1)
            dve.wait_ge(rank_ready, 2)
            build_slots(0)
            for c in (200, 203):
                nc.vector.memset(stat[:, c:c + 1], 0.0).then_inc(y_added, 1)
                nc.vector.memset(stat[:, c + 1:c + 2], 0.0).then_inc(o_hi, 1)
                nc.vector.memset(stat[:, c + 2:c + 3], 0.0).then_inc(o_lo, 1)
            dve.wait_ge(rounds_ready, 1)
            n_rounds = dve.value_load(rounds[0:1, 0:1], min_val=1, max_val=SEQ // SLOTS)

            def add_results(count):
                for j in range(4):
                    t, h = divmod(j, 2)
                    dve.wait_ge(comb_done, count + (j + 1))
                    nc.vector.tensor_tensor(X[:, t, h * HALF:(h + 1) * HALF], bank[6 + j % 2][:, :],
                                            X[:, t, h * HALF:(h + 1) * HALF], ALU.add).then_inc(y_added, 1)

            with dve.Fori(0, n_rounds) as r:
                with dve.Fori(0, PAIRS) as i:
                    it = r * PAIRS + i
                    dve.wait_ge(disp_done, it * 2 + 2)
                    nc.vector.tensor_copy(XE[:, 4:8, :], bank[5][:, :].rearrange("p (k n) -> p k n", k=4)).then_inc(xe_hi, 1)
                    add_results(it * 4)
                    dve.wait_ge(slots_free, it + 1)
                    build_slots(i * 2 + 2)
                    for e in range(2):
                        dve.wait_ge(used, it * PER_PAIR + (4 * e + 2))
                        nc.vector.tensor_scalar(GS, bank[0][:, :], LIMIT, None, ALU.min).then_inc(g_read, 1)
                        dve.wait_ge(sig_done, it * 2 + (e + 1))
                        dve.wait_ge(g_read, it * 2 + (e + 1))
                        nc.vector.tensor_tensor(SG, SG, GS, ALU.mult).then_inc(gs_done, 1)
                        dve.wait_ge(used, it * PER_PAIR + (4 * e + 4))
                        if e:
                            dve.wait_ge(act_ready, it * 2 + 1)
                        nc.vector.tensor_scalar(US, bank[1][:, :], LIMIT, -LIMIT, ALU.min, ALU.max).then_inc(u_read, 1)
                        dve.wait_ge(u_read, it * 2 + (e + 1))
                        dve.wait_ge(gs_done, it * 2 + (e + 1))
                        nc.vector.scalar_tensor_tensor(out=AH[:, e, :], in0=US, scalar=1.0, in1=SG, op0=ALU.add,
                                                       op1=ALU.mult).then_inc(act_ready, 1)
                    for e in range(2):
                        dve.wait_ge(used, it * PER_PAIR + (10 + 2 * e))
                        nc.vector.tensor_copy(OE[e * SLOTS:(e + 1) * SLOTS, HALF:D], bank[2][SLOTS:2 * SLOTS, :]).then_inc(o_hi, 1)
                dve.wait_ge(slots_built, (r + 1) * (8 * PAIRS) + 8)
                nc.vector.tensor_scalar(RANK, RANK, -float(SLOTS), None, ALU.add).then_inc(rank_ready, 1)
                dve.wait_ge(rank_ready, r * 2 + 3)
                next_round_pair()
                dve.wait_ge(rank_ready, r * 2 + 4)
            add_results(n_rounds * (4 * PAIRS))

        @block.tensor
        def _(pe):
            def turn4(dst, srcs, signal):
                for b in range(4):
                    ins = nc.tensor.transpose(dst[:, b * P:(b + 1) * P], srcs[b], ident)
                ins.then_inc(signal, 1)

            stationary = {}
            for name in PIECES:
                stationary[name] = {"mk": MEMT, "mv": MEMT, "wbp": Z2T, "wbm": OMT, "wba0": OT, "wba1": OT,
                                    "wo0": MGT, "wo1": MGT}.get(name, XNT)

            def unit(u):
                unit_k(u, 0, 4 if UNITS[u][1] in ("wbp", "wbm") else KD)

            def unit_k(u, first, after):
                n, name, t, c = UNITS[u]
                k_n = 4 if name in ("wbp", "wbm") else KD
                if u - 3 >= UNIT_OF[("wo0", 0, 0)]:
                    pe.wait_ge(h_ready, u - 3 - UNIT_OF[("wo0", 0, 0)] + 1)
                elif u >= 3:
                    pe.wait_ge(bank_read[u % 3], u // 3)
                short = name in ("wbp", "wbm")
                high, low = stationary[name][0:2]
                for k in range(first, after):
                    H = 2 * n + (c if short else k // 4)
                    if k % 4 == 0:
                        if H < EARLY:
                            pe.wait_ge(lo_early, H + 1)
                        else:
                            pe.wait_ge(lo_ready, H - EARLY + 1)
                    cols = slice((k % 4) * HALF, (k % 4 + 1) * HALF)
                    toks = slice(t * P, (t + 1) * P)
                    for m, (a, b) in enumerate(((high, upper(H)), (high, lower(H)), (low, upper(H)))):
                        ins = nc.tensor.matmul(UB[u % 3][:, :], a[:, k, toks], b[:, cols],
                                               start=(k == 0 and m == 0), stop=(k == k_n - 1 and m == 2))
                    if k == 3 and t == NT - 1 and not short:
                        ins.then_inc(first_half_used, 1)
                if after == k_n:
                    ins.then_inc(unit_done, 1)

            pe.wait_ge(ident_in, 16)
            pe.wait_ge(x_in, 16 * NT)
            for j in range(4):
                t, h = divmod(j, 2)
                turn4(bank[3 + j], [X[:, t, (4 * h + b) * P:(4 * h + b + 1) * P] for b in range(4)], xT_done)
            pe.wait_ge(xT_copied, 2)
            unit(0)
            pe.wait_ge(xT_copied, 4)
            unit(1)
            pe.wait_ge(mem_in, 16)
            for j in range(4):
                t, h = divmod(j, 2)
                turn4(bank[3 + j], [MEM[:, t, (4 * h + b) * P:(4 * h + b + 1) * P] for b in range(4)], mT_done)
            pe.wait_ge(mT_copied, 4)
            for u in range(2, 8):
                unit(u)
            pe.wait_ge(band_in, 32)
            for j in range(2):
                for g in (2 * j, 2 * j + 1):
                    for t in range(NT):
                        ins = nc.tensor.matmul(bank[4 + j][:, (g % 2) * SEQ:(g % 2 + 1) * SEQ], U[:, t, g * P:(g + 1) * P],
                                               BAND[:, t, g, :], start=(t == 0), stop=(t == NT - 1))
                ins.then_inc(z_done, 1)
            unit(8)
            unit(9)
            for j in range(2):
                pe.wait_ge(zT_copied, 2)
                for g in (2 * j, 2 * j + 1):
                    ins = nc.tensor.matmul(bank[4 + j][:, (g % 2) * SEQ:(g % 2 + 1) * SEQ], POOLW[:, g, :], ZT[:, g, :],
                                           start=True, stop=True)
                ins.then_inc(z2_done, 1)
            unit(10)
            unit(11)
            for j, (rows_, t) in enumerate(((KM, 0), (KM, 1), (QM, 0), (QM, 1))):
                pe.wait_ge(mem_normed, j // 2 + 1)
                pe.wait_ge(z2T_copied, 2)
                turn4(bank[(3, 6, 4, 5)[j]], [rows_[:, t, h * P:(h + 1) * P] for h in range(MHEADS)], kq_done)
            unit(12)
            unit(13)

            def mem_scores(h):
                if h == 0:
                    pe.wait_ge(kqT_copied, 4)
                if h >= 2:
                    pe.wait_ge(mexp_done, h - 1)
                for t in range(NT):
                    ins = nc.tensor.matmul(bank[4 + h % 2][:, t * SEQ:(t + 1) * SEQ], QMT[:, h, t * P:(t + 1) * P], KMT[:, h, :],
                                           start=True, stop=True)
                ins.then_inc(ms_done, 1)

            def mem_turn(h):
                if h >= 1:
                    pe.wait_ge(pt_copied, h)
                pe.wait_ge(mp_ready, h + 1)
                turn4(bank[6], [prob[:, h % 2, t * SEQ + m * P:t * SEQ + (m + 1) * P] for m in range(2) for t in range(NT)], mt_done)

            def mem_values(h):
                if h >= 1:
                    pe.wait_ge(omT_copied, h)
                pe.wait_ge(pt_copied, h + 1)
                for m in range(2):
                    ins = nc.tensor.matmul(bank[7][:, 0:SEQ], VM[:, m, h * P:(h + 1) * P], probT[:, h % 2, m * SEQ:(m + 1) * SEQ],
                                           start=(m == 0), stop=(m == 1))
                ins.then_inc(mo_done, 1)

            mem_scores(0)
            unit(14)
            mem_scores(1)
            mem_turn(0)
            unit(15)
            mem_values(0)
            mem_scores(2)
            mem_turn(1)
            unit(16)
            mem_values(1)
            mem_scores(3)
            mem_turn(2)
            unit(17)
            mem_values(2)
            mem_turn(3)
            unit(18)
            mem_values(3)
            unit(19)

            def turn_qk(h):
                if h == 0:
                    pe.wait_ge(normed, 8)
                else:
                    pe.wait_ge(qkT_copied, h)
                turn4(bank[3], [r[:, t, h * P:(h + 1) * P] for r in (Q, K) for t in range(NT)], qk_done)

            def scores(h):
                pe.wait_ge(qkT_copied, h + 1)
                if h >= 1:
                    pe.wait_ge(max_ready, h)
                else:
                    pe.wait_ge(mexp_done, MHEADS)
                for c in range(2):
                    part = qkt[c * HD:(c + 1) * HD, h % 2, :]
                    nc.tensor.matmul(bank[4 + c][:, 0:P], part[:, 0:P], part[:, SEQ:SEQ + P], start=True, stop=True)
                    ins = nc.tensor.matmul(bank[4 + c][:, P:3 * P], part[:, P:SEQ], part[:, SEQ:2 * SEQ], start=True, stop=True)
                ins.then_inc(sc_done, 1)

            def turn_a(h):
                pe.wait_ge(a_ready, h + 1)
                if h >= 1:
                    pe.wait_ge(at_copied, h)
                else:
                    pe.wait_ge(pt_copied, MHEADS)
                for b in range(3):
                    ins = nc.tensor.transpose(bank[6][:, b * P:(b + 1) * P], prob[:, h % 2, b * P:(b + 1) * P], ident)
                ins.then_inc(at_done, 1)

            def values(h):
                pe.wait_ge(at_copied, h + 1)
                if h >= 1:
                    pe.wait_ge(o_copied, h)
                else:
                    pe.wait_ge(omT_copied, MHEADS)
                cols = slice(h * P, (h + 1) * P)
                nc.tensor.matmul(bank[7][:, 0:P], probT[:, h % 2, 0:P], V[:, 0, cols], start=True, stop=True)
                nc.tensor.matmul(bank[7][:, P:2 * P], probT[:, h % 2, P:2 * P], V[:, 0, cols], start=True, stop=False)
                nc.tensor.matmul(bank[7][:, P:2 * P], probT[:, h % 2, 2 * P:3 * P], V[:, 1, cols], start=False,
                                 stop=True).then_inc(pv_done, 1)

            turn_qk(0)
            unit(20)
            scores(0)
            turn_qk(1)
            unit(21)
            pe.wait_ge(bank_read[19 % 3], 19 // 3 + 1)
            for h in range(HEADS):
                if h == 1:
                    pe.wait_ge(z2T_copied, 2)
                if h + 1 < HEADS:
                    scores(h + 1)
                if h == 0:
                    pe.wait_ge(omT_copied, MHEADS)
                unit(22 + 2 * h)
                turn_a(h)
                if h + 2 < HEADS:
                    turn_qk(h + 2)
                if h == HEADS - 1:
                    values(h)
                unit(23 + 2 * h)
                if h < HEADS - 1:
                    values(h)
            unit(38)
            unit(39)
            for j in range(4):
                t, h = divmod(j, 2)
                pe.wait_ge(o_normed, t + 1)
                turn4(bank[3 + j], [O[:, t, (4 * h + b) * P:(4 * h + b + 1) * P] for b in range(4)], oT_done)
            pe.wait_ge(oT_copied, 4)
            for u in range(40, 44):
                unit(u)
            pe.wait_ge(merged, 8)
            for j in range(4):
                t, h = divmod(j, 2)
                turn4(bank[3 + j], [MG[:, t, (4 * h + b) * P:(4 * h + b + 1) * P] for b in range(4)], mgT_done)
            pe.wait_ge(mgT_split, 4)
            for u in range(44, 47):
                unit(u)

            def turn_h(n, t, h):
                turn4(bank[3 + n], [X[:, t, (4 * h + b) * P:(4 * h + b + 1) * P] for b in range(4)], hT_done)

            def logits(t):
                for k in range(KD):
                    ins = nc.tensor.matmul(bank[7][:, t * EXPERTS:(t + 1) * EXPERTS], HNT[:, k, t * P:(t + 1) * P], WR[:, k, :],
                                           start=(k == 0), stop=(k == KD - 1))
                ins.then_inc(logit_done, 1)

            for n, (t, h) in enumerate(((0, 0), (1, 0), (0, 1))):
                pe.wait_ge(h_ready, n + 1)
                turn_h(n, t, h)
            unit_k(47, 0, 2)
            pe.wait_ge(hT_copied, 3)
            pe.wait_ge(late_in, 32)
            logits(0)
            unit_k(47, 2, KD)
            pe.wait_ge(h_ready, 4)
            turn_h(3, 1, 1)
            pe.wait_ge(hT_copied, 4)
            logits(1)
            pe.wait_ge(mask_ready, 2)
            for cols, parts in ((slice(0, 32), ((tri, 0),)), (slice(32, 64), ((ones, 0), (tri, 1))), (slice(64, 96), ((ones, 0), (ones, 1)))):
                for n, (m, t) in enumerate(parts):
                    ins = nc.tensor.matmul(bank[3][:, cols], m, MASK[:, t, :], start=(n == 0), stop=(n == len(parts) - 1))
            ins.then_inc(rank_done, 1)
            pe.wait_ge(gate_ready, 2)
            for t in range(NT):
                ins = nc.tensor.transpose(bank[6][0:EXPERTS, t * P:(t + 1) * P], GATE[:, t, :], ident)
            ins.then_inc(gT_done, 1)
            pe.wait_ge(seed_in, 16)
            pe.wait_ge(rounds_ready, 1)
            n_rounds = pe.value_load(rounds[0:1, 0:1], min_val=1, max_val=SEQ // SLOTS)

            def combine(it):
                pe.wait_ge(o_lo, it * 2 + 2)
                pe.wait_ge(o_hi, it * 2 + 2)
                pe.wait_ge(wT_copied, it + 1)
                for j in range(4):
                    t, h = divmod(j, 2)
                    pe.wait_ge(y_added, it * 4 + (j + 1))
                    nc.tensor.matmul(bank[6 + j % 2][:, :], PWT[:, t * P:(t + 1) * P], OE[:, h * HALF:(h + 1) * HALF],
                                     start=True, stop=True).then_inc(comb_done, 1)

            def project(it, e, m, first, dst):
                row = 2 * m + e
                for j in (first, first + 1):
                    s = moe_slot(j)
                    pe.wait_ge(ring_in[s], moe_landed(it, j))
                    w = ring[:, s, :].rearrange("p (k n) -> p k n", k=4)
                    for k in range(4):
                        kk = 4 * (j - first) + k
                        for h in range(2):
                            ins = nc.tensor.matmul(dst[h * SLOTS:(h + 1) * SLOTS, :], XE[:, kk, e * SLOTS:(e + 1) * SLOTS],
                                                   w[:, k, h * HALF:(h + 1) * HALF], start=(kk == 0), stop=False)
                    if j == first:
                        ins.then_inc(used, 1)
                for h in range(2):
                    ins = nc.tensor.matmul(dst[h * SLOTS:(h + 1) * SLOTS, :], sel[:, row, :],
                                           B4[:, h * HALF:(h + 1) * HALF], start=False, stop=True)
                ins.then_inc(used, 1)

            with pe.Fori(0, n_rounds) as r:
                with pe.Fori(0, PAIRS) as i:
                    it = r * PAIRS + i
                    pe.wait_ge(slots_built, it * 8 + 4)
                    for half in range(2):
                        for b in range(4):
                            for t in range(NT):
                                ins = nc.tensor.matmul(bank[4 + half][:, b * P:(b + 1) * P], HN[:, t, 4 * half + b, :], PT[:, t, :],
                                                       start=(t == 0), stop=(t == NT - 1))
                        ins.then_inc(disp_done, 1)
                    combine(it)
                    pe.wait_ge(slots_built, it * 8 + 8)
                    for t in range(NT):
                        ins = nc.tensor.transpose(bank[3][:, t * P:(t + 1) * P], PW[:, t, :], ident)
                    ins.then_inc(slots_free, 1)
                    pe.wait_ge(xe_lo, it + 1)
                    pe.wait_ge(xe_hi, it + 1)
                    pe.wait_ge(bias_in, it * 32 + 32)
                    project(it, 0, 0, 0, bank[0])
                    project(it, 0, 1, 2, bank[1])
                    pe.wait_ge(g_read, it * 2 + 1)
                    project(it, 1, 0, 4, bank[0])
                    pe.wait_ge(u_read, it * 2 + 1)
                    project(it, 1, 1, 6, bank[1])
                    for e in range(2):
                        pe.wait_ge(act_ready, it * 2 + (e + 1))
                        if e == 0:
                            pe.wait_ge(wT_copied, it + 2)
                        turn4(bank[3], [AH[:, e, j * P:(j + 1) * P] for j in range(4)], actT_done)
                        if e == 1:
                            pe.wait_ge(o_lo, it * 2 + 3)
                            pe.wait_ge(o_hi, it * 2 + 3)
                        pe.wait_ge(actT_copied, it * 2 + (e + 1))
                        for j in (8 + 2 * e, 9 + 2 * e):
                            s = moe_slot(j)
                            pe.wait_ge(ring_in[s], moe_landed(it, j))
                            w = ring[:, s, :].rearrange("p (k n) -> p k n", k=4)
                            half = j % 2
                            for k in range(4):
                                for h in range(2):
                                    ins = nc.tensor.matmul(bank[2][h * SLOTS:(h + 1) * SLOTS, :],
                                                           AHT[:, k, half * SLOTS:(half + 1) * SLOTS],
                                                           w[:, k, h * HALF:(h + 1) * HALF], start=(half == 0 and k == 0),
                                                           stop=(half == 1 and k == 3))
                            ins.then_inc(used, 1)
            combine(n_rounds * PAIRS)


_INS = ["x", "mem", "g_mix", "w_in", "b_gates", "q_norm", "k_norm", "lambda_q1", "lambda_k1", "lambda_q2", "lambda_k2",
        "g_subln", "pool_w", "pool_scale", "g_mem", "w_mem_kv", "mq_norm", "mk_norm", "w_b_attn", "w_b_pool", "w_b_mem",
        "w_out", "g_ffn", "w_router", "b_router", "w_gate", "b_gate", "w_up", "b_up", "w_down", "b_down"]


def kernel(**inputs):
    import concourse.bacc as bacc
    from concourse.bass_utils import run_bass_kernel_spmd

    nc = bacc.Bacc("TRN2", target_bir_lowering=False, num_devices=1)
    table, band = constants()
    arrays, args = {}, []
    for name in _INS + ["table", "band"]:
        a = {"table": table, "band": band}.get(name)
        a = np.ascontiguousarray(inputs[name]) if a is None else a
        arrays[f"in_{name}"] = a
        args.append(nc.dram_tensor(f"in_{name}", a.shape, mybir.dt.from_np(a.dtype), kind="ExternalInput").ap())
    args.append(nc.dram_tensor("out_0", (1, SEQ, D), F32, kind="ExternalOutput").ap())
    decoder_layer(nc, *args)
    r = run_bass_kernel_spmd(nc, [arrays], core_ids=[0])
    return r.results[0]["out_0"]
```

```python
from contextlib import ExitStack

import numpy as np

import concourse.bass as bass
from concourse import mybir

F32 = mybir.dt.float32
F32R = mybir.dt.float32r
I32 = mybir.dt.int32
ALU = mybir.AluOpType
ACT = mybir.ActivationFunctionType
AX_X = mybir.AxisListType.X

P = 128
SEQ, D = 256, 1024
NT = SEQ // P
KD = D // P
HALF = 512
HEADS, HD = 8, 64
MHEADS, MHD = 4, 128
GROUPS = 4
WINDOWS = (2, 4, 8, 16)
EXPERTS, TOP_K = 32, 4
SLOTS = 64
PAIRS = EXPERTS // 2
EPS = 1e-6
LAMBDA_INIT = 0.2
LIMIT, ALPHA = 7.0, 1.702
NEG = -1e30

PIECES = ["pool", "mk", "mv", "qm", "q0", "q1", "k0", "k1", "v0", "v1", "gp0", "gp1", "wbp",
          "gm0", "gm1", "wbm", "ga0", "ga1", "wba0", "wba1", "wo0", "wo1"]
RING = 9
PER_PAIR = 12
PER_TURN = 2 * PER_PAIR
MIX_SLOTS = 6
MOE_SLOT = (8, 5, 4, 6, 0, 2, 1, 3, 7)
HALVES = 5
HI_SLOT = (0, 1, 2, 3, 9)
RAW_SLOT = (4, 5, 6, 7, 8)
XLO_SLOT, LO_SLOT = 10, 11
BY_ACT = 23
EARLY = 2
UNITS = []
LAST_UNIT = []
for _n, _name in enumerate(PIECES):
    _cuts = 2 if _name in ("wbp", "wbm") else 1
    for _c in range(_cuts):
        for _t in range(NT):
            UNITS.append((_n, _name, _t, _c))
    LAST_UNIT.append(len(UNITS) - 1)
N_FULL = [sum(_m not in ("wbp", "wbm") for _m in PIECES[:_n + 1]) for _n in range(len(PIECES))]
UNIT_OF = {(name, t, c): u for u, (n, name, t, c) in enumerate(UNITS)}

C_ID, C_TRI, C_MASK, C_IOTA, C_COS, C_SIN, C_NSIN, C_SEL, C_ONE = 0, 128, 256, 512, 640, 704, 768, 832, 1088
C_ALL = 1216


def constants():
    c = np.zeros((P, C_ALL), np.float32)
    i = np.arange(P)
    c[:, C_ID:C_ID + P] = np.eye(P)
    c[:, C_TRI:C_TRI + P] = i[:, None] < i[None, :]
    c[:, C_MASK + P:C_MASK + 2 * P] = np.where(i[None, :] <= i[:, None], 0.0, NEG)
    c[:, C_IOTA:C_IOTA + P] = np.tile(np.arange(SLOTS), 2)[None, :]
    inv = np.float32(10000.0) ** (-np.arange(0, HD, 2, dtype=np.float32) / np.float32(HD))
    ang = (np.arange(SEQ, dtype=np.float32)[:, None] * inv[None, :].astype(np.float32)).astype(np.float32)
    for base, table in ((C_COS, np.cos(ang)), (C_SIN, np.sin(ang)), (C_NSIN, -np.sin(ang))):
        c[:, base:base + NT * HD // 2] = table.reshape(NT, P, HD // 2).transpose(1, 0, 2).reshape(P, -1)
    sel = (np.arange(4)[:, None, None] == np.arange(4)[None, :, None]) * np.ones((1, 1, SLOTS))
    c[0:4, C_SEL:C_SEL + 4 * SLOTS] = sel.reshape(4, -1)
    c[:, C_ONE:C_ONE + P] = 1.0
    band = np.zeros((SEQ, GROUPS, SEQ), np.float32)
    for g, w in enumerate(WINDOWS):
        for t in range(SEQ):
            band[max(0, t - w + 1):t + 1, g, t] = 1.0 / min(t + 1, w)
            band[t, g, t] -= 1.0
    return c, band


def decoder_layer(nc, x, mem, g_mix, w_in, b_gates, q_norm, k_norm, lambda_q1, lambda_k1, lambda_q2,
                  lambda_k2, g_subln, pool_w, pool_scale, g_mem, w_mem_kv, mq_norm, mk_norm, w_b_attn,
                  w_b_pool, w_b_mem, w_out, g_ffn, w_router, b_router, w_gate, b_gate, w_up, b_up,
                  w_down, b_down, table, band, out):
    with ExitStack() as ctx:
        def sb(name, shape, dt=F32):
            return ctx.enter_context(nc.sbuf_tensor(name, shape, dt))

        def sem(name):
            return ctx.enter_context(nc.semaphore(name))

        order = (8, 9, 10, 2, 0, 1, 3, 4, 5, 6, 7)
        with nc.sbuf_tensor("experts_ring", [P, RING, 4096], F32) as moe_ring:
            pass
        with ExitStack() as first_names:
            ring = first_names.enter_context(nc.sbuf_tensor("ring", [P, MIX_SLOTS, 4096], F32))
            region = {i: first_names.enter_context(nc.sbuf_tensor(f"region{i}", [P, 2048], F32)) for i in order[:4]}
            first_names.enter_context(nc.sbuf_tensor("attention_buffers", [P, 4096], F32))
            region.update({i: first_names.enter_context(nc.sbuf_tensor(f"region{i}", [P, 2048], F32)) for i in order[4:]})
        ring_r = sb("ring_split", [P, MIX_SLOTS, 4096], F32R)
        region_r = {i: sb(f"region{i}_split", [P, 2048], F32R) for i in order[:4]}
        prob = sb("prob", [P, 2, 768])
        probT = sb("probT", [P, 2, HALF])
        tmp = sb("tmp", [P, 2, HALF])
        rot = sb("rot", [P, 2, 2, NT, HD])
        region_r.update({i: sb(f"region{i}_split", [P, 2048], F32R) for i in order[4:]})
        half_slot = ring[:, :, :].rearrange("p s (h n) -> p (s h) n", h=2)
        half_slot_r = ring_r[:, :, :].rearrange("p s (h n) -> p (s h) n", h=2)
        con = sb("con", [P, C_ALL])
        small = sb("small", [P, 68])
        stat = sb("stat", [P, 208])
        gqk = sb("gqk", [P, 2, HD])
        qkt = region[9][:, 0:1024].rearrange("p (b n) -> p b n", b=2)
        rounds = sb("rounds", [P, 1], I32)

        ident = con[:, C_ID:C_ID + P]
        tri = con[:, C_TRI:C_TRI + P]
        ones = con[:, C_ONE:C_ONE + P]
        mask = con[:, C_MASK:C_MASK + 2 * P]
        iota = con[:, C_IOTA:C_IOTA + P]
        sel = con[0:4, C_SEL:C_SEL + 4 * SLOTS].rearrange("r (a s) -> r a s", a=4)

        minus_half = small[:, 3:4]
        mq_col, mk_col, sub_col = small[:, 0:1], small[:, 1:2], small[:, 2:3]
        psc_col = small[:, 4:8]
        nlam = small[:, 8:9]
        sub_gain = small[:, 11:12]
        lam_e = small[:, 9:11]
        gain_col = [small[:, 12 + 8 * i:20 + 8 * i] for i in range(3)]
        b_rt = small[:, 36:68]

        def rows_r(i, k=KD):
            return region_r[i][:, :].rearrange("p (k n) -> p k n", k=k)

        def lo_pair(slot):
            return [x[:, slot, :].rearrange("p (k n) -> p k n", k=KD) for x in (half_slot, half_slot_r)]

        def rows(i, inner):
            return region[i][:, :].rearrange("p (t n) -> p t n", t=NT) if inner == "t" else \
                region[i][:, :].rearrange("p (k n) -> p k n", k=KD)

        X = rows(0, "t")
        XLO, XLO_R = lo_pair(XLO_SLOT)
        LO, LO_R = lo_pair(LO_SLOT)
        XNT = (rows_r(1), XLO_R, XLO)
        Q = rows(2, "t")
        MEM = rows(3, "t")
        K = rows(3, "t")
        MEMT = (rows_r(4), LO_R, LO)
        V = rows(4, "t")
        BAND = region[5][:, :].rearrange("p (t g n) -> p t g n", t=NT, g=GROUPS)
        O = rows(5, "t")
        U = region[6][:, 0:1024].rearrange("p (t n) -> p t n", t=NT)
        QM = region[6][:, 1024:2048].rearrange("p (t n) -> p t n", t=NT)
        KM = region[7][:, 0:1024].rearrange("p (t n) -> p t n", t=NT)
        VM = region[7][:, 1024:2048].rearrange("p (t n) -> p t n", t=NT)
        G = {"p": rows(6, "t"), "m": rows(7, "t"), "a": rows(6, "t")}
        MG = rows(8, "t")
        ZT = region[8][:, 0:1024].rearrange("p (g n) -> p g n", g=GROUPS)
        KMT = region[9][:, 0:1024].rearrange("p (h n) -> p h n", h=MHEADS)
        QMT = region[9][:, 1024:2048].rearrange("p (h n) -> p h n", h=MHEADS)
        OT = (rows_r(9), rows_r(2), rows(2, "k"))
        OMT = (rows_r(10)[:, 0:4, :], LO_R[:, 4:8, :], LO[:, 4:8, :])
        Z2T = (rows_r(10)[:, 4:8, :], LO_R[:, 0:4, :], LO[:, 0:4, :])
        MGT = (rows_r(10), rows_r(5), None)
        POOLW = region[10][:, 0:512].rearrange("p (g n) -> p g n", g=GROUPS)
        JUNK = region[8][:, 1024:2048]
        SQ = JUNK.rearrange("p (b n) -> p b n", b=2)

        HN = region[1][:, :].rearrange("p (t k n) -> p t k n", t=NT, k=KD)
        HNT = rows(2, "k")
        H_JUNK = region[6][:, 0:1024]
        LATE_TMP = region[7][:, 0:512]
        GFF = region[3][:, 0:1024]
        WR = region[3][:, 1024:1280].rearrange("p (k e) -> p k e", k=KD)
        LG = region[3][:, 1280:1344].rearrange("p (t e) -> p t e", t=NT)
        RG = region[3][:, 1792:1928].rearrange("p (a t e) -> p a t e", a=2, t=NT)
        RANKS, GATES = RG[:, 0], RG[:, 1]
        RANK, GATE = RANKS[:, :, 0:EXPERTS], GATES[:, :, 0:EXPERTS]
        MASK = region[3][:, 1408:1472].rearrange("p (t e) -> p t e", t=NT)
        SCR = region[3][:, 1536:1792].rearrange("p (a e) -> p a e", e=EXPERTS)
        XE = region[4][:, 0:1024].rearrange("p (k s) -> p k s", k=KD)
        OE = region[4][:, 1024:2048]
        GS, SG, US = region[5][:, 0:512], region[5][:, 512:1024], region[5][:, 1024:1536]
        AH = region[6][:, 0:1024].rearrange("p (e n) -> p e n", e=2)
        AHT = region[6][:, 1024:1536].rearrange("p (j s) -> p j s", j=4)
        PT = region[7][:, 0:256].rearrange("p (t s) -> p t s", t=NT)
        PW = region[7][:, 256:512].rearrange("p (t s) -> p t s", t=NT)
        PWT = region[7][:, 512:768]
        B4 = [region[7][0:4, 1024:2048], region[3][0:4, 0:1024]]

        bank = [ctx.enter_context(nc.psum_tensor(f"bank{i}", [P, HALF], F32)) for i in range(8)]
        UB = bank[0:3]

        ident_in, x_in, mem_in, con_in, gain_in, mem_gain_in, vec_in, band_in, late_in = (sem(n) for n in (
            "ident_in", "x_in", "mem_in", "con_in", "gain_in", "mem_gain_in", "vec_in", "band_in", "late_in"))
        raw_in = [sem(f"raw_in{i}") for i in range(HALVES)]
        hi_early, hi_act, hi_dve, lo_ready, lo_early, first_half_used = (sem(n) for n in ("hi_early", "hi_act", "hi_dve", "lo_ready", "lo_early", "first_half_used"))
        oT_split, mgT_split = sem("oT_split"), sem("mgT_split")
        ring_in = [sem(f"ring_in{i}") for i in range(RING)]
        gbias_in = [sem(f"gbias_in{i}") for i in range(3)]
        squares = sem("squares")
        exponent_ready, ms_ready, root_done = sem("exponent_ready"), sem("ms_ready"), sem("root_done")
        gms_ready, groot_done, sq_done = sem("gms_ready"), sem("groot_done"), sem("sq_done")
        xT_done, xT_copied = sem("xT_done"), sem("xT_copied")
        mT_done, mT_copied = sem("mT_done"), sem("mT_copied")
        unit_done = sem("unit_done")
        bank_read = [sem(f"bank_read{i}") for i in range(3)]
        z_done, zT_copied, z2_done, z2T_copied = (sem(n) for n in ("z_done", "zT_copied", "z2_done", "z2T_copied"))
        mem_normed, kq_done, kqT_copied = sem("mem_normed"), sem("kq_done"), sem("kqT_copied")
        ms_done, mmax_ready, mexp_done, mp_ready = (sem(n) for n in ("ms_done", "mmax_ready", "mexp_done", "mp_ready"))
        mt_done, pt_copied, mo_done, omT_copied = (sem(n) for n in ("mt_done", "pt_copied", "mo_done", "omT_copied"))
        rot_ready, normed = sem("rot_ready"), sem("normed")
        lam_sum, lam_exp = sem("lam_sum"), sem("lam_exp")
        qk_done, qkT_copied, sc_done, max_ready = (sem(n) for n in ("qk_done", "qkT_copied", "sc_done", "max_ready"))
        exp_done, a_ready, at_done, at_copied = (sem(n) for n in ("exp_done", "a_ready", "at_done", "at_copied"))
        pv_done, o_copied = sem("pv_done"), sem("o_copied")
        gexp_done, o_normed, oT_done, oT_copied = (sem(n) for n in ("gexp_done", "o_normed", "oT_done", "oT_copied"))
        merged, mgT_done, mgT_copied = sem("merged"), sem("mgT_done"), sem("mgT_copied")
        h_ready, hn_ready, hT_done, hT_copied = (sem(n) for n in ("h_ready", "hn_ready", "hT_done", "hT_copied"))
        logit_done, top_ready, lexp_done, mask_ready = (sem(n) for n in ("logit_done", "top_ready", "lexp_done", "mask_ready"))
        rank_done, gate_ready, gT_done, rounds_ready = (sem(n) for n in ("rank_done", "gate_ready", "gT_done", "rounds_ready"))
        seed_clear, seed_in = sem("seed_clear"), sem("seed_in")
        dve_step = sem("dve_step")
        slots_free, slots_built = sem("slots_free"), sem("slots_built")
        disp_done, xe_lo, xe_hi = sem("disp_done"), sem("xe_lo"), sem("xe_hi")
        comb_done, y_added, rank_ready, wT_copied = (sem(n) for n in ("comb_done", "y_added", "rank_ready", "wT_copied"))
        bias_in, used = sem("bias_in"), sem("used")
        g_read, sig_done, gs_done, u_read = (sem(n) for n in ("g_read", "sig_done", "gs_done", "u_read"))
        act_ready, actT_done, actT_copied = sem("act_ready"), sem("actT_done"), sem("actT_copied")
        o_lo, o_hi, out_done = sem("o_lo"), sem("o_hi"), sem("out_done")

        win = w_in.rearrange("(k p) n -> p k n", p=P)
        wkv = w_mem_kv.rearrange("(k p) n -> p k n", p=P)
        wba = w_b_attn.rearrange("(k p) n -> p k n", p=P)
        wo = w_out.rearrange("(k p) n -> p k n", p=P)
        src = {"pool": win[:, :, 3072:3584], "mk": wkv[:, :, 0:512], "mv": wkv[:, :, 512:1024],
               "qm": win[:, :, 3584:4096], "wbp": w_b_pool.rearrange("(k p) n -> p k n", p=P),
               "wbm": w_b_mem.rearrange("(k p) n -> p k n", p=P)}
        for h in range(2):
            for name, base in (("q", 0), ("k", 1024), ("v", 2048), ("ga", 4096), ("gp", 5120), ("gm", 6144)):
                src[f"{name}{h}"] = win[:, :, base + h * 512:base + h * 512 + 512]
            src[f"wba{h}"] = wba[:, :, h * 512:h * 512 + 512]
            src[f"wo{h}"] = wo[:, :, h * 512:h * 512 + 512]

        def half_source(H):
            n, h = divmod(H, 2)
            w = src[PIECES[n]]
            return w[:, :, h * HALF:(h + 1) * HALF] if PIECES[n] in ("wbp", "wbm") else w[:, 4 * h:4 * h + 4, :]

        def raw(H):
            return half_slot[:, RAW_SLOT[H % HALVES], :]

        def lower(H):
            return half_slot_r[:, RAW_SLOT[H % HALVES], :]

        def upper(H):
            return half_slot_r[:, HI_SLOT[H % HALVES], :]

        def upper_made(engine, H):
            if H < BY_ACT:
                engine.wait_ge(hi_act, H - EARLY + 1)
            else:
                engine.wait_ge(hi_dve, H - BY_ACT + 1)

        def half_free(engine, H):
            n, h = divmod(H, 2)
            if h == 1:
                engine.wait_ge(unit_done, LAST_UNIT[n] + 1)
            elif PIECES[n] in ("wbp", "wbm"):
                engine.wait_ge(unit_done, LAST_UNIT[n] - 1)
            else:
                engine.wait_ge(first_half_used, N_FULL[n])

        N0 = len(PIECES)

        def expert_piece(j):
            m, h = divmod(j, 2)
            which = [(w_gate, 0), (w_up, 0), (w_gate, 1), (w_up, 1), (w_down, 0), (w_down, 1)][m]
            return which[0], which[1], h

        turn_slot = [MOE_SLOT[q % RING] for q in range(PER_TURN)]

        def moe_slot(q):
            return turn_slot[q]

        def moe_landed(turn, q):
            return turn * (16 * turn_slot.count(turn_slot[q])) + 16 * turn_slot[:q + 1].count(turn_slot[q])

        def place_left(turn, q):
            before = [b for b in range(q - PER_TURN, q) if turn_slot[b % PER_TURN] == turn_slot[q]][-1]
            return turn * PER_TURN + (before + 1)

        block = ctx.enter_context(nc.Block())

        @block.sync
        def _(sp):
            sp.dma_start(X[:, 0, :], x[0, 0:P, :]).then_inc(x_in, 16)
            sp.dma_start(X[:, 1, :], x[0, P:SEQ, :]).then_inc(x_in, 16)

            def load(H):
                if H >= HALVES:
                    half_free(sp, H - HALVES)
                sp.dma_start(raw(H).rearrange("p (k n) -> p k n", k=4), half_source(H)).then_inc(raw_in[H % HALVES], 16)

            load(0)
            load(1)
            sp.dma_start(MEM, mem[0].rearrange("(t p) n -> p t n", p=P)).then_inc(mem_in, 16)
            with nc.allow_non_contiguous_dma(reason="short per-partition vector"):
                sp.dma_start(gain_col[1], g_mem.rearrange("(k p) -> p k", p=P)).then_inc(mem_gain_in, 16)
            load(2)
            load(3)
            def row(v):
                return v.rearrange("(a n) -> a n", a=1)

            lam4 = tmp[:, 1, 0:4 * HD].rearrange("p (a n) -> p a n", a=4)
            with nc.allow_non_contiguous_dma(reason="short per-partition vectors"):
                for a, v in enumerate((lambda_q1, lambda_k1, lambda_q2, lambda_k2)):
                    sp.dma_start(lam4[:, a, :], row(v).to_broadcast([P, HD])).then_inc(vec_in, 16)
                sp.dma_start(gqk[:, 0, :], row(q_norm).to_broadcast([P, HD])).then_inc(vec_in, 16)
                sp.dma_start(gqk[:, 1, :], row(k_norm).to_broadcast([P, HD])).then_inc(vec_in, 16)
                for dst, v in ((mq_col, mq_norm.rearrange("(p a) -> p a", a=1)), (mk_col, mk_norm.rearrange("(p a) -> p a", a=1)),
                               (sub_col, g_subln.rearrange("(p a) -> p a", a=1)), (psc_col, pool_scale.rearrange("(g p) -> p g", p=P)),
                               (gain_col[2], g_ffn.rearrange("(k p) -> p k", p=P)), (b_rt, row(b_router).to_broadcast([P, EXPERTS])),
                               (con[:, P:C_ALL], table[:, P:C_ALL])):
                    sp.dma_start(dst, v).then_inc(con_in, 16)
            load(4)
            def load_expert(pair, q):
                j = q % PER_PAIR
                w, e, h = expert_piece(j)
                one = w[bass.ds(pair * 2 + e, 1), :, :].rearrange("e r n -> (e r) n")
                if j < 8:
                    part = one.rearrange("(p k) n -> p k n", k=KD)[:, 4 * h:4 * h + 4, :]
                else:
                    part = one[h * HALF:(h + 1) * HALF, :].rearrange("(p k) n -> p k n", k=4)
                dst = moe_ring[:, moe_slot(q), :].rearrange("p (k n) -> p k n", k=4)
                sp.dma_start(dst, part).then_inc(ring_in[moe_slot(q)], 16)

            def biases(d, s):
                sp.dma_start(B4[s][0:2, :], b_gate[bass.ds(d * 4 + s * 2, 2), :]).then_inc(bias_in, 16)
                sp.dma_start(B4[s][2:4, :], b_up[bass.ds(d * 4 + s * 2, 2), :]).then_inc(bias_in, 16)

            def rest_of_turn(turn, d):
                for q in range(RING, PER_TURN):
                    sp.wait_ge(used, place_left(turn, q))
                    if q == PER_PAIR:
                        biases(d, 1)
                    load_expert(d * 2 + q // PER_PAIR, q)

            def start_of_turn(turn, d):
                for q in range(RING):
                    sp.wait_ge(used, place_left(turn, q))
                    if q == 0:
                        biases(d, 0)
                    load_expert(d * 2, q)

            for H in range(HALVES, 2 * N0):
                load(H)
                if H == HALVES + 2:
                    sp.dma_start(BAND, band.rearrange("(t p) g n -> p t g n", p=P)).then_inc(band_in, 16)
                    sp.dma_start(POOLW, pool_w.rearrange("g p n -> p g n")).then_inc(band_in, 16)
                if H == 2 * PIECES.index("wba1"):
                    sp.wait_ge(pv_done, HEADS)
                    sp.wait_ge(merged, 4)
                    load_expert(0, 0)
                if H == 2 * PIECES.index("wo0"):
                    sp.wait_ge(unit_done, UNIT_OF[("ga1", NT - 1, 0)] + 1)
                    biases(0, 0)
                    load_expert(0, 1)
            for q, name in enumerate(("wba1", "merged", "wo0", "wo0", "wo1", "wo1", "logits"), 2):
                if name == "logits":
                    sp.wait_ge(logit_done, NT)
                elif name == "merged":
                    sp.wait_ge(mgT_done, 4)
                else:
                    sp.wait_ge(unit_done, UNIT_OF[(name, NT - 1, 0)] + 1)
                load_expert(0, q)

            def round_of(r):
                base = r * (PAIRS // 2)
                with sp.Fori(0, PAIRS // 2 - 1) as d:
                    rest_of_turn(base + d, d)
                    start_of_turn(base + d + 1, d + 1)
                rest_of_turn(base + (PAIRS // 2 - 1), PAIRS // 2 - 1)

            round_of(0)
            sp.wait_ge(rounds_ready, 1)
            n_rounds = sp.value_load(rounds[0:1, 0:1], min_val=1, max_val=SEQ // SLOTS)
            with sp.If(n_rounds > 1):
                with sp.Fori(1, n_rounds) as r:
                    start_of_turn(r * (PAIRS // 2), 0)
                    round_of(r)
            for j in range(4):
                t, h = divmod(j, 2)
                sp.wait_ge(y_added, n_rounds * (4 * PAIRS) + 2 + (j + 1))
                sp.dma_start(out[0, t * P:(t + 1) * P, h * HALF:(h + 1) * HALF],
                             X[:, t, h * HALF:(h + 1) * HALF]).then_inc(out_done, 16)
            sp.wait_ge(out_done, 16 * 4)

        @block.gpsimd
        def _(pool):
            def root(n, cols):
                pool.wait_ge(ms_ready, n + 1)
                nc.gpsimd.tensor_tensor(stat[:, cols], stat[:, cols], minus_half.to_broadcast([P, cols.stop - cols.start]),
                                        ALU.pow).then_inc(root_done, 1)

            nc.gpsimd.memset(minus_half, -0.5).then_inc(exponent_ready, 1)
            def lower_parts(first, after):
                for H in range(first, after):
                    upper_made(pool, H)
                    nc.gpsimd.tensor_tensor(lower(H), raw(H), upper(H), ALU.subtract).then_inc(lo_ready, 1)

            pool.wait_ge(exponent_ready, 1)
            root(0, slice(0, 2))
            lower_parts(EARLY, 4)
            root(1, slice(2, 4))
            lower_parts(4, 8)
            pool.wait_ge(con_in, 16 * 7)
            pool.wait_ge(vec_in, 16 * 6)
            h = HD // 2

            def angles(base):
                return con[:, base:base + NT * h].rearrange("p (t n) -> p t n", t=NT)

            for w in range(2):
                lo = gqk[:, w, 0:h].unsqueeze(1).to_broadcast([P, NT, h])
                hi = gqk[:, w, h:HD].unsqueeze(1).to_broadcast([P, NT, h])
                for o, a, b in ((rot[:, w, 0, :, 0:h], lo, angles(C_COS)), (rot[:, w, 0, :, h:HD], hi, angles(C_COS)),
                                (rot[:, w, 1, :, 0:h], hi, angles(C_NSIN)), (rot[:, w, 1, :, h:HD], lo, angles(C_SIN))):
                    nc.gpsimd.tensor_tensor(o, a, b, ALU.mult).then_inc(rot_ready, 1)

            def gate_bias(n, branch, first):
                for t in range(NT):
                    pool.dma_start(G[branch][:, t, :], b_gates[first:first + D].rearrange("(a n) -> a n", a=1)
                                   .to_broadcast([P, D])).then_inc(gbias_in[n], 16)

            lower_parts(8, 20)
            pool.wait_ge(kq_done, 4)
            pool.wait_ge(z_done, 2)
            gate_bias(0, "p", D)
            lower_parts(20, 23)
            pool.wait_ge(mo_done, MHEADS)
            gate_bias(1, "m", 2 * D)
            lower_parts(23, 30)
            last = UNIT_OF[("wbp", 1, 1)]
            pool.wait_ge(bank_read[last % 3], last // 3 + 1)
            gate_bias(2, "a", 0)

            lower_parts(30, 37)
            pool.wait_ge(pv_done, HEADS)
            root(2, slice(128, 144))
            nc.gpsimd.memset(OE, 0.0).then_inc(seed_clear, 1)
            lower_parts(37, 41)
            pool.wait_ge(merged, 4)
            pool.wait_ge(seed_clear, 1)
            pool.dma_start(OE[0:EXPERTS, :], b_down).then_inc(seed_in, 16)
            nc.gpsimd.memset(PWT, 0.0).then_inc(seed_clear, 1)
            pool.dma_start(GFF, g_ffn.rearrange("(a n) -> a n", a=1).to_broadcast([P, D])).then_inc(late_in, 16)
            pool.dma_start(WR, w_router.rearrange("(k p) e -> p k e", p=P)).then_inc(late_in, 16)
            lower_parts(41, 44)
            root(3, slice(4, 5))
            root(4, slice(5, 6))

        @block.scalar
        def _(act):
            act.dma_start(con[:, C_ID:C_ID + P], table[:, C_ID:C_ID + P]).then_inc(ident_in, 16)
            with nc.allow_non_contiguous_dma(reason="short per-partition vectors"):
                act.dma_start(gain_col[0], g_mix.rearrange("(k p) -> p k", p=P)).then_inc(gain_in, 16)

            def evac(u, dst):
                _, name, t, _ = UNITS[u]
                n = 1 if name in ("mk", "mv") else 0
                act.wait_ge(unit_done, u + 1)
                act.wait_ge(root_done, n + 1)
                nc.scalar.activation(dst, UB[u % 3][:, :], ACT.Copy, scale=stat[:, 2 * n + t:2 * n + t + 1]).then_inc(bank_read[u % 3], 1)

            def hi(H):
                act.wait_ge(raw_in[H % HALVES], 16 * (H // HALVES + 1))
                if H < EARLY:
                    for cols in (slice(0, 1024), slice(1024, 2048)):
                        nc.scalar.activation(upper(H)[:, cols], raw(H)[:, cols], ACT.Copy).then_inc(hi_early, 1)
                else:
                    nc.scalar.activation(upper(H), raw(H), ACT.Copy).then_inc(hi_act, 1)

            def root(n, cols):
                act.wait_ge(gms_ready, n + 1)
                nc.scalar.activation(stat[:, cols], stat[:, cols], ACT.Sqrt).then_inc(groot_done, 1)

            def gate_exp(u):
                _, name, t, _ = UNITS[u]
                g = G[name[1]][:, t, int(name[2]) * HALF:(int(name[2]) + 1) * HALF]
                act.wait_ge(bank_read[u % 3], u // 3 + 1)
                nc.scalar.activation(g, g, ACT.Tanh, scale=0.5).then_inc(gexp_done, 1)

            act.wait_ge(x_in, 16 * NT)
            for t in range(NT):
                if t:
                    act.wait_ge(squares, t)
                nc.scalar.activation(JUNK, X[:, t, :], ACT.Square, accum_out=stat[:, t:t + 1]).then_inc(squares, 1)
            hi(0)
            hi(1)
            act.wait_ge(mem_in, 16)
            for t in range(NT):
                act.wait_ge(squares, 2 + t)
                nc.scalar.activation(JUNK, MEM[:, t, :], ACT.Square, accum_out=stat[:, 2 + t:3 + t]).then_inc(squares, 1)
            hi(2)
            hi(3)
            evac(0, U[:, 0, :])
            hi(4)
            evac(1, U[:, 1, :])
            hi(5)
            hi(6)
            evac(2, KM[:, 0, :])
            evac(3, KM[:, 1, :])
            hi(7)
            hi(8)
            evac(4, VM[:, 0, :])
            root(0, slice(8, 16))
            evac(5, VM[:, 1, :])
            hi(9)
            hi(10)
            evac(6, QM[:, 0, :])
            evac(7, QM[:, 1, :])
            hi(11)
            for j in range(2):
                act.wait_ge(z_done, j + 1)
                nc.scalar.activation(ZT[:, 2 * j:2 * j + 2, :], bank[4 + j][:, :].rearrange("p (g n) -> p g n", g=2),
                                     ACT.Copy).then_inc(zT_copied, 1)
            root(1, slice(16, 24))

            def qk_dst(u):
                _, name, t, _ = UNITS[u]
                return {"q": Q, "k": K, "v": V}[name[0]][:, t, int(name[1]) * HALF:(int(name[1]) + 1) * HALF]

            def qk_unit(u):
                if u % 2 == 0:
                    hi(u + 4)
                act.wait_ge(unit_done, u + 1)
                act.wait_ge(root_done, 1)
                if u >= 10:
                    act.wait_ge(gms_ready, u - 7)
                else:
                    act.wait_ge(squares, 4)
                t = UNITS[u][2]
                nc.scalar.activation(SQ[:, u % 2, :], UB[u % 3][:, :], ACT.Square, scale=stat[:, t:t + 1]).then_inc(sq_done, 1)
                evac(u, qk_dst(u))
                root(u - 6, slice(24 + 8 * (u % 2), 32 + 8 * (u % 2)))
                if u % 2 == 1:
                    hi(u + 4)

            for u in range(8, 16):
                qk_unit(u)
            act.wait_ge(lam_sum, 1)
            nc.scalar.activation(lam_e, lam_e, ACT.Exp).then_inc(lam_exp, 1)

            def mem_exp(h):
                act.wait_ge(mmax_ready, h + 1)
                for t in range(NT):
                    c = 64 + 4 * (h % 2) + t
                    ins = nc.scalar.activation(prob[:, h % 2, t * SEQ:(t + 1) * SEQ], bank[4 + h % 2][:, t * SEQ:(t + 1) * SEQ],
                                               ACT.Exp, bias=stat[:, c:c + 1], scale=MHD ** -0.5,
                                               accum_out=stat[:, c + 2:c + 3])
                ins.then_inc(mexp_done, 1)

            def mem_probT(h):
                act.wait_ge(mt_done, h + 1)
                nc.scalar.activation(probT[:, h % 2, :], bank[6][:, :], ACT.Copy).then_inc(pt_copied, 1)

            mem_exp(0)
            hi(20)
            evac(16, qk_dst(16))
            mem_exp(1)
            mem_probT(0)
            evac(17, qk_dst(17))
            hi(21)
            mem_exp(2)
            mem_probT(1)
            hi(22)
            evac(18, qk_dst(18))
            mem_exp(3)
            mem_probT(2)
            evac(19, qk_dst(19))
            mem_probT(3)

            def qkT(h):
                act.wait_ge(qk_done, h + 1)
                nc.scalar.activation(qkt[:, h % 2, :], bank[3][:, :], ACT.Copy).then_inc(qkT_copied, 1)

            def exps(h):
                act.wait_ge(max_ready, h + 1)
                for c in range(2):
                    for t, (a, b) in enumerate(((0, P), (P, 3 * P))):
                        s = prob[:, h % 2, c * 384 + a:c * 384 + b]
                        m = 96 + 16 * (h % 2) + 2 * c + t
                        ins = nc.scalar.activation(s, s, ACT.Exp, bias=stat[:, m:m + 1], scale=HD ** -0.5,
                                                   accum_out=stat[:, m + 4:m + 5])
                ins.then_inc(exp_done, 1)

            def aT(h):
                act.wait_ge(at_done, h + 1)
                nc.scalar.activation(probT[:, h % 2, 0:384], bank[6][:, 0:384], ACT.Copy).then_inc(at_copied, 1)

            def o_out(h):
                act.wait_ge(pv_done, h + 1)
                nc.scalar.activation(O[:, :, h * P:(h + 1) * P], bank[7][:, 0:256].rearrange("p (t n) -> p t n", t=NT),
                                     ACT.Copy).then_inc(o_copied, 1)

            qkT(0)
            gate_exp(20)
            exps(0)
            qkT(1)
            gate_exp(21)
            for h in range(HEADS):
                for_gate = [u for u in (22 + 2 * h, 23 + 2 * h) if UNITS[u][1][0] == "g"]
                if h + 1 < HEADS:
                    exps(h + 1)
                if h == HEADS - 1:
                    aT(h)
                if 22 + 2 * h in for_gate:
                    gate_exp(22 + 2 * h)
                if h < HEADS - 1:
                    aT(h)
                if h + 2 < HEADS:
                    qkT(h + 2)
                if h == HEADS - 1:
                    o_out(h)
                if 23 + 2 * h in for_gate:
                    gate_exp(23 + 2 * h)
                if h < HEADS - 1:
                    o_out(h)
            gate_exp(38)
            for j in range(4):
                if j == 2:
                    gate_exp(39)
                act.wait_ge(oT_done, j + 1)
                t, h = divmod(j, 2)
                nc.scalar.activation(OT[0][:, 4 * h:4 * h + 4, t * P:(t + 1) * P],
                                     bank[3 + j][:, :].rearrange("p (k n) -> p k n", k=4), ACT.Copy,
                                     scale=sub_gain).then_inc(oT_copied, 1)
            for j in range(4):
                act.wait_ge(mgT_done, j + 1)
                h, t = divmod(j, 2)
                nc.scalar.activation(MGT[0][:, 4 * h:4 * h + 4, t * P:(t + 1) * P],
                                     bank[3 + j][:, :].rearrange("p (k n) -> p k n", k=4), ACT.Copy, scale=0.5).then_inc(mgT_copied, 1)

            def h_square(t):
                act.wait_ge(h_ready, 3 + t)
                act.wait_ge(squares, 4 + t)
                nc.scalar.activation(H_JUNK, X[:, t, :], ACT.Square, accum_out=stat[:, 4 + t:5 + t]).then_inc(squares, 1)

            h_square(0)
            for t in range(NT):
                act.wait_ge(top_ready, t + 1)
                nc.scalar.activation(GATE[:, t, :], LG[:, t, :], ACT.Exp, bias=stat[:, 180 + t:181 + t]).then_inc(lexp_done, 1)
                if t == 0:
                    h_square(1)
            act.wait_ge(gT_done, 1)
            act.wait_ge(seed_clear, 2)
            nc.scalar.activation(PWT[0:EXPERTS, :], bank[6][0:EXPERTS, 0:SEQ], ACT.Copy).then_inc(wT_copied, 1)
            act.wait_ge(rounds_ready, 1)
            n_rounds = act.value_load(rounds[0:1, 0:1], min_val=1, max_val=SEQ // SLOTS)
            with act.Fori(0, n_rounds) as r:
                with act.Fori(0, PAIRS // 2) as d:
                    for s in range(2):
                        i = d * 2 + s
                        it = r * PAIRS + i
                        act.wait_ge(disp_done, it * 2 + 1)
                        nc.scalar.activation(XE[:, 0:4, :], bank[4][:, :].rearrange("p (k n) -> p k n", k=4),
                                             ACT.Copy).then_inc(xe_lo, 1)
                        for e in range(2):
                            act.wait_ge(g_read, it * 2 + (e + 1))
                            nc.scalar.activation(SG, GS, ACT.Sigmoid, scale=ALPHA).then_inc(sig_done, 1)
                            if e == 0:
                                act.wait_ge(slots_free, it + 1)
                                act.wait_ge(comb_done, it * 4 + 4)
                                nc.scalar.activation(PWT, bank[3][:, 0:SEQ], ACT.Copy).then_inc(wT_copied, 1)
                        for e in range(2):
                            act.wait_ge(actT_done, it * 2 + (e + 1))
                            nc.scalar.activation(AHT, bank[3][:, :].rearrange("p (j s) -> p j s", j=4),
                                                 ACT.Copy).then_inc(actT_copied, 1)
                            act.wait_ge(used, it * PER_PAIR + (10 + 2 * e))
                            nc.scalar.activation(OE[e * SLOTS:(e + 1) * SLOTS, 0:HALF], bank[2][0:SLOTS, :],
                                                 ACT.Copy).then_inc(o_lo, 1)

        @block.vector
        def _(dve):
            n_step = [0]

            def link(ins):
                n_step[0] += 1
                ins.then_inc(dve_step, 1)
                dve.wait_ge(dve_step, n_step[0])

            def mean_square(n, cols, width):
                nc.vector.tensor_scalar(stat[:, cols], stat[:, cols], 1.0 / width, EPS, ALU.mult, ALU.add).then_inc(ms_ready, 1)

            def group_root(n, cols, width):
                nc.vector.tensor_scalar(stat[:, cols], stat[:, cols], 1.0 / width, EPS, ALU.mult, ALU.add).then_inc(gms_ready, 1)
                dve.wait_ge(groot_done, n + 1)
                link(nc.vector.reciprocal(stat[:, cols], stat[:, cols]))

            def hi(H):
                dve.wait_ge(raw_in[H % HALVES], 16 * (H // HALVES + 1))
                nc.vector.tensor_copy(upper(H), raw(H)).then_inc(hi_dve, 1)

            def lo(H):
                for step, cols in enumerate((slice(0, 1024), slice(1024, 2048))):
                    dve.wait_ge(hi_early, 2 * H + step + 1)
                    nc.vector.tensor_tensor(lower(H)[:, cols], raw(H)[:, cols], upper(H)[:, cols],
                                            ALU.subtract).then_inc(lo_early, 1)

            def split(product, operand, blocks, cols, signal):
                high, low, place = (x[:, blocks, cols] for x in operand)
                link(product(place))
                link(nc.vector.tensor_copy(high, place))
                nc.vector.tensor_tensor(low, place, high, ALU.subtract).then_inc(signal, 1)

            def turned(n, j):
                dst, done, copied = ((XNT, xT_done, xT_copied), (MEMT, mT_done, mT_copied))[n]
                dve.wait_ge(done, j + 1)
                t, h = divmod(j, 2)
                split(lambda place: nc.vector.tensor_tensor(place, bank[3 + j][:, :].rearrange("p (k n) -> p k n", k=4),
                                                            gain_col[n][:, 4 * h:4 * h + 4].unsqueeze(2).to_broadcast([P, 4, P]),
                                                            ALU.mult),
                      dst, slice(4 * h, 4 * h + 4), slice(t * P, (t + 1) * P), copied)

            dve.wait_ge(gain_in, 16)
            turned(0, 0)
            turned(0, 1)
            lo(0)
            turned(0, 2)
            lo(1)
            turned(0, 3)
            dve.wait_ge(squares, 2)
            mean_square(0, slice(0, 2), D)
            dve.wait_ge(mem_gain_in, 16)
            turned(1, 0)
            turned(1, 1)
            turned(1, 2)
            turned(1, 3)
            dve.wait_ge(squares, 4)
            mean_square(1, slice(2, 4), D)
            dve.wait_ge(vec_in, 16 * 6)
            lam4 = tmp[:, 1, 0:4 * HD].rearrange("p (a n) -> p a n", a=4)
            for a in range(2):
                link(nc.vector.tensor_tensor(tmp[:, 0, a * HD:(a + 1) * HD], lam4[:, 2 * a, :], lam4[:, 2 * a + 1, :], ALU.mult))
            nc.vector.tensor_reduce(lam_e, tmp[:, 0, 0:2 * HD].rearrange("p (a n) -> p a n", a=2), AX_X,
                                    ALU.add).then_inc(lam_sum, 1)

            def group_stats(rows3, groups, sq, col, width):
                link(nc.vector.tensor_tensor(sq, rows3, rows3, ALU.mult))
                link(nc.vector.tensor_reduce(stat[:, col:col + groups], sq, AX_X, ALU.add))

            dve.wait_ge(lam_sum, 1)
            for n, (rows_, first, col) in enumerate(((KM, 2, 8), (QM, 6, 16))):
                for u in (first, first + 1):
                    dve.wait_ge(bank_read[u % 3], u // 3 + 1)
                flat = rows_.rearrange("p t (h n) -> p (t h) n", n=MHD)
                group_stats(flat, 8, tmp[:, :, :].rearrange("p t (h n) -> p (t h) n", n=MHD), col, MHD)
                group_root(n, slice(col, col + 8), MHD)
                nc.vector.tensor_tensor(flat, flat, stat[:, col:col + 8].unsqueeze(2).to_broadcast([P, 8, MHD]),
                                        ALU.mult).then_inc(mem_normed, 1)

            def norm_rotate(u):
                _, name, t, _ = UNITS[u]
                w = 0 if name[0] == "q" else 1
                raw = (Q if w == 0 else K)[:, t, int(name[1]) * HALF:(int(name[1]) + 1) * HALF].rearrange("p (m n) -> p m n", n=HD)
                a = tmp[:, 0, :].rearrange("p (m n) -> p m n", n=HD)
                b = tmp[:, 1, :].rearrange("p (m n) -> p m n", n=HD)
                col = 24 + 8 * (u % 2)
                hf = HD // 2
                if u > 8:
                    dve.wait_ge(normed, u - 8)
                dve.wait_ge(bank_read[u % 3], u // 3 + 1)
                dve.wait_ge(sq_done, u - 7)
                link(nc.vector.tensor_reduce(stat[:, col:col + 8], SQ[:, u % 2, :].rearrange("p (m n) -> p m n", n=HD), AX_X, ALU.add))
                group_root(u - 6, slice(col, col + 8), HD)
                link(nc.vector.tensor_tensor(a, raw, stat[:, col:col + 8].unsqueeze(2).to_broadcast([P, 8, HD]), ALU.mult))
                nc.vector.tensor_tensor(b[:, :, 0:hf], a[:, :, hf:HD],
                                        rot[:, w, 1, t, 0:hf].unsqueeze(1).to_broadcast([P, 8, hf]), ALU.mult)
                link(nc.vector.tensor_tensor(b[:, :, hf:HD], a[:, :, 0:hf],
                                             rot[:, w, 1, t, hf:HD].unsqueeze(1).to_broadcast([P, 8, hf]), ALU.mult))
                link(nc.vector.tensor_tensor(a, a, rot[:, w, 0, t, :].unsqueeze(1).to_broadcast([P, 8, HD]), ALU.mult))
                nc.vector.tensor_tensor(raw, a, b, ALU.add).then_inc(normed, 1)

            dve.wait_ge(lam_sum, 1)
            dve.wait_ge(rot_ready, 8)
            norm_rotate(8)
            norm_rotate(9)
            dve.wait_ge(con_in, 16 * 7)
            link(nc.vector.tensor_scalar(sub_gain, sub_col, 1.0 - LAMBDA_INIT, None, ALU.mult))
            for j in range(2):
                dve.wait_ge(z2_done, j + 1)
                split(lambda place: nc.vector.tensor_tensor(place, bank[4 + j][:, :].rearrange("p (g n) -> p g n", g=2),
                                                            psc_col[:, 2 * j:2 * j + 2].unsqueeze(2).to_broadcast([P, 2, SEQ]),
                                                            ALU.mult),
                      Z2T, slice(2 * j, 2 * j + 2), slice(0, SEQ), z2T_copied)
            norm_rotate(10)
            norm_rotate(11)
            for j, (dst, t, gain) in enumerate(((KMT, 0, mk_col), (KMT, 1, mk_col), (QMT, 0, mq_col), (QMT, 1, mq_col))):
                dve.wait_ge(kq_done, j + 1)
                nc.vector.tensor_scalar(dst[:, :, t * P:(t + 1) * P], bank[(3, 6, 4, 5)[j]][:, :].rearrange("p (h n) -> p h n", h=MHEADS),
                                        gain, None, ALU.mult).then_inc(kqT_copied, 1)
            norm_rotate(12)
            norm_rotate(13)

            def mem_max(h):
                c = 64 + 4 * (h % 2)
                dve.wait_ge(ms_done, h + 1)
                link(nc.vector.tensor_reduce(stat[:, c:c + 2], bank[4 + h % 2][:, :].rearrange("p (t n) -> p t n", t=NT), AX_X,
                                             ALU.max, negate=True))
                nc.vector.tensor_scalar(stat[:, c:c + 2], stat[:, c:c + 2], MHD ** -0.5, None, ALU.mult).then_inc(mmax_ready, 1)

            def mem_scale(h):
                c = 66 + 4 * (h % 2)
                dve.wait_ge(mexp_done, h + 1)
                link(nc.vector.reciprocal(stat[:, c:c + 2], stat[:, c:c + 2]))
                p = prob[:, h % 2, 0:HALF].rearrange("p (t n) -> p t n", t=NT)
                nc.vector.tensor_tensor(p, p, stat[:, c:c + 2].unsqueeze(2).to_broadcast([P, NT, SEQ]), ALU.mult).then_inc(mp_ready, 1)

            def mem_out(h):
                dve.wait_ge(mo_done, h + 1)
                split(lambda place: nc.vector.tensor_copy(place, bank[7][:, 0:SEQ]), OMT, h, slice(0, SEQ), omT_copied)

            norm_rotate(14)
            norm_rotate(15)
            mem_max(0)
            mem_scale(0)
            mem_max(1)
            mem_scale(1)
            mem_out(0)
            mem_max(2)
            mem_scale(2)
            mem_out(1)
            mem_max(3)
            mem_scale(3)
            mem_out(2)
            dve.wait_ge(lam_exp, 1)
            link(nc.vector.tensor_tensor(nlam, lam_e[:, 1:2], lam_e[:, 0:1], ALU.subtract))
            link(nc.vector.tensor_scalar(nlam, nlam, -LAMBDA_INIT, None, ALU.add))

            def add_bias(u):
                _, name, t, _ = UNITS[u]
                g = G[name[1]][:, t, int(name[2]) * HALF:(int(name[2]) + 1) * HALF]
                dve.wait_ge(gbias_in["pma".index(name[1])], 16 * NT)
                dve.wait_ge(unit_done, u + 1)
                nc.vector.scalar_tensor_tensor(out=g, in0=UB[u % 3][:, :], scalar=stat[:, t:t + 1], in1=g, op0=ALU.mult,
                                               op1=ALU.add).then_inc(bank_read[u % 3], 1)

            gates_before = {}
            seen = 0
            for u, (_, name, t, _) in enumerate(UNITS):
                if name[0] == "g":
                    seen += 1
                    gates_before[(name[1], t, int(name[2]))] = seen

            def merge(u):
                _, name, t, c = UNITS[u]
                branch, n = {"wbp": ("p", c), "wbm": ("m", c), "wba0": ("a", 0), "wba1": ("a", 1)}[name]
                cols = slice(n * HALF, (n + 1) * HALF)
                g = G[branch][:, t, cols]
                dve.wait_ge(gexp_done, gates_before[(branch, t, n)])
                dve.wait_ge(unit_done, u + 1)
                dst = {"p": MG[:, t, cols], "m": tmp[:, 0, :], "a": LATE_TMP}[branch]
                nc.vector.scalar_tensor_tensor(out=dst, in0=g, scalar=1.0, in1=UB[u % 3][:, :], op0=ALU.add,
                                               op1=ALU.mult).then_inc(bank_read[u % 3], 1)
                dve.wait_ge(bank_read[u % 3], u // 3 + 1)
                if branch == "p":
                    return
                nc.vector.tensor_tensor(MG[:, t, cols], MG[:, t, cols], dst, ALU.add).then_inc(merged, 1)
                n_merged[0] += 1
                dve.wait_ge(merged, n_merged[0])

            n_merged = [0]

            split_after = {}
            for n in range(10, N0):
                if n == 17:
                    continue
                short = PIECES[n] in ("wbp", "wbm")
                second = LAST_UNIT[n] - (2 if short else 1)
                for H, u in ((2 * n + 3, second - 1 if short else second), (2 * n + 4, second)):
                    if H < 2 * N0:
                        split_after.setdefault(u, []).append(H)

            def split_next(u):
                for H in split_after.get(u, ()):
                    hi(H)

            def unit(u):
                (add_bias if UNITS[u][1][0] == "g" else merge)(u)
                split_next(u)

            def head_max(h):
                dve.wait_ge(sc_done, h + 1)
                m = 96 + 16 * (h % 2)
                for c in range(2):
                    s = prob[:, h % 2, c * 384:(c + 1) * 384]
                    b = bank[4 + c]
                    nc.vector.tensor_tensor(s[:, 0:P], b[:, 0:P], mask[:, P:2 * P], ALU.add)
                    link(nc.vector.tensor_tensor(s[:, P:3 * P], b[:, P:3 * P], mask, ALU.add))
                    nc.vector.tensor_reduce(stat[:, m + 2 * c:m + 2 * c + 1], s[:, 0:P], AX_X, ALU.max)
                    link(nc.vector.tensor_reduce(stat[:, m + 2 * c + 1:m + 2 * c + 2], s[:, P:3 * P], AX_X, ALU.max))
                nc.vector.tensor_scalar(stat[:, m:m + 4], stat[:, m:m + 4], -HD ** -0.5, None, ALU.mult).then_inc(max_ready, 1)

            def head_weights(h):
                m = 96 + 16 * (h % 2) + 4
                dve.wait_ge(exp_done, h + 1)
                link(nc.vector.reciprocal(stat[:, m:m + 4], stat[:, m:m + 4]))
                link(nc.vector.tensor_scalar(stat[:, m + 2:m + 4], stat[:, m + 2:m + 4], nlam, None, ALU.mult))
                for t, (a, b) in enumerate(((0, P), (P, 3 * P))):
                    p0, p1 = prob[:, h % 2, a:b], prob[:, h % 2, 384 + a:384 + b]
                    link(nc.vector.tensor_scalar(p0, p0, stat[:, m + t:m + t + 1], None, ALU.mult))
                    ins = nc.vector.scalar_tensor_tensor(out=p0, in0=p1, scalar=stat[:, m + 2 + t:m + 3 + t], in1=p0,
                                                         op0=ALU.mult, op1=ALU.add)
                ins.then_inc(a_ready, 1)

            add_bias(20)
            mem_out(3)
            head_max(0)
            split_next(20)
            head_weights(0)
            unit(21)
            for h in range(HEADS):
                if h + 1 < HEADS:
                    head_max(h + 1)
                unit(22 + 2 * h)
                if h + 1 < HEADS:
                    head_weights(h + 1)
                    unit(23 + 2 * h)
            dve.wait_ge(o_copied, HEADS)
            sq = region[2][:, 0:1024].rearrange("p (h n) -> p h n", h=HEADS)
            for t in range(NT):
                link(nc.vector.tensor_tensor(sq, O[:, t, :].rearrange("p (h n) -> p h n", h=HEADS),
                                             O[:, t, :].rearrange("p (h n) -> p h n", h=HEADS), ALU.mult))
                link(nc.vector.tensor_reduce(stat[:, 128 + 8 * t:136 + 8 * t], sq, AX_X, ALU.add))
            mean_square(2, slice(128, 144), P)
            hi(37)
            hi(38)
            dve.wait_ge(root_done, 3)
            for t in range(NT):
                o3 = O[:, t, :].rearrange("p (h n) -> p h n", h=HEADS)
                nc.vector.tensor_tensor(o3, o3, stat[:, 128 + 8 * t:136 + 8 * t].unsqueeze(2).to_broadcast([P, HEADS, P]),
                                        ALU.mult).then_inc(o_normed, 1)
            unit(37)
            unit(38)
            for j in range(4):
                if j == 2:
                    unit(39)
                dve.wait_ge(oT_copied, j + 1)
                t, h = divmod(j, 2)
                at = (slice(None), slice(4 * h, 4 * h + 4), slice(t * P, (t + 1) * P))
                nc.vector.scalar_tensor_tensor(out=OT[1][at], in0=bank[3 + j][:, :].rearrange("p (k n) -> p k n", k=4),
                                               scalar=sub_gain, in1=OT[0][at], op0=ALU.mult, op1=ALU.subtract).then_inc(oT_split, 1)
            def merged_lower(j):
                dve.wait_ge(mgT_copied, j + 1)
                h, t = divmod(j, 2)
                at = (slice(None), slice(4 * h, 4 * h + 4), slice(t * P, (t + 1) * P))
                nc.vector.scalar_tensor_tensor(out=MGT[1][at], in0=bank[3 + j][:, :].rearrange("p (k n) -> p k n", k=4), scalar=0.5,
                                               in1=MGT[0][at], op0=ALU.mult, op1=ALU.subtract).then_inc(mgT_split, 1)

            for u in range(40, 43):
                unit(u)
            merged_lower(0)
            merged_lower(1)
            unit(43)
            merged_lower(2)
            merged_lower(3)

            def add_h(u):
                _, name, t, _ = UNITS[u]
                cols = slice(int(name[2]) * HALF, (int(name[2]) + 1) * HALF)
                dve.wait_ge(unit_done, u + 1)
                nc.vector.tensor_tensor(X[:, t, cols], UB[u % 3][:, :], X[:, t, cols], ALU.add).then_inc(h_ready, 1)
                split_next(u)

            def copy_hT(n, t, h):
                dve.wait_ge(hT_done, n + 1)
                nc.vector.tensor_tensor(HNT[:, 4 * h:4 * h + 4, t * P:(t + 1) * P],
                                        bank[3 + n][:, :].rearrange("p (k n) -> p k n", k=4),
                                        gain_col[2][:, 4 * h:4 * h + 4].unsqueeze(2).to_broadcast([P, 4, P]),
                                        ALU.mult).then_inc(hT_copied, 1)

            def norm_h(t):
                dve.wait_ge(late_in, 32)
                nc.vector.scalar_tensor_tensor(
                    out=HN[:, t, :, :], in0=X[:, t, :].rearrange("p (n k) -> p k n", k=KD), scalar=stat[:, 4 + t:5 + t],
                    in1=GFF.rearrange("p (n k) -> p k n", k=KD), op0=ALU.mult, op1=ALU.mult).then_inc(hn_ready, 1)

            def route(t):
                top = stat[:, 160 + 8 * t:168 + 8 * t]
                dve.wait_ge(root_done, 4 + t)
                dve.wait_ge(logit_done, t + 1)
                link(nc.vector.scalar_tensor_tensor(out=LG[:, t, :], in0=bank[7][:, t * EXPERTS:(t + 1) * EXPERTS],
                                                    scalar=stat[:, 4 + t:5 + t], in1=b_rt, op0=ALU.mult, op1=ALU.add))
                link(nc.vector.max(top, LG[:, t, :]))
                nc.vector.tensor_scalar(stat[:, 180 + t:181 + t], top[:, 0:1], -1.0, None, ALU.mult).then_inc(top_ready, 1)
                fourth = top[:, TOP_K - 1:TOP_K]
                above, equal, run, zero = (SCR[:, 4 * t + i, :] for i in range(4))
                count = stat[:, 184 + t:185 + t]
                nc.vector.memset(zero, 0.0)
                nc.vector.tensor_scalar(above, LG[:, t, :], fourth, None, ALU.is_gt)
                link(nc.vector.tensor_scalar(equal, LG[:, t, :], fourth, None, ALU.is_equal))
                nc.vector.tensor_reduce(count, above, AX_X, ALU.add)
                link(nc.vector.tensor_tensor_scan(run, equal, zero, 0.0, ALU.add, ALU.add))
                link(nc.vector.tensor_scalar(run, run, count, float(TOP_K), ALU.add, ALU.is_le))
                link(nc.vector.tensor_tensor(equal, equal, run, ALU.mult))
                nc.vector.tensor_tensor(MASK[:, t, :], above, equal, ALU.add).then_inc(mask_ready, 1)

            def weigh(t):
                s = stat[:, 188 + t:189 + t]
                dve.wait_ge(mask_ready, t + 1)
                dve.wait_ge(lexp_done, t + 1)
                link(nc.vector.tensor_tensor(GATE[:, t, :], GATE[:, t, :], MASK[:, t, :], ALU.mult))
                link(nc.vector.tensor_reduce(s, GATE[:, t, :], AX_X, ALU.add))
                link(nc.vector.reciprocal(s, s))
                nc.vector.tensor_scalar(GATE[:, t, :], GATE[:, t, :], s, None, ALU.mult).then_inc(gate_ready, 1)

            for u in range(44, 47):
                add_h(u)
            for n, (t, h) in enumerate(((0, 0), (1, 0), (0, 1))):
                copy_hT(n, t, h)
            dve.wait_ge(squares, 5)
            mean_square(3, slice(4, 5), D)
            route(0)
            weigh(0)
            norm_h(0)
            add_h(47)
            copy_hT(3, 1, 1)
            dve.wait_ge(squares, 6)
            mean_square(4, slice(5, 6), D)
            route(1)
            weigh(1)
            norm_h(1)
            dve.wait_ge(gate_ready, 2)
            dve.wait_ge(rank_done, 1)
            link(nc.vector.scalar_tensor_tensor(out=RANK, in0=bank[3][:, 0:64].rearrange("p (t e) -> p t e", t=NT), scalar=1.0,
                                                in1=MASK, op0=ALU.add, op1=ALU.mult))
            link(nc.vector.tensor_reduce(stat[:, 190:191], bank[3][:, 64:96], AX_X, ALU.max))
            nc.vector.tensor_scalar(stat[:, 192:193], stat[:, 190:191], float(SLOTS), 1.0, ALU.is_gt, ALU.add)
            nc.vector.tensor_scalar(stat[:, 193:194], stat[:, 190:191], float(2 * SLOTS), None, ALU.is_gt)
            link(nc.vector.tensor_scalar(stat[:, 194:195], stat[:, 190:191], float(3 * SLOTS), None, ALU.is_gt))
            link(nc.vector.tensor_reduce(stat[:, 191:192], stat[:, 192:195], AX_X, ALU.add))
            nc.vector.tensor_copy(rounds[:, :], stat[:, 191:192]).then_inc(rounds_ready, 1)
            link(nc.vector.tensor_scalar(RANK, RANK, -1.0, None, ALU.add))

            def next_round_pair():
                nc.vector.tensor_scalar(RANKS[:, :, EXPERTS:EXPERTS + 2], RANK[:, :, 0:2], -float(SLOTS), None,
                                        ALU.add).then_inc(rank_ready, 1)

            def build_slots(first):
                for dst, weighted in ((PT, False), (PW, True)):
                    for t in range(NT):
                        for e in range(2):
                            cols = slice(e * SLOTS, (e + 1) * SLOTS)
                            rank = RANKS[:, t, bass.ds(first + e, 1)]
                            if weighted:
                                nc.vector.tensor_scalar(PW[:, t, cols], iota[:, cols], rank, GATES[:, t, bass.ds(first + e, 1)],
                                                        ALU.is_equal, ALU.mult).then_inc(slots_built, 1)
                            else:
                                nc.vector.tensor_scalar(PT[:, t, cols], iota[:, cols], rank, None,
                                                        ALU.is_equal).then_inc(slots_built, 1)

            next_round_pair()
            nc.vector.tensor_copy(GATES[:, :, EXPERTS:EXPERTS + 2], GATE[:, :, 0:2]).then_inc(rank_ready, 1)
            dve.wait_ge(rank_ready, 2)
            build_slots(0)
            for c in (200, 203):
                nc.vector.memset(stat[:, c:c + 1], 0.0).then_inc(y_added, 1)
                nc.vector.memset(stat[:, c + 1:c + 2], 0.0).then_inc(o_hi, 1)
                nc.vector.memset(stat[:, c + 2:c + 3], 0.0).then_inc(o_lo, 1)
            dve.wait_ge(rounds_ready, 1)
            n_rounds = dve.value_load(rounds[0:1, 0:1], min_val=1, max_val=SEQ // SLOTS)

            def add_results(count):
                for j in range(4):
                    t, h = divmod(j, 2)
                    dve.wait_ge(comb_done, count + (j + 1))
                    nc.vector.tensor_tensor(X[:, t, h * HALF:(h + 1) * HALF], bank[6 + j % 2][:, :],
                                            X[:, t, h * HALF:(h + 1) * HALF], ALU.add).then_inc(y_added, 1)

            with dve.Fori(0, n_rounds) as r:
                with dve.Fori(0, PAIRS // 2) as d:
                    for s in range(2):
                        i = d * 2 + s
                        it = r * PAIRS + i
                        dve.wait_ge(disp_done, it * 2 + 2)
                        nc.vector.tensor_copy(XE[:, 4:8, :], bank[5][:, :].rearrange("p (k n) -> p k n", k=4)).then_inc(xe_hi, 1)
                        dve.wait_ge(slots_free, it + 1)
                        build_slots(i * 2 + 2)
                        for e in range(2):
                            dve.wait_ge(used, it * PER_PAIR + (4 * e + 2))
                            nc.vector.tensor_scalar(GS, bank[0][:, :], LIMIT, None, ALU.min).then_inc(g_read, 1)
                            dve.wait_ge(sig_done, it * 2 + (e + 1))
                            dve.wait_ge(g_read, it * 2 + (e + 1))
                            nc.vector.tensor_tensor(SG, SG, GS, ALU.mult).then_inc(gs_done, 1)
                            dve.wait_ge(used, it * PER_PAIR + (4 * e + 4))
                            if e:
                                dve.wait_ge(act_ready, it * 2 + 1)
                            nc.vector.tensor_scalar(US, bank[1][:, :], LIMIT, -LIMIT, ALU.min, ALU.max).then_inc(u_read, 1)
                            dve.wait_ge(u_read, it * 2 + (e + 1))
                            dve.wait_ge(gs_done, it * 2 + (e + 1))
                            nc.vector.scalar_tensor_tensor(
                                out=AH[:, e, :].rearrange("p (j n) -> p j n", j=4), in0=US.rearrange("p (n j) -> p j n", j=4),
                                scalar=1.0, in1=SG.rearrange("p (n j) -> p j n", j=4), op0=ALU.add, op1=ALU.mult).then_inc(act_ready, 1)
                            if e == 0:
                                add_results(it * 4)
                        for e in range(2):
                            dve.wait_ge(used, it * PER_PAIR + (10 + 2 * e))
                            nc.vector.tensor_copy(OE[e * SLOTS:(e + 1) * SLOTS, HALF:D], bank[2][SLOTS:2 * SLOTS, :]).then_inc(o_hi, 1)
                dve.wait_ge(slots_built, (r + 1) * (8 * PAIRS) + 8)
                nc.vector.tensor_scalar(RANK, RANK, -float(SLOTS), None, ALU.add).then_inc(rank_ready, 1)
                dve.wait_ge(rank_ready, r * 2 + 3)
                next_round_pair()
                dve.wait_ge(rank_ready, r * 2 + 4)
            add_results(n_rounds * (4 * PAIRS))

        @block.tensor
        def _(pe):
            def turn4(dst, srcs, signal):
                for b in range(4):
                    ins = nc.tensor.transpose(dst[:, b * P:(b + 1) * P], srcs[b], ident)
                ins.then_inc(signal, 1)

            stationary = {}
            for name in PIECES:
                stationary[name] = {"mk": MEMT, "mv": MEMT, "wbp": Z2T, "wbm": OMT, "wba0": OT, "wba1": OT,
                                    "wo0": MGT, "wo1": MGT}.get(name, XNT)

            def unit(u):
                unit_k(u, 0, 4 if UNITS[u][1] in ("wbp", "wbm") else KD)

            def unit_k(u, first, after):
                n, name, t, c = UNITS[u]
                k_n = 4 if name in ("wbp", "wbm") else KD
                if u - 3 >= UNIT_OF[("wo0", 0, 0)]:
                    pe.wait_ge(h_ready, u - 3 - UNIT_OF[("wo0", 0, 0)] + 1)
                elif u >= 3:
                    pe.wait_ge(bank_read[u % 3], u // 3)
                short = name in ("wbp", "wbm")
                high, low = stationary[name][0:2]
                for k in range(first, after):
                    H = 2 * n + (c if short else k // 4)
                    if H < EARLY:
                        if k % 2 == 0:
                            pe.wait_ge(lo_early, 2 * H + k % 4 // 2 + 1)
                    elif k % 4 == 0:
                        pe.wait_ge(lo_ready, H - EARLY + 1)
                    cols = slice((k % 4) * HALF, (k % 4 + 1) * HALF)
                    toks = slice(t * P, (t + 1) * P)
                    for m, (a, b) in enumerate(((high, upper(H)), (high, lower(H)), (low, upper(H)))):
                        ins = nc.tensor.matmul(UB[u % 3][:, :], a[:, k, toks], b[:, cols],
                                               start=(k == 0 and m == 0), stop=(k == k_n - 1 and m == 2))
                    if k == 3 and t == NT - 1 and not short:
                        ins.then_inc(first_half_used, 1)
                if after == k_n:
                    ins.then_inc(unit_done, 1)

            pe.wait_ge(ident_in, 16)
            pe.wait_ge(x_in, 16 * NT)
            for j in range(4):
                t, h = divmod(j, 2)
                turn4(bank[3 + j], [X[:, t, (4 * h + b) * P:(4 * h + b + 1) * P] for b in range(4)], xT_done)
            pe.wait_ge(xT_copied, 2)
            unit(0)
            pe.wait_ge(mem_in, 16)
            for j in range(4):
                t, h = divmod(j, 2)
                pe.wait_ge(xT_copied, j + 1)
                turn4(bank[3 + j], [MEM[:, t, (4 * h + b) * P:(4 * h + b + 1) * P] for b in range(4)], mT_done)
            unit(1)
            pe.wait_ge(mT_copied, 2)
            unit(2)
            pe.wait_ge(mT_copied, 4)
            for u in range(3, 8):
                unit(u)
            pe.wait_ge(band_in, 32)
            for j in range(2):
                for g in (2 * j, 2 * j + 1):
                    for t in range(NT):
                        ins = nc.tensor.matmul(bank[4 + j][:, (g % 2) * SEQ:(g % 2 + 1) * SEQ], U[:, t, g * P:(g + 1) * P],
                                               BAND[:, t, g, :], start=(t == 0), stop=(t == NT - 1))
                ins.then_inc(z_done, 1)
            unit(8)
            unit(9)
            for j in range(2):
                pe.wait_ge(zT_copied, 2)
                for g in (2 * j, 2 * j + 1):
                    ins = nc.tensor.matmul(bank[4 + j][:, (g % 2) * SEQ:(g % 2 + 1) * SEQ], POOLW[:, g, :], ZT[:, g, :],
                                           start=True, stop=True)
                ins.then_inc(z2_done, 1)
            unit(10)
            unit(11)
            for j, (rows_, t) in enumerate(((KM, 0), (KM, 1), (QM, 0), (QM, 1))):
                pe.wait_ge(mem_normed, j // 2 + 1)
                pe.wait_ge(z2T_copied, 2)
                turn4(bank[(3, 6, 4, 5)[j]], [rows_[:, t, h * P:(h + 1) * P] for h in range(MHEADS)], kq_done)
            unit(12)
            unit(13)

            def mem_scores(h):
                if h == 0:
                    pe.wait_ge(kqT_copied, 4)
                if h >= 2:
                    pe.wait_ge(mexp_done, h - 1)
                for t in range(NT):
                    ins = nc.tensor.matmul(bank[4 + h % 2][:, t * SEQ:(t + 1) * SEQ], QMT[:, h, t * P:(t + 1) * P], KMT[:, h, :],
                                           start=True, stop=True)
                ins.then_inc(ms_done, 1)

            def mem_turn(h):
                if h >= 1:
                    pe.wait_ge(pt_copied, h)
                pe.wait_ge(mp_ready, h + 1)
                turn4(bank[6], [prob[:, h % 2, t * SEQ + m * P:t * SEQ + (m + 1) * P] for m in range(2) for t in range(NT)], mt_done)

            def mem_values(h):
                if h >= 1:
                    pe.wait_ge(omT_copied, h)
                pe.wait_ge(pt_copied, h + 1)
                for m in range(2):
                    ins = nc.tensor.matmul(bank[7][:, 0:SEQ], VM[:, m, h * P:(h + 1) * P], probT[:, h % 2, m * SEQ:(m + 1) * SEQ],
                                           start=(m == 0), stop=(m == 1))
                ins.then_inc(mo_done, 1)

            unit(14)
            unit(15)
            mem_scores(0)
            unit(16)
            mem_scores(1)
            unit_k(17, 0, 4)
            mem_turn(0)
            unit_k(17, 4, KD)
            mem_values(0)
            mem_scores(2)
            mem_turn(1)
            unit(18)
            mem_values(1)
            mem_scores(3)
            mem_turn(2)
            unit(19)
            mem_values(2)
            mem_turn(3)

            def turn_qk(h):
                if h == 0:
                    pe.wait_ge(normed, 8)
                else:
                    pe.wait_ge(qkT_copied, h)
                turn4(bank[3], [r[:, t, h * P:(h + 1) * P] for r in (Q, K) for t in range(NT)], qk_done)

            def scores(h):
                pe.wait_ge(qkT_copied, h + 1)
                if h >= 1:
                    pe.wait_ge(max_ready, h)
                else:
                    pe.wait_ge(mexp_done, MHEADS)
                for c in range(2):
                    part = qkt[c * HD:(c + 1) * HD, h % 2, :]
                    nc.tensor.matmul(bank[4 + c][:, 0:P], part[:, 0:P], part[:, SEQ:SEQ + P], start=True, stop=True)
                    ins = nc.tensor.matmul(bank[4 + c][:, P:3 * P], part[:, P:SEQ], part[:, SEQ:2 * SEQ], start=True, stop=True)
                ins.then_inc(sc_done, 1)

            def turn_a(h):
                pe.wait_ge(a_ready, h + 1)
                if h >= 1:
                    pe.wait_ge(at_copied, h)
                else:
                    pe.wait_ge(pt_copied, MHEADS)
                for b in range(3):
                    ins = nc.tensor.transpose(bank[6][:, b * P:(b + 1) * P], prob[:, h % 2, b * P:(b + 1) * P], ident)
                ins.then_inc(at_done, 1)

            def values(h):
                pe.wait_ge(at_copied, h + 1)
                if h >= 1:
                    pe.wait_ge(o_copied, h)
                else:
                    pe.wait_ge(omT_copied, MHEADS)
                cols = slice(h * P, (h + 1) * P)
                nc.tensor.matmul(bank[7][:, 0:P], probT[:, h % 2, 0:P], V[:, 0, cols], start=True, stop=True)
                nc.tensor.matmul(bank[7][:, P:2 * P], probT[:, h % 2, P:2 * P], V[:, 0, cols], start=True, stop=False)
                nc.tensor.matmul(bank[7][:, P:2 * P], probT[:, h % 2, 2 * P:3 * P], V[:, 1, cols], start=False,
                                 stop=True).then_inc(pv_done, 1)

            turn_qk(0)
            unit(20)
            mem_values(3)
            scores(0)
            turn_qk(1)
            unit(21)
            pe.wait_ge(bank_read[19 % 3], 19 // 3 + 1)
            for h in range(HEADS):
                if h == 1:
                    pe.wait_ge(z2T_copied, 2)
                if h + 1 < HEADS:
                    scores(h + 1)
                if h == 0:
                    pe.wait_ge(omT_copied, MHEADS)
                unit(22 + 2 * h)
                turn_a(h)
                if h + 2 < HEADS:
                    turn_qk(h + 2)
                if h == HEADS - 1:
                    values(h)
                unit(23 + 2 * h)
                if h < HEADS - 1:
                    values(h)
            unit(38)
            unit(39)
            for j in range(4):
                t, h = divmod(j, 2)
                pe.wait_ge(o_normed, t + 1)
                turn4(bank[3 + j], [O[:, t, (4 * h + b) * P:(4 * h + b + 1) * P] for b in range(4)], oT_done)
            pe.wait_ge(oT_split, 2)
            unit(40)
            pe.wait_ge(oT_split, 4)
            unit(41)
            unit(42)

            def turn_merged(j):
                h, t = divmod(j, 2)
                pe.wait_ge(merged, 5 + j)
                turn4(bank[3 + j], [MG[:, t, (4 * h + b) * P:(4 * h + b + 1) * P] for b in range(4)], mgT_done)

            turn_merged(0)
            turn_merged(1)
            unit(43)
            turn_merged(2)
            turn_merged(3)
            pe.wait_ge(mgT_split, 3)
            unit(44)
            pe.wait_ge(mgT_split, 4)
            unit(45)
            unit(46)

            def turn_h(n, t, h):
                turn4(bank[3 + n], [X[:, t, (4 * h + b) * P:(4 * h + b + 1) * P] for b in range(4)], hT_done)

            def logits(t):
                for k in range(KD):
                    ins = nc.tensor.matmul(bank[7][:, t * EXPERTS:(t + 1) * EXPERTS], HNT[:, k, t * P:(t + 1) * P], WR[:, k, :],
                                           start=(k == 0), stop=(k == KD - 1))
                ins.then_inc(logit_done, 1)

            for n, (t, h) in enumerate(((0, 0), (1, 0), (0, 1))):
                pe.wait_ge(h_ready, n + 1)
                turn_h(n, t, h)
            unit_k(47, 0, 2)
            pe.wait_ge(hT_copied, 3)
            pe.wait_ge(late_in, 32)
            logits(0)
            unit_k(47, 2, KD)
            pe.wait_ge(h_ready, 4)
            turn_h(3, 1, 1)
            pe.wait_ge(hT_copied, 4)
            logits(1)
            pe.wait_ge(mask_ready, 2)
            for cols, parts in ((slice(0, 32), ((tri, 0),)), (slice(32, 64), ((ones, 0), (tri, 1))), (slice(64, 96), ((ones, 0), (ones, 1)))):
                for n, (m, t) in enumerate(parts):
                    ins = nc.tensor.matmul(bank[3][:, cols], m, MASK[:, t, :], start=(n == 0), stop=(n == len(parts) - 1))
            ins.then_inc(rank_done, 1)
            pe.wait_ge(gate_ready, 2)
            for t in range(NT):
                ins = nc.tensor.transpose(bank[6][0:EXPERTS, t * P:(t + 1) * P], GATE[:, t, :], ident)
            ins.then_inc(gT_done, 1)
            pe.wait_ge(seed_in, 16)
            pe.wait_ge(rounds_ready, 1)
            n_rounds = pe.value_load(rounds[0:1, 0:1], min_val=1, max_val=SEQ // SLOTS)

            def combine(it):
                pe.wait_ge(o_lo, it * 2 + 2)
                pe.wait_ge(o_hi, it * 2 + 2)
                pe.wait_ge(wT_copied, it + 1)
                for j in range(4):
                    t, h = divmod(j, 2)
                    pe.wait_ge(y_added, it * 4 + (j + 1))
                    nc.tensor.matmul(bank[6 + j % 2][:, :], PWT[:, t * P:(t + 1) * P], OE[:, h * HALF:(h + 1) * HALF],
                                     start=True, stop=True).then_inc(comb_done, 1)

            def project(it, turn, s, e, m, first, dst):
                row = 2 * m + e
                for j in (first, first + 1):
                    q = s * PER_PAIR + j
                    pe.wait_ge(ring_in[moe_slot(q)], moe_landed(turn, q))
                    w = moe_ring[:, moe_slot(q), :].rearrange("p (k n) -> p k n", k=4)
                    for k in range(4):
                        kk = 4 * (j - first) + k
                        for h in range(2):
                            ins = nc.tensor.matmul(dst[h * SLOTS:(h + 1) * SLOTS, :], XE[:, kk, e * SLOTS:(e + 1) * SLOTS],
                                                   w[:, k, h * HALF:(h + 1) * HALF], start=(kk == 0), stop=False)
                    if j == first:
                        ins.then_inc(used, 1)
                for h in range(2):
                    ins = nc.tensor.matmul(dst[h * SLOTS:(h + 1) * SLOTS, :], sel[:, row, :],
                                           B4[s][:, h * HALF:(h + 1) * HALF], start=False, stop=True)
                ins.then_inc(used, 1)

            with pe.Fori(0, n_rounds) as r:
                with pe.Fori(0, PAIRS // 2) as d:
                    for s in range(2):
                        i = d * 2 + s
                        it = r * PAIRS + i
                        turn = r * (PAIRS // 2) + d
                        pe.wait_ge(slots_built, it * 8 + 4)
                        for half in range(2):
                            for b in range(4):
                                for t in range(NT):
                                    ins = nc.tensor.matmul(bank[4 + half][:, b * P:(b + 1) * P], HN[:, t, 4 * half + b, :], PT[:, t, :],
                                                           start=(t == 0), stop=(t == NT - 1))
                            ins.then_inc(disp_done, 1)
                        pe.wait_ge(slots_built, it * 8 + 8)
                        for t in range(NT):
                            ins = nc.tensor.transpose(bank[3][:, t * P:(t + 1) * P], PW[:, t, :], ident)
                        ins.then_inc(slots_free, 1)
                        pe.wait_ge(xe_lo, it + 1)
                        pe.wait_ge(xe_hi, it + 1)
                        pe.wait_ge(bias_in, it * 32 + 32)
                        project(it, turn, s, 0, 0, 0, bank[0])
                        project(it, turn, s, 0, 1, 2, bank[1])
                        combine(it)
                        pe.wait_ge(g_read, it * 2 + 1)
                        project(it, turn, s, 1, 0, 4, bank[0])
                        pe.wait_ge(u_read, it * 2 + 1)
                        project(it, turn, s, 1, 1, 6, bank[1])
                        for e in range(2):
                            pe.wait_ge(act_ready, it * 2 + (e + 1))
                            if e == 0:
                                pe.wait_ge(wT_copied, it + 2)
                            turn4(bank[3], [AH[:, e, j * P:(j + 1) * P] for j in range(4)], actT_done)
                            if e == 1:
                                pe.wait_ge(o_lo, it * 2 + 3)
                                pe.wait_ge(o_hi, it * 2 + 3)
                            pe.wait_ge(actT_copied, it * 2 + (e + 1))
                            for j in (8 + 2 * e, 9 + 2 * e):
                                q = s * PER_PAIR + j
                                pe.wait_ge(ring_in[moe_slot(q)], moe_landed(turn, q))
                                w = moe_ring[:, moe_slot(q), :].rearrange("p (k n) -> p k n", k=4)
                                half = j % 2
                                for k in range(4):
                                    for h in range(2):
                                        ins = nc.tensor.matmul(bank[2][h * SLOTS:(h + 1) * SLOTS, :],
                                                               AHT[:, k, half * SLOTS:(half + 1) * SLOTS],
                                                               w[:, k, h * HALF:(h + 1) * HALF], start=(half == 0 and k == 0),
                                                               stop=(half == 1 and k == 3))
                                ins.then_inc(used, 1)
            combine(n_rounds * PAIRS)


_INS = ["x", "mem", "g_mix", "w_in", "b_gates", "q_norm", "k_norm", "lambda_q1", "lambda_k1", "lambda_q2", "lambda_k2",
        "g_subln", "pool_w", "pool_scale", "g_mem", "w_mem_kv", "mq_norm", "mk_norm", "w_b_attn", "w_b_pool", "w_b_mem",
        "w_out", "g_ffn", "w_router", "b_router", "w_gate", "b_gate", "w_up", "b_up", "w_down", "b_down"]


def kernel(**inputs):
    import concourse.bacc as bacc
    from concourse.bass_utils import run_bass_kernel_spmd

    nc = bacc.Bacc("TRN2", target_bir_lowering=False, num_devices=1)
    table, band = constants()
    arrays, args = {}, []
    for name in _INS + ["table", "band"]:
        a = {"table": table, "band": band}.get(name)
        a = np.ascontiguousarray(inputs[name]) if a is None else a
        arrays[f"in_{name}"] = a
        args.append(nc.dram_tensor(f"in_{name}", a.shape, mybir.dt.from_np(a.dtype), kind="ExternalInput").ap())
    args.append(nc.dram_tensor("out_0", (1, SEQ, D), F32, kind="ExternalOutput").ap())
    decoder_layer(nc, *args)
    r = run_bass_kernel_spmd(nc, [arrays], core_ids=[0])
    return r.results[0]["out_0"]
```
